# Optimizing a Trainium2 kernel written in Bass

```python
import math
import jax, jax.numpy as jnp
from jax import lax
import numpy as np

D_MODEL = 1024
BATCH = 1
SEQ = 256
DEPTH = 2

D_FF = 2816
NORM_EPS = 1e-6
NSA_HEADS = 8
NSA_KV_HEADS = 2
NSA_GROUP = NSA_HEADS // NSA_KV_HEADS
NSA_HEAD_DIM = 64
CMP_BLOCK = 32
CMP_STRIDE = 16
SEL_BLOCK = 64
SEL_TOPK = 16
WINDOW = 512
Q_BLOCK = 128
ROPE_THETA = 10000.0
FORCE_SCORE = 1e4
SSD_HEADS = 16
SSD_HEAD_DIM = 64
SSD_D_INNER = SSD_HEADS * SSD_HEAD_DIM
SSD_GROUPS = 2
SSD_STATE = 128
SSD_CONV = 4
SSD_CHUNK = 128
SSD_NORM_EPS = 1e-5
RWKV_HEAD_DIM = 64
RWKV_HEADS = D_MODEL // RWKV_HEAD_DIM
DECAY_LORA = 64
AAA_LORA = 64
GATE_LORA = 160
RWKV_GN_EPS = 64e-5

N_EVEN = (DEPTH + 1) // 2
N_ODD = DEPTH // 2

NSA_Q_W = NSA_HEADS * NSA_HEAD_DIM
NSA_KV_W = NSA_KV_HEADS * NSA_HEAD_DIM
SSD_XBC = SSD_D_INNER + 2 * SSD_GROUPS * SSD_STATE
IN_SPLITS = (NSA_Q_W, NSA_KV_W, NSA_KV_W, NSA_KV_W, NSA_KV_W, NSA_KV_W, NSA_KV_W,
             NSA_HEADS * 3, SSD_D_INNER, SSD_XBC, SSD_HEADS)
IN_WIDTH = sum(IN_SPLITS)
MIX_OUT_WIDTH = NSA_Q_W + SSD_D_INNER


def rmsnorm(x, g, eps=NORM_EPS):
    xf = x.astype(jnp.float32)
    y = xf * lax.rsqrt(jnp.mean(xf * xf, -1, keepdims=True) + eps)
    return (y * g.astype(jnp.float32)).astype(x.dtype)

def swiglu(x, w_gate, w_up, w_down):
    return (jax.nn.silu(x @ w_gate) * (x @ w_up)) @ w_down

def rope_tables(seq, dim):
    inv = ROPE_THETA ** (-jnp.arange(0, dim, 2, dtype=jnp.float32) / dim)
    ang = jnp.arange(seq, dtype=jnp.float32)[:, None] * inv[None, :]
    return jnp.cos(ang), jnp.sin(ang)

def apply_rope(x, cos, sin):
    shape = (1, x.shape[1]) + (1,) * (x.ndim - 3) + (cos.shape[-1],)
    c = cos.reshape(shape).astype(x.dtype)
    s = sin.reshape(shape).astype(x.dtype)
    x1, x2 = jnp.split(x, 2, axis=-1)
    return jnp.concatenate([x1 * c - x2 * s, x2 * c + x1 * s], -1)

def masked_softmax(s, mask):
    s = jnp.where(mask, s.astype(jnp.float32), -1e30)
    p = jnp.where(mask, jnp.exp(s - jnp.max(s, -1, keepdims=True)), 0.0)
    return p / jnp.maximum(jnp.sum(p, -1, keepdims=True), 1e-30)

def compress_blocks(k, pe, w1, w2):
    b, s, h, d = k.shape
    n_cmp = (s - CMP_BLOCK) // CMP_STRIDE + 1
    idx = jnp.arange(n_cmp)[:, None] * CMP_STRIDE + jnp.arange(CMP_BLOCK)[None, :]
    blk = k[:, idx] + pe[None, None, :, None, :]
    blk = jnp.moveaxis(blk, 3, 2).reshape(b, n_cmp, h, CMP_BLOCK * d)
    return jax.nn.silu(blk @ w1) @ w2

def nsa_attention(q, k_cmp, v_cmp, k_sel, v_sel, k_win, v_win, gates,
                  pe_k, w1_k, w2_k, pe_v, w1_v, w2_v):
    b, s, hkv, g, d = q.shape
    kc = compress_blocks(k_cmp, pe_k, w1_k, w2_k)
    vc = compress_blocks(v_cmp, pe_v, w1_v, w2_v)
    n_cmp = kc.shape[1]
    n_sel = s // SEL_BLOCK
    topk = min(SEL_TOPK, n_sel)
    cmp_start = jnp.arange(n_cmp) * CMP_STRIDE
    cmp_end = cmp_start + CMP_BLOCK - 1
    sel_start = jnp.arange(n_sel) * SEL_BLOCK
    overlap = ((cmp_start[:, None] < sel_start[None, :] + SEL_BLOCK)
               & (cmp_end[:, None] >= sel_start[None, :])).astype(jnp.float32)
    ks_blk = jnp.moveaxis(k_sel, 2, 1).reshape(b, hkv, n_sel, SEL_BLOCK, d)
    vs_blk = jnp.moveaxis(v_sel, 2, 1).reshape(b, hkv, n_sel, SEL_BLOCK, d)
    pad = ((0, 0), (WINDOW, 0), (0, 0), (0, 0))
    kw_pad = jnp.pad(k_win, pad)
    vw_pad = jnp.pad(v_win, pad)
    bi = jnp.arange(b)[:, None, None, None]
    hi = jnp.arange(hkv)[None, :, None, None]
    blk_ids = jnp.arange(n_sel)

    def block(qi):
        s0 = qi * Q_BLOCK
        qb = lax.dynamic_slice_in_dim(q, s0, Q_BLOCK, 1)
        gb = lax.dynamic_slice_in_dim(gates, s0, Q_BLOCK, 1)
        t = s0 + jnp.arange(Q_BLOCK)
        p_c = masked_softmax(jnp.einsum('bqhgd,bchd->bhgqc', qb, kc),
                             cmp_end[None, :] <= t[:, None])
        o_c = jnp.einsum('bhgqc,bchd->bqhgd', p_c.astype(vc.dtype), vc)
        imp = jnp.einsum('bhgqc,cj->bhqj', p_c, overlap)
        cur = t // SEL_BLOCK
        forced = ((blk_ids[None, :] == 0) | (blk_ids[None, :] == cur[:, None])
                  | (blk_ids[None, :] == cur[:, None] - 1))
        valid = sel_start[None, :] <= t[:, None]
        imp = jnp.where(valid, jnp.where(forced, FORCE_SCORE, imp), -jnp.inf)
        _, sel = lax.top_k(imp, topk)
        kg = ks_blk[bi, hi, sel].reshape(b, hkv, Q_BLOCK, topk * SEL_BLOCK, d)
        vg = vs_blk[bi, hi, sel].reshape(b, hkv, Q_BLOCK, topk * SEL_BLOCK, d)
        tok = (sel[..., None] * SEL_BLOCK + jnp.arange(SEL_BLOCK)).reshape(
            b, hkv, Q_BLOCK, topk * SEL_BLOCK)
        p_s = masked_softmax(jnp.einsum('bqhgd,bhqnd->bhgqn', qb, kg),
                             (tok <= t[:, None])[:, :, None])
        o_s = jnp.einsum('bhgqn,bhqnd->bqhgd', p_s.astype(vg.dtype), vg)
        kw = lax.dynamic_slice_in_dim(kw_pad, s0, Q_BLOCK + WINDOW, 1)
        vw = lax.dynamic_slice_in_dim(vw_pad, s0, Q_BLOCK + WINDOW, 1)
        kp = s0 - WINDOW + jnp.arange(Q_BLOCK + WINDOW)
        mask_w = ((kp[None, :] <= t[:, None]) & (kp[None, :] > t[:, None] - WINDOW)
                  & (kp[None, :] >= 0))
        p_w = masked_softmax(jnp.einsum('bqhgd,bkhd->bhgqk', qb, kw), mask_w)
        o_w = jnp.einsum('bhgqk,bkhd->bqhgd', p_w.astype(vw.dtype), vw)
        return gb[..., 0:1] * o_c + gb[..., 1:2] * o_s + gb[..., 2:3] * o_w

    out = lax.map(block, jnp.arange(s // Q_BLOCK))
    return jnp.moveaxis(out, 0, 1).reshape(b, s, hkv * g * d)

def causal_depthwise_conv(x, w, bias):
    y = lax.conv_general_dilated(x, w, window_strides=(1,), padding=[(SSD_CONV - 1, 0)],
                                 dimension_numbers=('NWC', 'WIO', 'NWC'),
                                 feature_group_count=x.shape[-1])
    return y + bias

def ssd_chunked(x, dt, a, bmat, cmat):
    b, s, h, p = x.shape
    g, n = bmat.shape[2], bmat.shape[3]
    r = h // g
    l = SSD_CHUNK
    c = s // l
    xd = (x * dt[..., None]).reshape(b, c, l, g, r, p)
    a_cs = jnp.cumsum(jnp.moveaxis((dt * a).reshape(b, c, l, g, r), 2, -1), axis=-1)
    bm = bmat.reshape(b, c, l, g, n)
    cm = cmat.reshape(b, c, l, g, n)
    causal = jnp.tril(jnp.ones((l, l), bool))
    seg = jnp.exp(jnp.where(causal, a_cs[..., :, None] - a_cs[..., None, :], -jnp.inf))
    cb = jnp.einsum('bclgn,bcsgn->bcgls', cm, bm)
    y_diag = jnp.einsum('bcgrls,bcsgrp->bclgrp', cb[:, :, :, None] * seg, xd)
    decay_states = jnp.exp(a_cs[..., -1:] - a_cs)
    states = jnp.einsum('bclgn,bcgrl,bclgrp->bcgrpn', bm, decay_states, xd)
    chunk_decay = jnp.exp(a_cs[..., -1])

    def step(carry, inp):
        st, dec = inp
        return carry * dec[..., None, None] + st, carry

    _, states_in = lax.scan(step, jnp.zeros_like(states[:, 0]),
                            (jnp.moveaxis(states, 1, 0), jnp.moveaxis(chunk_decay, 1, 0)))
    states_in = jnp.moveaxis(states_in, 0, 1)
    y_off = jnp.einsum('bclgn,bcgrpn,bcgrl->bclgrp', cm, states_in, jnp.exp(a_cs))
    return (y_diag + y_off).reshape(b, s, h, p)

def mamba2_branch(z, xbc, dt_raw, conv_w, conv_b, dt_bias, a_log, d_skip, norm_w):
    b, s, _ = z.shape
    f32 = jnp.float32
    xbc = jax.nn.silu(causal_depthwise_conv(xbc, conv_w, conv_b))
    xs, bm, cm = jnp.split(xbc, [SSD_D_INNER, SSD_D_INNER + SSD_GROUPS * SSD_STATE], -1)
    xs = xs.reshape(b, s, SSD_HEADS, SSD_HEAD_DIM).astype(f32)
    dt = jax.nn.softplus(dt_raw.astype(f32) + dt_bias.astype(f32))
    a = -jnp.exp(a_log.astype(f32))
    y = ssd_chunked(xs, dt, a, bm.reshape(b, s, SSD_GROUPS, SSD_STATE).astype(f32),
                    cm.reshape(b, s, SSD_GROUPS, SSD_STATE).astype(f32))
    y = y + xs * d_skip.astype(f32)[:, None]
    y = y.reshape(b, s, SSD_D_INNER) * jax.nn.silu(z.astype(f32))
    yg = y.reshape(b, s, SSD_GROUPS, SSD_D_INNER // SSD_GROUPS)
    yg = yg * lax.rsqrt(jnp.mean(yg * yg, -1, keepdims=True) + SSD_NORM_EPS)
    return (yg.reshape(b, s, SSD_D_INNER) * norm_w.astype(f32)).astype(z.dtype)

def nsa_ssd_mixer(h, cos, sin, w_in, pe_k, w1_k, w2_k, pe_v, w1_v, w2_v,
                  conv_w, conv_b, dt_bias, a_log, d_skip, ssd_norm_w, w_out):
    b, s, _ = h.shape
    proj = h @ w_in
    offs = np.cumsum(IN_SPLITS)[:-1].tolist()
    q, kc, vc, ks, vs, kw, vw, gl, z, xbc, dt = jnp.split(proj, offs, -1)
    kvshape = (b, s, NSA_KV_HEADS, NSA_HEAD_DIM)
    q = apply_rope(q.reshape(b, s, NSA_KV_HEADS, NSA_GROUP, NSA_HEAD_DIM), cos, sin) * (NSA_HEAD_DIM ** -0.5)
    kc = apply_rope(kc.reshape(kvshape), cos, sin)
    ks = apply_rope(ks.reshape(kvshape), cos, sin)
    kw = apply_rope(kw.reshape(kvshape), cos, sin)
    gates = jax.nn.sigmoid(gl).reshape(b, s, NSA_KV_HEADS, NSA_GROUP, 3)
    o_a = nsa_attention(q, kc, vc.reshape(kvshape), ks, vs.reshape(kvshape), kw, vw.reshape(kvshape),
                        gates, pe_k, w1_k, w2_k, pe_v, w1_v, w2_v)
    o_b = mamba2_branch(z, xbc, dt, conv_w, conv_b, dt_bias, a_log, d_skip, ssd_norm_w)
    return jnp.concatenate([o_a, o_b], -1) @ w_out

def rwkv7_time_mix(h, mu, w_r, w_k, w_v, w_o, w0, w1, w2, a0, a1, a2, g1, g2,
                   k_k, k_a, r_k, ln_g, ln_b):
    b, s, d = h.shape
    f32 = jnp.float32
    xx = jnp.pad(h, ((0, 0), (1, 0), (0, 0)))[:, :-1] - h
    xr, xw, xk, xv, xa, xg = [h + xx * mu[i] for i in range(6)]
    r = xr @ w_r
    w = -jax.nn.softplus(-(w0 + jnp.tanh(xw @ w1) @ w2)) - 0.5
    k = xk @ w_k
    v = xv @ w_v
    a = jax.nn.sigmoid(a0 + (xa @ a1) @ a2)
    g = jax.nn.sigmoid(xg @ g1) @ g2
    heads = lambda t: t.reshape(b, s, RWKV_HEADS, RWKV_HEAD_DIM).astype(f32)
    kk = heads(k * k_k)
    kk = kk / jnp.maximum(jnp.sqrt(jnp.sum(kk * kk, -1, keepdims=True)), 1e-12)
    k = k * (1 + (a - 1) * k_a)
    r_, k_, v_, a_ = heads(r), heads(k), heads(v), heads(a)
    decay = jnp.exp(-jnp.exp(heads(w)))

    def step(state, inp):
        r_t, d_t, k_t, v_t, kk_t, a_t = inp
        sa = jnp.einsum('bhij,bhj->bhi', state, -kk_t)
        state = (state * d_t[:, :, None, :] + sa[..., None] * (kk_t * a_t)[:, :, None, :]
                 + v_t[..., None] * k_t[:, :, None, :])
        return state, jnp.einsum('bhij,bhj->bhi', state, r_t)

    xs = tuple(jnp.moveaxis(t, 1, 0) for t in (r_, decay, k_, v_, kk, a_))
    _, y = lax.scan(step, jnp.zeros((b, RWKV_HEADS, RWKV_HEAD_DIM, RWKV_HEAD_DIM), f32), xs)
    y = jnp.moveaxis(y, 0, 1)
    mean = jnp.mean(y, -1, keepdims=True)
    var = jnp.mean(jnp.square(y - mean), -1, keepdims=True)
    y = ((y - mean) * lax.rsqrt(var + RWKV_GN_EPS)).reshape(b, s, d)
    y = y * ln_g.astype(f32) + ln_b.astype(f32)
    bonus = jnp.sum(r_ * k_ * r_k.astype(f32), -1, keepdims=True) * v_
    y = y + bonus.reshape(b, s, d)
    return (y * g.astype(f32)).astype(h.dtype) @ w_o

def first_inputs(seed: int = 0) -> dict:
    key = jax.random.key(seed)
    ks = iter(jax.random.split(key, 48))
    nrm = lambda shape, scale: scale * jax.random.normal(next(ks), shape, jnp.float32)
    uni = lambda shape, lo, hi: jax.random.uniform(next(ks), shape, jnp.float32, lo, hi)
    D, F, E, O = D_MODEL, D_FF, N_EVEN, N_ODD
    L, KD = CMP_BLOCK, NSA_HEAD_DIM
    x = nrm((BATCH, SEQ, D), 1.0)
    norm_gains = 1.0 + nrm((DEPTH, 6, D), 0.05)
    ffn1_w_gate = nrm((DEPTH, D, F), D ** -0.5)
    ffn1_w_up = nrm((DEPTH, D, F), D ** -0.5)
    ffn1_w_down = nrm((DEPTH, F, D), F ** -0.5)
    ffn2_w_gate = nrm((DEPTH, D, F), D ** -0.5)
    ffn2_w_up = nrm((DEPTH, D, F), D ** -0.5)
    ffn2_w_down = nrm((DEPTH, F, D), F ** -0.5)
    ab_w_in = nrm((E, D, IN_WIDTH), D ** -0.5)
    a_cmp_pe_k = nrm((E, L, KD), 0.02)
    a_cmp_w1_k = nrm((E, L * KD, KD), (L * KD) ** -0.5)
    a_cmp_w2_k = nrm((E, KD, KD), KD ** -0.5)
    a_cmp_pe_v = nrm((E, L, KD), 0.02)
    a_cmp_w1_v = nrm((E, L * KD, KD), (L * KD) ** -0.5)
    a_cmp_w2_v = nrm((E, KD, KD), KD ** -0.5)
    b_conv_w = nrm((E, SSD_CONV, 1, SSD_XBC), SSD_CONV ** -0.5)
    b_conv_b = nrm((E, SSD_XBC), 0.02)
    dt0 = jnp.exp(uni((E, SSD_HEADS), math.log(1e-3), math.log(1e-1)))
    b_dt_bias = dt0 + jnp.log(-jnp.expm1(-dt0))
    b_a_log = jnp.log(uni((E, SSD_HEADS), 1.0, 16.0))
    b_d_skip = 1.0 + nrm((E, SSD_HEADS), 0.1)
    b_norm_w = 1.0 + nrm((E, SSD_D_INNER), 0.05)
    ab_w_out = nrm((E, MIX_OUT_WIDTH, D), MIX_OUT_WIDTH ** -0.5)
    c_mu = uni((O, 6, D), 0.0, 1.0)
    c_w_r = nrm((O, D, D), D ** -0.5)
    c_w_k = nrm((O, D, D), D ** -0.5)
    c_w_v = nrm((O, D, D), D ** -0.5)
    c_w_o = nrm((O, D, D), D ** -0.5)
    c_w0 = uni((O, D), -6.0, 1.0)
    c_w1 = nrm((O, D, DECAY_LORA), D ** -0.5)
    c_w2 = nrm((O, DECAY_LORA, D), 0.1 * DECAY_LORA ** -0.5)
    c_a0 = nrm((O, D), 0.1)
    c_a1 = nrm((O, D, AAA_LORA), D ** -0.5)
    c_a2 = nrm((O, AAA_LORA, D), 0.1 * AAA_LORA ** -0.5)
    c_g1 = nrm((O, D, GATE_LORA), D ** -0.5)
    c_g2 = nrm((O, GATE_LORA, D), GATE_LORA ** -0.5)
    c_k_k = 0.85 + nrm((O, D), 0.05)
    c_k_a = 1.0 + nrm((O, D), 0.05)
    c_r_k = nrm((O, RWKV_HEADS, RWKV_HEAD_DIM), 0.1)
    c_ln_g = 1.0 + nrm((O, D), 0.05)
    c_ln_b = nrm((O, D), 0.02)
    return {'x': x, 'norm_gains': norm_gains,
            'ffn1_w_gate': ffn1_w_gate, 'ffn1_w_up': ffn1_w_up, 'ffn1_w_down': ffn1_w_down,
            'ffn2_w_gate': ffn2_w_gate, 'ffn2_w_up': ffn2_w_up, 'ffn2_w_down': ffn2_w_down,
            'ab_w_in': ab_w_in, 'a_cmp_pe_k': a_cmp_pe_k, 'a_cmp_w1_k': a_cmp_w1_k,
            'a_cmp_w2_k': a_cmp_w2_k, 'a_cmp_pe_v': a_cmp_pe_v, 'a_cmp_w1_v': a_cmp_w1_v,
            'a_cmp_w2_v': a_cmp_w2_v, 'b_conv_w': b_conv_w, 'b_conv_b': b_conv_b,
            'b_dt_bias': b_dt_bias, 'b_a_log': b_a_log, 'b_d_skip': b_d_skip,
            'b_norm_w': b_norm_w, 'ab_w_out': ab_w_out,
            'c_mu': c_mu, 'c_w_r': c_w_r, 'c_w_k': c_w_k, 'c_w_v': c_w_v, 'c_w_o': c_w_o,
            'c_w0': c_w0, 'c_w1': c_w1, 'c_w2': c_w2, 'c_a0': c_a0, 'c_a1': c_a1, 'c_a2': c_a2,
            'c_g1': c_g1, 'c_g2': c_g2, 'c_k_k': c_k_k, 'c_k_a': c_k_a, 'c_r_k': c_r_k,
            'c_ln_g': c_ln_g, 'c_ln_b': c_ln_b}

def first_block(x, norm_gains, ffn1_w_gate, ffn1_w_up, ffn1_w_down, ffn2_w_gate, ffn2_w_up,
              ffn2_w_down, ab_w_in, a_cmp_pe_k, a_cmp_w1_k, a_cmp_w2_k, a_cmp_pe_v, a_cmp_w1_v,
              a_cmp_w2_v, b_conv_w, b_conv_b, b_dt_bias, b_a_log, b_d_skip, b_norm_w, ab_w_out,
              c_mu, c_w_r, c_w_k, c_w_v, c_w_o, c_w0, c_w1, c_w2, c_a0, c_a1, c_a2, c_g1, c_g2,
              c_k_k, c_k_a, c_r_k, c_ln_g, c_ln_b):
    cos, sin = rope_tables(x.shape[1], NSA_HEAD_DIM)
    for layer in range(DEPTH):
        ng = norm_gains[layer]
        hdn = swiglu(rmsnorm(x, ng[0]), ffn1_w_gate[layer], ffn1_w_up[layer], ffn1_w_down[layer])
        x = x + 0.5 * rmsnorm(hdn, ng[1])
        hdn = rmsnorm(x, ng[2])
        i = layer // 2
        if layer % 2 == 0:
            hdn = nsa_ssd_mixer(hdn, cos, sin, ab_w_in[i], a_cmp_pe_k[i], a_cmp_w1_k[i],
                                a_cmp_w2_k[i], a_cmp_pe_v[i], a_cmp_w1_v[i], a_cmp_w2_v[i],
                                b_conv_w[i], b_conv_b[i], b_dt_bias[i], b_a_log[i], b_d_skip[i],
                                b_norm_w[i], ab_w_out[i])
        else:
            hdn = rwkv7_time_mix(hdn, c_mu[i], c_w_r[i], c_w_k[i], c_w_v[i], c_w_o[i], c_w0[i],
                                 c_w1[i], c_w2[i], c_a0[i], c_a1[i], c_a2[i], c_g1[i], c_g2[i],
                                 c_k_k[i], c_k_a[i], c_r_k[i], c_ln_g[i], c_ln_b[i])
        x = x + rmsnorm(hdn, ng[3])
        hdn = swiglu(rmsnorm(x, ng[4]), ffn2_w_gate[layer], ffn2_w_up[layer], ffn2_w_down[layer])
        x = x + 0.5 * rmsnorm(hdn, ng[5])
    return x


CHUNK = 64
N_MIXERS = 2
N_CONV_LAYERS = (DEPTH + 1) // 2
N_GDN_LAYERS = DEPTH // 2
CONV_WIDTH = 3
GDN_HEADS = 8
GDN_HEAD_DIM = D_MODEL // GDN_HEADS
GDN_QK_DIM = GDN_HEADS * GDN_HEAD_DIM
GDN_V_DIM = GDN_HEADS * GDN_HEAD_DIM
GDN_CONV_WIDTH = 4
GDN_IN_DIM = 2 * GDN_QK_DIM + 2 * GDN_V_DIM + 2 * GDN_HEADS
N_GROUPS = 8
EXPERTS_PER_GROUP = 8
N_EXPERTS = N_GROUPS * EXPERTS_PER_GROUP
TOP_K = 2
D_EXPERT = D_MODEL // 4
D_SHARED = D_MODEL // 2
MOE_BLOCK = 128


def rmsnorm_2(x, w):
    xf = x.astype(jnp.float32)
    y = xf * lax.rsqrt(jnp.mean(xf * xf, axis=-1, keepdims=True) + NORM_EPS)
    return (y * w.astype(jnp.float32)).astype(x.dtype)

def l2norm(x):
    xf = x.astype(jnp.float32)
    return xf * lax.rsqrt(jnp.sum(xf * xf, axis=-1, keepdims=True) + NORM_EPS)

def causal_dwconv(x, w):
    K = w.shape[0]
    T = x.shape[1]
    xp = jnp.pad(x, ((0, 0), (K - 1, 0), (0, 0)))
    y = xp[:, 0:T] * w[0]
    for k in range(1, K):
        y = y + xp[:, k:k + T] * w[k]
    return y

def short_conv_mixer(h, w_in, conv_w, w_out):
    bcx = h @ w_in
    b, cg, xv = jnp.split(bcx, 3, axis=-1)
    y = b * causal_dwconv(cg * xv, conv_w)
    return y @ w_out

def chunk_gated_delta_rule(q, k, v, g, beta):
    out_dtype = v.dtype
    B, T, H, Dk = q.shape
    Dv = v.shape[-1]
    n = T // CHUNK

    def blocks(a):
        a = a.astype(jnp.float32).reshape((B, n, CHUNK, H) + a.shape[3:])
        return jnp.moveaxis(a, 3, 1)

    q, k, v, g, beta = (blocks(a) for a in (q, k, v, g, beta))
    gc = jnp.cumsum(g, axis=-1)
    idx = jnp.arange(CHUNK)
    causal = idx[:, None] >= idx[None, :]
    strict = idx[:, None] > idx[None, :]
    diff = gc[..., :, None] - gc[..., None, :]
    decay = jnp.exp(jnp.where(causal, diff, -jnp.inf))
    kb = k * beta[..., None]
    lower = jnp.where(strict, jnp.einsum('bhncd,bhnsd->bhncs', kb, k) * decay, 0.0)
    rhs = jnp.concatenate([v * beta[..., None], kb * jnp.exp(gc)[..., None]], axis=-1)
    sol = lax.linalg.triangular_solve(lower, rhs, left_side=True, lower=True,
                                      unit_diagonal=True)
    u, w = sol[..., :Dv], sol[..., Dv:]
    attn = jnp.einsum('bhncd,bhnsd->bhncs', q, k) * decay
    q_dec = q * jnp.exp(gc)[..., None]
    g_last = gc[..., -1]
    k_dec = k * jnp.exp(g_last[..., None] - gc)[..., None]

    def step(S, inp):
        u_n, w_n, qd_n, kd_n, a_n, gl_n = inp
        v_new = u_n - jnp.einsum('bhcd,bhde->bhce', w_n, S)
        o_n = (jnp.einsum('bhcd,bhde->bhce', qd_n, S)
               + jnp.einsum('bhcs,bhse->bhce', a_n, v_new))
        S = S * jnp.exp(gl_n)[..., None, None] + jnp.einsum('bhcd,bhce->bhde', kd_n, v_new)
        return S, o_n

    xs = tuple(jnp.moveaxis(a, 2, 0) for a in (u, w, q_dec, k_dec, attn, g_last))
    S0 = jnp.zeros((B, H, Dk, Dv), jnp.float32)
    _, o = lax.scan(step, S0, xs)
    o = jnp.transpose(o, (1, 0, 3, 2, 4)).reshape(B, T, H, Dv)
    return o.astype(out_dtype)

def gated_deltanet_mixer(h, w_in, conv_w, a_log, dt_bias, norm_w, w_out):
    B, T, _ = h.shape
    H, Dh = GDN_HEADS, GDN_HEAD_DIM
    proj = h @ w_in
    s1 = 2 * GDN_QK_DIM + GDN_V_DIM
    s2 = s1 + GDN_V_DIM
    qkv = proj[..., :s1]
    z = proj[..., s1:s2]
    b = proj[..., s2:s2 + H]
    a = proj[..., s2 + H:]
    qkv = jax.nn.silu(causal_dwconv(qkv, conv_w))
    q = qkv[..., :GDN_QK_DIM].reshape(B, T, H, Dh)
    k = qkv[..., GDN_QK_DIM:2 * GDN_QK_DIM].reshape(B, T, H, Dh)
    v = qkv[..., 2 * GDN_QK_DIM:].reshape(B, T, H, Dh)
    q = l2norm(q) * (Dh ** -0.5)
    k = l2norm(k)
    beta = jax.nn.sigmoid(b.astype(jnp.float32))
    g = -jnp.exp(a_log.astype(jnp.float32)) * jax.nn.softplus(
        a.astype(jnp.float32) + dt_bias.astype(jnp.float32))
    o = chunk_gated_delta_rule(q, k, v, g, beta)
    o = rmsnorm_2(o, norm_w) * jax.nn.silu(z.reshape(B, T, H, Dh))
    return o.reshape(B, T, GDN_V_DIM) @ w_out

def hier_moe(h, w_rg, b_rg, w_re, b_re, w_gate, w_up, w_down, ws_gate, ws_up, ws_down, w_sg):
    B, T, D = h.shape
    xt = h.reshape(-1, D)
    N = xt.shape[0]
    gl = (xt @ w_rg + b_rg).astype(jnp.float32)
    gp = jax.nn.softmax(gl, axis=-1)
    g_sel = jnp.argmax(gl, axis=-1)
    p_sel = jnp.take_along_axis(gp, g_sel[:, None], axis=-1)[:, 0]
    el = (xt @ w_re + b_re).astype(jnp.float32).reshape(N, N_GROUPS, EXPERTS_PER_GROUP)
    el_sel = jnp.take_along_axis(el, g_sel[:, None, None], axis=1)[:, 0]
    top_v, top_i = lax.top_k(el_sel, TOP_K)
    gate = jax.nn.softmax(top_v, axis=-1) * p_sel[:, None]
    eid = g_sel[:, None] * EXPERTS_PER_GROUP + top_i
    S = N * TOP_K
    flat_e = eid.reshape(-1)
    flat_tok = jnp.repeat(jnp.arange(N), TOP_K)
    flat_gate = gate.reshape(-1)
    order = jnp.argsort(flat_e)
    e_sorted = flat_e[order]
    tok_sorted = flat_tok[order]
    gate_sorted = flat_gate[order].astype(xt.dtype)
    counts = jnp.bincount(flat_e, length=N_EXPERTS)
    starts = jnp.cumsum(counts) - counts
    padded = (counts + MOE_BLOCK - 1) // MOE_BLOCK * MOE_BLOCK
    pends = jnp.cumsum(padded)
    pstarts = pends - padded
    dest = pstarts[e_sorted] + (jnp.arange(S) - starts[e_sorted])
    n_blocks = -(-S // MOE_BLOCK) + N_EXPERTS
    P = n_blocks * MOE_BLOCK
    buf = jnp.zeros((P, D), xt.dtype).at[dest].set(xt[tok_sorted])
    block_e = jnp.minimum(
        jnp.searchsorted(pends, jnp.arange(n_blocks) * MOE_BLOCK, side='right'), N_EXPERTS - 1)

    def expert_block(args):
        xb, e = args
        hid = jax.nn.silu(xb @ w_gate[e]) * (xb @ w_up[e])
        return hid @ w_down[e]

    out = lax.map(expert_block, (buf.reshape(n_blocks, MOE_BLOCK, D), block_e)).reshape(P, D)
    y = jnp.zeros((N, D), xt.dtype).at[tok_sorted].add(out[dest] * gate_sorted[:, None])
    ys = (jax.nn.silu(xt @ ws_gate) * (xt @ ws_up)) @ ws_down
    y = y + jax.nn.sigmoid(xt @ w_sg) * ys
    return y.reshape(B, T, D)

def second_inputs(seed: int = 0) -> dict:
    key = jax.random.key(seed)
    ks = jax.random.split(key, 32)
    D = D_MODEL
    nrm = jax.random.normal
    f32 = jnp.float32
    dt = jnp.exp(jax.random.uniform(ks[11], (N_GDN_LAYERS, GDN_HEADS), f32,
                                    np.log(1e-3), np.log(1e-1)))
    return {
        "x": nrm(ks[0], (BATCH, SEQ, D), f32),
        "c": nrm(ks[1], (BATCH, D), f32),
        "ada_w": nrm(ks[2], (DEPTH, D, 6 * D), f32) * (0.3 * D ** -0.5),
        "ada_b": nrm(ks[3], (DEPTH, 6 * D), f32) * 0.02,
        "norm_w": 1.0 + 0.05 * nrm(ks[4], (DEPTH, 4, D), f32),
        "conv_in_w": nrm(ks[5], (N_CONV_LAYERS, D, 3 * D), f32) * D ** -0.5,
        "conv_w": nrm(ks[6], (N_CONV_LAYERS, CONV_WIDTH, D), f32) * CONV_WIDTH ** -0.5,
        "conv_out_w": nrm(ks[7], (N_CONV_LAYERS, D, D), f32) * D ** -0.5,
        "gdn_in_w": nrm(ks[8], (N_GDN_LAYERS, D, GDN_IN_DIM), f32) * D ** -0.5,
        "gdn_conv_w": nrm(ks[9], (N_GDN_LAYERS, GDN_CONV_WIDTH, 2 * GDN_QK_DIM + GDN_V_DIM), f32) * 0.5,
        "gdn_a_log": jnp.log(jax.random.uniform(ks[10], (N_GDN_LAYERS, GDN_HEADS), f32, 1.0, 16.0)),
        "gdn_dt_bias": dt + jnp.log(-jnp.expm1(-dt)),
        "gdn_norm_w": 1.0 + 0.05 * nrm(ks[12], (N_GDN_LAYERS, GDN_HEAD_DIM), f32),
        "gdn_out_w": nrm(ks[13], (N_GDN_LAYERS, GDN_V_DIM, D), f32) * GDN_V_DIM ** -0.5,
        "moe_group_w": nrm(ks[14], (DEPTH, D, N_GROUPS), f32) * D ** -0.5,
        "moe_group_b": nrm(ks[15], (DEPTH, N_GROUPS), f32) * 0.01,
        "moe_expert_w": nrm(ks[16], (DEPTH, D, N_EXPERTS), f32) * D ** -0.5,
        "moe_expert_b": nrm(ks[17], (DEPTH, N_EXPERTS), f32) * 0.01,
        "moe_w_gate": nrm(ks[18], (DEPTH, N_EXPERTS, D, D_EXPERT), f32) * D ** -0.5,
        "moe_w_up": nrm(ks[19], (DEPTH, N_EXPERTS, D, D_EXPERT), f32) * D ** -0.5,
        "moe_w_down": nrm(ks[20], (DEPTH, N_EXPERTS, D_EXPERT, D), f32) * D_EXPERT ** -0.5,
        "shared_w_gate": nrm(ks[21], (DEPTH, D, D_SHARED), f32) * D ** -0.5,
        "shared_w_up": nrm(ks[22], (DEPTH, D, D_SHARED), f32) * D ** -0.5,
        "shared_w_down": nrm(ks[23], (DEPTH, D_SHARED, D), f32) * D_SHARED ** -0.5,
        "shared_gate_w": nrm(ks[24], (DEPTH, D, 1), f32) * D ** -0.5,
    }

def second_block(x, c, ada_w, ada_b, norm_w, conv_in_w, conv_w, conv_out_w,
              gdn_in_w, gdn_conv_w, gdn_a_log, gdn_dt_bias, gdn_norm_w, gdn_out_w,
              moe_group_w, moe_group_b, moe_expert_w, moe_expert_b,
              moe_w_gate, moe_w_up, moe_w_down,
              shared_w_gate, shared_w_up, shared_w_down, shared_gate_w):
    cs = jax.nn.silu(c)
    for i in range(DEPTH):
        mod = (cs @ ada_w[i] + ada_b[i])[:, None, :]
        sh1, sc1, gt1, sh2, sc2, gt2 = jnp.split(mod, 6, axis=-1)
        h = rmsnorm_2(x, norm_w[i, 0]) * (1.0 + sc1) + sh1
        j = i // N_MIXERS
        if i % N_MIXERS == 0:
            y = short_conv_mixer(h, conv_in_w[j], conv_w[j], conv_out_w[j])
        else:
            y = gated_deltanet_mixer(h, gdn_in_w[j], gdn_conv_w[j], gdn_a_log[j],
                                     gdn_dt_bias[j], gdn_norm_w[j], gdn_out_w[j])
        x = x + gt1 * rmsnorm_2(y, norm_w[i, 1])
        h = rmsnorm_2(x, norm_w[i, 2]) * (1.0 + sc2) + sh2
        y = hier_moe(h, moe_group_w[i], moe_group_b[i], moe_expert_w[i], moe_expert_b[i],
                     moe_w_gate[i], moe_w_up[i], moe_w_down[i],
                     shared_w_gate[i], shared_w_up[i], shared_w_down[i], shared_gate_w[i])
        x = x + gt2 * rmsnorm_2(y, norm_w[i, 3])
    return x


def setup_inputs(seed=0):
    out = dict(first_inputs(seed))
    for name, value in second_inputs(seed + 1).items():
        if name != "x":
            out[name + "_2"] = value
    return out


def reference(
    x, norm_gains, ffn1_w_gate, ffn1_w_up, ffn1_w_down, ffn2_w_gate, ffn2_w_up, ffn2_w_down,
    ab_w_in, a_cmp_pe_k, a_cmp_w1_k, a_cmp_w2_k, a_cmp_pe_v, a_cmp_w1_v, a_cmp_w2_v, b_conv_w,
    b_conv_b, b_dt_bias, b_a_log, b_d_skip, b_norm_w, ab_w_out, c_mu, c_w_r, c_w_k, c_w_v,
    c_w_o, c_w0, c_w1, c_w2, c_a0, c_a1, c_a2, c_g1, c_g2, c_k_k, c_k_a, c_r_k, c_ln_g, c_ln_b,
    c_2, ada_w_2, ada_b_2, norm_w_2, conv_in_w_2, conv_w_2, conv_out_w_2, gdn_in_w_2,
    gdn_conv_w_2, gdn_a_log_2, gdn_dt_bias_2, gdn_norm_w_2, gdn_out_w_2, moe_group_w_2,
    moe_group_b_2, moe_expert_w_2, moe_expert_b_2, moe_w_gate_2, moe_w_up_2, moe_w_down_2,
    shared_w_gate_2, shared_w_up_2, shared_w_down_2, shared_gate_w_2,
):
    x = first_block(
        x, norm_gains, ffn1_w_gate, ffn1_w_up, ffn1_w_down, ffn2_w_gate, ffn2_w_up, ffn2_w_down,
        ab_w_in, a_cmp_pe_k, a_cmp_w1_k, a_cmp_w2_k, a_cmp_pe_v, a_cmp_w1_v, a_cmp_w2_v,
        b_conv_w, b_conv_b, b_dt_bias, b_a_log, b_d_skip, b_norm_w, ab_w_out, c_mu, c_w_r,
        c_w_k, c_w_v, c_w_o, c_w0, c_w1, c_w2, c_a0, c_a1, c_a2, c_g1, c_g2, c_k_k, c_k_a,
        c_r_k, c_ln_g, c_ln_b,
    )
    return second_block(
        x, c_2, ada_w_2, ada_b_2, norm_w_2, conv_in_w_2, conv_w_2, conv_out_w_2, gdn_in_w_2,
        gdn_conv_w_2, gdn_a_log_2, gdn_dt_bias_2, gdn_norm_w_2, gdn_out_w_2, moe_group_w_2,
        moe_group_b_2, moe_expert_w_2, moe_expert_b_2, moe_w_gate_2, moe_w_up_2, moe_w_down_2,
        shared_w_gate_2, shared_w_up_2, shared_w_down_2, shared_gate_w_2,
    )


_drawn_inputs = setup_inputs


def setup_inputs(seed=0):
    import zlib

    import numpy as np

    out = dict(_drawn_inputs(seed))
    spreads = {}
    factors = {'a_cmp_pe_k': 64.0,
     'a_cmp_pe_v': 8.0,
     'c_w1': 8.0,
     'c_w2': 8.0,
     'c_ln_b': 4.487,
     'gdn_norm_w_2': 64.0,
     'moe_group_b_2': 25.653,
     'moe_expert_b_2': 30.569}
    for name, (base, spread) in spreads.items():
        noise = np.random.default_rng([zlib.crc32(name.encode()), seed]).standard_normal(out[name].shape)
        drawn = base * np.exp(spread * noise) if base else spread * noise
        out[name] = __import__('jax').numpy.asarray(drawn.astype(out[name].dtype))
    for name, factor in factors.items():
        out[name] = (out[name] * factor).astype(out[name].dtype)
    return out
```

```python
from contextlib import ExitStack

import numpy as np
import concourse.bass as bass
import concourse.mybir as mybir
from concourse.alu_op_type import AluOpType as ALU

F32 = mybir.dt.float32
ACT = mybir.ActivationFunctionType
AX = mybir.AxisListType.X

P = 128
D = 1024
T = 256
C = D // P
TT = T // P
SLOT = 2048
RING = 8
FB = 256
FFN_BLOCKS = 2816 // FB
N_EXP = 64
N_GRP = 8
SHARED_BLOCKS = 512 // FB
NORM_EPS = 1e-6
NEG = -1e30


class Pack:

    def __init__(self):
        self.at, self.parts, self.n = {}, [], 0

    def add(self, name, a):
        a = np.asarray(a)
        full = np.zeros((P, a.shape[1]), np.float32)
        full[:a.shape[0]] = a
        self.at[name] = (self.n, a.shape[1])
        self.parts.append(full)
        self.n += a.shape[1]

    def features(self, name, a):
        self.add(name, np.asarray(a).reshape(-1, P).T)

    def rows(self, name, a):
        a = np.asarray(a).reshape(1, -1)
        self.add(name, np.broadcast_to(a, (P, a.shape[1])))


def columns_slot(w):
    out = np.zeros((P, C, FB), np.float32)
    out[:, :, :w.shape[1]] = w.reshape(C, P, w.shape[1]).transpose(1, 0, 2)
    return out.reshape(P, SLOT)


def rows_slot(w):
    return w.reshape(2, P, D).transpose(1, 0, 2).reshape(P, SLOT)


def shape_constants(pk):
    i = np.arange(P)
    s, t = i[:, None], i[None, :]
    pk.add("ident", (s == t).astype(np.float32))
    pk.add("ones", np.ones((P, P), np.float32))
    pk.add("half_ones", (s // 64 == t // 64).astype(np.float32))
    pk.add("upto", (s <= t).astype(np.float32))
    pk.add("before", (s < t).astype(np.float32))
    same = s // 64 == t // 64
    pk.add("upto64", (same & (s <= t)).astype(np.float32))
    pk.add("before64", (same & (s < t)).astype(np.float32))
    for l in (1, 2, 4, 8, 16, 32, 64):
        pk.add(f"level{l}", ((s // (2 * l) == t // (2 * l)) & (s % (2 * l) < l) & (t % (2 * l) >= l)).astype(np.float32))
    inv = (10000.0 ** (-np.arange(0, 64, 2, dtype=np.float32) / np.float32(64))).astype(np.float32)
    ang = np.arange(T, dtype=np.float32)[:, None] * inv[None, :]
    pk.add("cos", np.cos(ang).astype(np.float32).T[np.arange(P) % 32])
    pk.add("sin", np.sin(ang).astype(np.float32).T[np.arange(P) % 32])
    turn = np.zeros((P, P), np.float32)
    for m in range(P):
        turn[m + 32 if m % 64 < 32 else m - 32, m] = -1.0 if m % 64 < 32 else 1.0
    pk.add("turn", turn)
    for q in range(TT):
        tok = q * P + i[:, None]
        pk.add(f"causal{q}", np.where(np.arange(T)[None, :] <= tok, 0.0, NEG).astype(np.float32))
        keep = (np.arange(15)[None, :] * 16 + 31 <= tok)
        pk.add(f"cmp_keep{q}", np.broadcast_to(keep[:, None, :], (P, 8, 15)).reshape(P, 120).astype(np.float32))
        pk.add(f"cmp_add{q}", np.broadcast_to(np.where(keep, 0.0, NEG)[:, None, :], (P, 8, 15)).reshape(P, 120).astype(np.float32))
    seg = np.ones(T, np.float32)
    seg[::64] = 0.0
    pk.rows("not_first64", seg)
    pk.rows("rank8", np.arange(8, 0, -1).astype(np.float32))


def lay_out(a):
    a = {k: np.asarray(v) for k, v in a.items()}
    pk, slots = Pack(), []
    shape_constants(pk)

    def by_columns(w):
        for n in range(0, w.shape[1], FB):
            slots.append(columns_slot(w[:, n:n + FB]))

    def by_rows(w):
        for n in range(0, w.shape[0], FB):
            slots.append(rows_slot(w[n:n + FB]))

    def gated(g, u, d):
        for n in range(0, g.shape[1], FB):
            slots.append(columns_slot(g[:, n:n + FB]))
            slots.append(columns_slot(u[:, n:n + FB]))
            slots.append(rows_slot(d[n:n + FB]))

    for layer in range(2):
        for n in range(6):
            pk.features(f"a{layer}_gain{n}", a["norm_gains"][layer, n])
        gated(a["ffn1_w_gate"][layer], a["ffn1_w_up"][layer], a["ffn1_w_down"][layer])
        if layer == 0:
            w = a["ab_w_in"][0]
            q, kc, vc, ks, vs, kw, vw, gl, z, xbc, dt = np.split(
                w, np.cumsum([512, 128, 128, 128, 128, 128, 128, 24, 1024, 1536])[:].tolist(), axis=1)
            by_columns(xbc)
            by_columns(z)
            pair = [h for j in range(4) for h in (j, j + 4)]
            by_columns(np.concatenate([q[:, h * 64:h * 64 + 64] for h in pair], 1))
            by_columns(np.concatenate([kc, vc, ks, kw], 1))
            by_columns(np.concatenate([vs, vw], 1))
            for w1 in (a["a_cmp_w1_k"][0], a["a_cmp_w1_v"][0]):
                w1 = w1.reshape(32, 64, 64).transpose(1, 0, 2).reshape(64, SLOT)
                slots.append(np.concatenate([w1, w1], 0))
            wo = a["ab_w_out"][0]
            by_rows(np.concatenate([wo[h * 64:h * 64 + 64] for h in pair] + [wo[512:]], 0))
            pk.add("w_gl_dt", np.concatenate([gl, dt], 1).reshape(C, P, 40).transpose(1, 0, 2).reshape(P, C * 40))
            for n in ("k", "v"):
                pe = a[f"a_cmp_pe_{n}"][0].T
                pk.add(f"cmp_pe_{n}", np.concatenate([pe, pe], 0))
                pk.add(f"cmp_w2_{n}", a[f"a_cmp_w2_{n}"][0])
            for k in range(4):
                pk.features(f"ssd_conv{k}", a["b_conv_w"][0, k, 0])
            pk.features("ssd_conv_b", a["b_conv_b"][0])
            pk.rows("dt_bias", a["b_dt_bias"][0])
            pk.rows("a_log", a["b_a_log"][0])
            pk.features("d_skip", np.repeat(a["b_d_skip"][0], 64))
            pk.features("ssd_norm", a["b_norm_w"][0])
        else:
            for n in range(6):
                pk.features(f"mu{n}", a["c_mu"][0, n])
            by_columns(np.concatenate([a["c_w1"][0], a["c_a1"][0]], 1))
            by_columns(a["c_g1"][0])
            lora = np.zeros((P, 2, D), np.float32)
            lora[:64, 0], lora[:64, 1] = a["c_w2"][0], a["c_a2"][0]
            slots.append(lora.reshape(P, SLOT))
            lora = np.zeros((P, 2, D), np.float32)
            lora[:, 0], lora[:32, 1] = a["c_g2"][0][:P], a["c_g2"][0][P:]
            slots.append(lora.reshape(P, SLOT))
            for n in ("r", "k", "v"):
                by_columns(a[f"c_w_{n}"][0])
            by_columns(a["c_w_o"][0])
            for n in ("w0", "a0", "k_k", "k_a", "r_k", "ln_g", "ln_b"):
                pk.features(n, a[f"c_{n}"][0].reshape(-1))
        gated(a["ffn2_w_gate"][layer], a["ffn2_w_up"][layer], a["ffn2_w_down"][layer])

    pk.features("c", a["c_2"][0])
    for i in range(2):
        pk.features(f"ada_b{i}", a["ada_b_2"][i])
        for n in range(4):
            pk.features(f"b{i}_norm{n}", a["norm_w_2"][i, n])
        by_columns(a["ada_w_2"][i])
        if i == 0:
            for j in range(4):
                for part in range(3):
                    by_columns(a["conv_in_w_2"][0][:, part * D + j * FB:part * D + (j + 1) * FB])
            for k in range(3):
                pk.features(f"conv{k}", a["conv_w_2"][0, k])
            by_columns(a["conv_out_w_2"][0])
        else:
            by_columns(a["gdn_in_w_2"][0][:, :4096])
            pk.add("w_ba", a["gdn_in_w_2"][0][:, 4096:].reshape(C, P, 16).transpose(1, 0, 2).reshape(P, C * 16))
            for k in range(4):
                pk.features(f"gdn_conv{k}", a["gdn_conv_w_2"][0, k])
            pk.rows("gdn_a_log", a["gdn_a_log_2"][0])
            pk.rows("gdn_dt_bias", a["gdn_dt_bias_2"][0])
            pk.features("gdn_norm", a["gdn_norm_w_2"][0])
            by_columns(a["gdn_out_w_2"][0])
        router = np.concatenate([a["moe_group_w_2"][i], a["moe_expert_w_2"][i], a["shared_gate_w_2"][i]], 1)
        pk.add(f"router{i}", router.reshape(C, P, 73).transpose(1, 0, 2).reshape(P, C * 73))
        pk.rows(f"router_b{i}", np.concatenate([a["moe_group_b_2"][i], a["moe_expert_b_2"][i]]))
        for e in range(N_EXP):
            gated(a["moe_w_gate_2"][i, e], a["moe_w_up_2"][i, e], a["moe_w_down_2"][i, e])
        gated(a["shared_w_gate_2"][i], a["shared_w_up_2"][i], a["shared_w_down_2"][i])
    xT = a["x"][0].T.reshape(C, P, T).transpose(1, 0, 2)
    return np.ascontiguousarray(xT), slots, pk


class Queue:

    def __init__(self, sem):
        self.sem, self.count, self.todo, self.seen = sem, 0, [], {}

    def wait(self, *tokens):
        for tok in tokens:
            if tok is None:
                continue
            if isinstance(tok, list):
                self.wait(*tok)
            elif self.seen.get(id(tok[0]), 0) < tok[1]:
                self.seen[id(tok[0])] = tok[1]
                self.todo.append(lambda e, s=tok[0], v=tok[1]: e.wait_ge(s, v))

    def silent(self, fn):
        self.todo.append(fn)

    def do(self, fn, *tokens):
        self.wait(*tokens)
        self.count += 1
        self.todo.append(lambda e: fn(e).then_inc(self.sem, 1))
        return (self.sem, self.count)

    def play(self, e):
        for fn in self.todo:
            fn(e)


class Kernel:
    def __init__(self, nc, x_in, w_in, pack_in, out, n_slots, at):
        self.nc, self.x_in, self.w_in, self.pack_in, self.out = nc, x_in, w_in, pack_in, out
        self.n_slots, self.at = n_slots, at
        self.ctx = ExitStack()
        c = self.ctx
        sem = lambda n: c.enter_context(nc.semaphore(n))
        self.pe, self.dve = Queue(sem("pe_done")), Queue(sem("dve_done"))
        self.act, self.pool = Queue(sem("act_done")), Queue(sem("pool_done"))
        self.sp = Queue(None)
        self.in_sem, self.out_sem = sem("inputs_in"), sem("output_out")
        self.slot_sem = [sem(f"slot_in{i}") for i in range(RING)]
        sb = lambda n, s: c.enter_context(nc.sbuf_tensor(n, s, F32))
        self.ring = sb("weight_ring", [P, RING, SLOT])
        self.pk = sb("params_sb", [P, pack_in.shape[1]])
        self.x = sb("x_sb", [P, C, T])
        self.h = sb("h_sb", [P, C, T])
        self.y = sb("y_sb", [P, C, T])
        self.rms = sb("inv_rms", [P, 2, T])
        self.bank = [c.enter_context(nc.psum_tensor(f"bank{i}", [P, 512], F32)) for i in range(8)]
        self.free = {}
        self.turn = 0
        self.next_slot = 0
        self.stage_no = 0
        self.sp.silent(lambda e: e.dma_start(self.pk[:, :], pack_in).then_inc(self.in_sem, 16))
        self.sp.silent(lambda e: e.dma_start(self.x[:, :, :], x_in).then_inc(self.in_sem, 16))
        self.inputs = (self.in_sem, 32)
        for i in range(min(RING, n_slots)):
            self.load_slot(i)
        self.x_tok = self.inputs
        self.h_free = self.y_free = self.rms_free = None
        self.cs = None

    def par(self, name, lo=0, n=None, rows=P):
        o, w = self.at[name]
        return self.pk[0:rows, o + lo:o + (w if n is None else lo + n)]

    def load_slot(self, i, *after):
        self.sp.wait(*after)
        self.sp.silent(lambda e: e.dma_start(self.ring[:, i % RING, :], self.w_in[i])
                       .then_inc(self.slot_sem[i % RING], 16))

    def slot(self):
        i = self.next_slot
        self.next_slot += 1
        return i, self.ring[:, i % RING, :], (self.slot_sem[i % RING], 16 * (i // RING + 1))

    def slot_read(self, i, tok):
        if i + RING < self.n_slots:
            self.load_slot(i + RING, tok)

    def half(self, banks=(4, 5, 6, 7)):
        ps, b, fr = self.full(banks)
        return ps[:, 0:T], b, fr

    def full(self, banks=(4, 5, 6, 7)):
        b = banks[self.turn % len(banks)]
        self.turn += 1
        return self.bank[b], b, self.free.get(b)

    def read_by(self, b, *toks):
        self.free[b] = list(toks)

    def mm(self, out, lhsT, rhs, start, stop, shared=False):
        self.pe.silent(lambda e: e.matmul(out, lhsT, rhs, start=start, stop=stop, skip_group_check=shared))

    def mm_end(self, out, lhsT, rhs, start, stop, shared=False):
        return self.pe.do(lambda e: e.matmul(out, lhsT, rhs, start=start, stop=stop, skip_group_check=shared))

    def transposed(self, out, in_, last=False):
        n = in_.shape[0]
        ident = self.par("ident", 0, n, n)
        if last:
            return self.pe.do(lambda e: e.transpose(out, in_, ident))
        self.pe.silent(lambda e: e.transpose(out, in_, ident))

    def tt(self, q, out, a, b, op, *tok):
        return q.do(lambda e: e.tensor_tensor(out, a, b, op), *tok)

    def ts(self, q, out, a, s1, s2, op0, op1, *tok):
        if op1 is None:
            return q.do(lambda e: e.tensor_scalar(out, a, s1, None, op0), *tok)
        return q.do(lambda e: e.tensor_scalar(out, a, s1, s2, op0, op1), *tok)

    def stt(self, out, a, s, b, op0, op1, *tok):
        return self.dve.do(lambda e: e.scalar_tensor_tensor(out=out, in0=a, scalar=s, in1=b, op0=op0, op1=op1), *tok)

    def func(self, out, a, f, *tok, scale=1.0, bias=0.0, accum=None):
        if accum is None:
            return self.act.do(lambda e: e.activation(out, a, f, scale=scale, bias=bias), *tok)
        return self.act.do(lambda e: e.activation(out, a, f, scale=scale, bias=bias, accum_out=accum), *tok)

    def copy(self, q, out, a, *tok):
        if q is self.act:
            return self.func(out, a, ACT.Copy, *tok)
        return q.do(lambda e: e.tensor_copy(out, a), *tok)

    def reduce(self, out, a, op, *tok):
        return self.dve.do(lambda e: e.tensor_reduce(out, a, AX, op), *tok)

    def barrier(self):
        toks = [(q.sem, q.count) for q in (self.pe, self.dve, self.act, self.pool) if q.count]
        for q in (self.pe, self.dve, self.act, self.pool):
            q.wait(*toks)

    def stage(self):
        self.barrier()
        self.stage_no += 1
        st = ExitStack()
        no, nc = self.stage_no, self.nc

        def sb(name, shape):
            return st.enter_context(nc.sbuf_tensor(f"{name}_{no}", shape, F32))
        return st, sb

    def inv_rms(self, squares, n, eps, toks, lhs="ones", scale=1.0, out=None):
        ps, key, fr = self.half()
        self.pe.wait(fr, self.inputs)
        for c, s in enumerate(squares):
            self.pe.wait(toks[c])
            if c == len(squares) - 1:
                tok = self.mm_end(ps[:, 0:s.shape[-1]], self.par(lhs), s, c == 0, True)
            else:
                self.mm(ps[:, 0:s.shape[-1]], self.par(lhs), s, c == 0, False)
        w = squares[0].shape[-1]
        out = self.rms[:, 0, :] if out is None else out
        s2 = 1.0 / (scale * scale)
        t = self.ts(self.dve, out, ps[:, 0:w], s2 / n, s2 * eps, ALU.mult, ALU.add, tok, self.rms_free)
        self.read_by(key, t)
        t = self.func(out, out, ACT.Ln, t)
        return self.func(out, out, ACT.Exp, t, scale=-0.5)

    def norm_x(self, gain, shift=None, tok=None):
        sq = self.y
        toks = []
        for n in range(4):
            t = self.func(sq[:, 2 * n:2 * n + 2, :], self.x[:, 2 * n:2 * n + 2, :], ACT.Square, self.x_tok, self.y_free)
            toks += [t, t]
        r = self.inv_rms([sq[:, c, :] for c in range(C)], D, NORM_EPS, toks)
        self.y_free = (self.pe.sem, self.pe.count)
        out = []
        for c in range(C):
            t = self.stt(self.h[:, c, :], self.x[:, c, :], gain[:, c:c + 1], self.rms[:, 0, :], ALU.mult, ALU.mult,
                         r, self.h_free, tok)
            if shift is not None:
                t = self.func(self.h[:, c, :], self.h[:, c, :], ACT.Identity, t, bias=shift[:, c:c + 1])
            out.append(t)
        self.rms_free = (self.dve.sem, self.dve.count)
        return out

    def add_back(self, y_toks, gain, scale, tok=None):
        toks, ysb = [], []
        sq = self.h
        for b in range(4):
            t = self.func(sq[:, 2 * b:2 * b + 2, :], self.bank[b][:, :].rearrange("p (c t) -> p c t", c=2), ACT.Square, y_toks[b])
            toks += [t, t]
            v = self.copy(self.dve, self.y[:, 2 * b:2 * b + 2, :], self.bank[b][:, :].rearrange("p (c t) -> p c t", c=2), y_toks[b], self.y_free, t)
            self.read_by(b, t, v)
            ysb.append(v)
        r = self.inv_rms([sq[:, c, :] for c in range(C)], D, NORM_EPS, toks, scale=scale)
        self.h_free = (self.pe.sem, self.pe.count)
        xt = []
        for c in range(C):
            t = self.stt(self.y[:, c, :], self.y[:, c, :], gain[:, c:c + 1], self.rms[:, 0, :], ALU.mult, ALU.mult, r, ysb[c // 2], tok)
            t = self.tt(self.pool, self.x[:, c, :], self.x[:, c, :], self.y[:, c, :], ALU.add, t, self.x_tok)
            xt.append(t)
        self.rms_free = (self.dve.sem, self.dve.count)
        self.x_tok = xt[-1]
        self.y_free = xt[-1]

    def gated_blocks(self, h_toks, n_blocks, gates=None, gate_tok=None, first=True, last=True, index=lambda b: b):
        st, sb = (self.scope, self.sbs)
        silu, hid = self.silu, self.hid
        pend = []

        def down():
            u, i_d, wd, d_tok, hid_tok = pend.pop(0)
            fc = u % 2
            self.pe.wait(hid_tok, d_tok)
            if u == 0:
                for b in range(4):
                    self.pe.wait(self.free.get(b))
            end = last and u == 2 * n_blocks - 1
            toks = []
            for c in range(C):
                args = (self.bank[c // 2][:, (c % 2) * T:(c % 2 + 1) * T], wd[:, fc * D + c * P:fc * D + (c + 1) * P],
                        hid[:, u % 4, :], first and u == 0 and c % 2 == 0, end and c % 2 == 1, True)
                if c == C - 1 or (end and c % 2):
                    toks.append(self.mm_end(*args))
                else:
                    self.mm(*args)
            self.hid_free[u % 4] = toks[-1]
            if fc == 1:
                self.slot_read(i_d, toks[-1])
            return toks

        for b in range(n_blocks):
            i_g, wg, g_tok = self.slot()
            i_u, wu, u_tok = self.slot()
            i_d, wd, d_tok = self.slot()
            for fc in range(2):
                u = 2 * b + fc
                bk = 4 + u % 3
                ps = self.bank[bk]
                self.pe.wait(self.free.get(bk))
                self.pe.wait(g_tok)
                for c in range(C):
                    if u == 0:
                        self.pe.wait(h_toks[c])
                    self.mm(ps[:, 0:T], wg[:, c * FB + fc * P:c * FB + (fc + 1) * P], self.h[:, c, :], c == 0, c == C - 1)
                self.pe.wait(u_tok)
                for c in range(C):
                    a = (ps[:, T:2 * T], wu[:, c * FB + fc * P:c * FB + (fc + 1) * P], self.h[:, c, :], c == 0, c == C - 1)
                    if c < C - 1:
                        self.mm(*a)
                    else:
                        up = self.mm_end(*a)
                if fc == 1:
                    self.slot_read(i_g, up)
                    self.slot_read(i_u, up)
                if gates is not None and fc == 0:
                    self.pe.wait(gate_tok, self.free.get(7))
                    gp = self.bank[7][:, 0:T]
                    n = gates.shape[0]
                    e = index(b)
                    gb = self.mm_end(gp, self.par("ident", e, 1, n).to_broadcast([n, P]), gates, True, True)
                    g_sb = self.gate_sb[:, b % 2, :]
                    gc = self.copy(self.act, g_sb, gp, gb, self.gate_free[b % 2])
                    self.read_by(7, gc)
                s = self.func(silu[:, u % 4, :], ps[:, 0:T], ACT.Silu, up, self.silu_free[u % 4])
                m = self.tt(self.dve, hid[:, u % 4, :], silu[:, u % 4, :], ps[:, T:2 * T], ALU.mult, s, up, self.hid_free[u % 4])
                self.silu_free[u % 4] = m
                self.read_by(bk, s, m)
                if gates is not None:
                    m = self.tt(self.dve, hid[:, u % 4, :], hid[:, u % 4, :], g_sb, ALU.mult, m, gc)
                    self.gate_free[b % 2] = m
                pend.append((u, i_d, wd, d_tok, m))
                if len(pend) > 2:
                    toks = down()
        while pend:
            toks = down()
        return toks

    def gated_scope(self):
        self.scope, sb = self.stage()
        self.sbs = sb
        self.silu, self.hid, self.gate_sb = sb("silu", [P, 4, T]), sb("hid", [P, 4, T]), sb("gate_rows", [P, 2, T])
        self.silu_free, self.hid_free, self.gate_free = [None] * 4, [None] * 4, [None] * 2

    def ffn(self, g_in, g_out):
        self.gated_scope()
        h_toks = self.norm_x(self.par(g_in))
        y = self.gated_blocks(h_toks, FFN_BLOCKS)
        self.add_back(y, self.par(g_out), 0.5)
        self.scope.close()

    def columns(self, act_in, toks, n_slots, consume, tiles=2):
        for n in range(n_slots):
            i, w, tok = self.slot()
            for fc in range(tiles):
                ps, key, fr = self.half()
                self.pe.wait(fr, tok)
                for c in range(C):
                    self.pe.wait(toks[c])
                    a = (ps, w[:, c * FB + fc * P:c * FB + (fc + 1) * P], act_in[:, c, :], c == 0, c == C - 1)
                    if c < C - 1:
                        self.mm(*a)
                    else:
                        end = self.mm_end(*a)
                self.read_by(key, consume(2 * n + fc, ps, end))
            self.slot_read(i, end)

    def project_out(self, src, n_chunks, toks):
        for b in range(4):
            self.pe.wait(self.free.get(b))
        out = []
        for n in range(n_chunks // 2):
            i, w, tok = self.slot()
            self.pe.wait(tok)
            for k in range(2):
                kc = 2 * n + k
                self.pe.wait(toks[kc])
                end = kc == n_chunks - 1
                for c in range(C):
                    a = (self.bank[c // 2][:, (c % 2) * T:(c % 2 + 1) * T], w[:, k * D + c * P:k * D + (c + 1) * P],
                         src(kc), kc == 0 and c % 2 == 0, end and c % 2 == 1, True)
                    if (end and c % 2) or (k == 1 and c == C - 1):
                        t = self.mm_end(*a)
                        if end:
                            out.append(t)
                    else:
                        self.mm(*a)
            self.slot_read(i, t)
        return out

    def project_columns_out(self, src, toks):
        out = []
        for n in range(4):
            i, w, tok = self.slot()
            self.pe.wait(tok, self.free.get(n))
            for fc in range(2):
                for c in range(C):
                    self.pe.wait(toks[c])
                    a = (self.bank[n][:, fc * T:(fc + 1) * T], w[:, c * FB + fc * P:c * FB + (fc + 1) * P], src[:, c, :], c == 0, c == C - 1)
                    if c < C - 1:
                        self.mm(*a)
                    else:
                        t = self.mm_end(*a)
            self.slot_read(i, t)
            out.append(t)
        return out

    def finish(self):
        self.sp.wait(self.x_tok)
        self.sp.silent(lambda e: e.dma_start(self.out, self.x[:, :, :]).then_inc(self.out_sem, 16))
        self.sp.silent(lambda e: e.wait_ge(self.out_sem, 16))
        block = self.ctx.enter_context(self.nc.Block())

        @block.sync
        def _(e):
            self.sp.play(e)

        @block.tensor
        def _(e):
            self.pe.play(e)

        @block.vector
        def _(e):
            self.dve.play(e)

        @block.scalar
        def _(e):
            self.act.play(e)

        @block.gpsimd
        def _(e):
            self.pool.play(e)
        self.ctx.close()

    def silu_c(self):
        self.cs = self.ctx.enter_context(self.nc.sbuf_tensor("silu_c", [P, C], F32))
        self.mod = [self.ctx.enter_context(self.nc.sbuf_tensor(f"mod{i}", [P, 6 * C], F32)) for i in range(2)]
        self.gain = self.ctx.enter_context(self.nc.sbuf_tensor("mod_gain", [P, 2, 4, C], F32))
        self.cs_tok = self.func(self.cs[:, :], self.par("c"), ACT.Silu, self.inputs)

    def modulation(self, i):
        if self.cs is None:
            self.silu_c()
        self.pe.wait(self.cs_tok)
        ps, b, fr = self.full()
        self.pe.wait(fr)
        for n in range(6 * D // FB):
            s, w, tok = self.slot()
            self.pe.wait(tok)
            for fc in range(2):
                j = 2 * n + fc
                for c in range(C):
                    a = (ps[:, j:j + 1], w[:, c * FB + fc * P:c * FB + (fc + 1) * P], self.cs[:, c:c + 1], c == 0, c == C - 1)
                    if c == C - 1 and fc == 1:
                        end = self.mm_end(*a)
                    else:
                        self.mm(*a)
            self.slot_read(s, end)
        mod, g = self.mod[i], self.gain
        t = self.tt(self.dve, mod[:, :], ps[:, 0:6 * C], self.par(f"ada_b{i}"), ALU.add, end, self.inputs)
        self.read_by(b, t)
        part = lambda n: mod[:, n * C:(n + 1) * C]
        toks = []
        for n, (m, w) in enumerate(((1, 0), (4, 2))):
            toks.append(self.stt(g[:, i, w, :], part(m), 1.0, self.par(f"b{i}_norm{w}"), ALU.add, ALU.mult, t))
        for m, w in ((2, 1), (5, 3)):
            toks.append(self.tt(self.dve, g[:, i, w, :], part(m), self.par(f"b{i}_norm{w}"), ALU.mult, t))
        self.mod_tok = toks[-1]

    def first_equal(self, out, vals, best, tmp, tok):
        t = self.ts(self.dve, tmp, vals, best, None, ALU.is_equal, None, tok)
        t = self.tt(self.dve, tmp, tmp, self.par("rank8"), ALU.mult, t)
        t = self.reduce(out[:, 0:1], tmp, ALU.max, t)
        t = self.ts(self.dve, tmp, tmp, out[:, 0:1], None, ALU.is_equal, None, t)
        return self.copy(self.dve, out, tmp, t)

    def router(self, i, sb, h_toks):
        gates_T = sb("gates_T", [N_EXP + 1, T])
        done = []
        for q in range(TT):
            ps, key, fr = self.half()
            self.pe.wait(fr, self.inputs)
            for c in range(C):
                self.pe.wait(h_toks[c])
                a = (ps[:, 0:73], self.h[:, c, q * P:(q + 1) * P], self.par(f"router{i}", c * 73, 73), c == 0, c == C - 1)
                end = self.mm_end(*a) if c == C - 1 else self.mm(*a)
            lg, s = sb(f"logits{q}", [P, 73]), sb(f"route{q}", [P, 96])
            t = self.tt(self.dve, lg[:, 0:72], ps[:, 0:72], self.par(f"router_b{i}"), ALU.add, end)
            gates = sb(f"gates{q}", [P, N_EXP + 1])
            t0 = self.func(gates[:, N_EXP:N_EXP + 1], ps[:, 72:73], ACT.Sigmoid, end, t)
            self.read_by(key, t, t0)
            gl, el = lg[:, 0:8], lg[:, 8:72]
            best, psel, tmp, grp, tmp2 = s[:, 0:1], s[:, 1:2], s[:, 8:16], s[:, 16:24], s[:, 24:32]
            t = self.reduce(best, gl, ALU.max, t)
            t1 = self.first_equal(grp, gl, best, tmp, t)
            t = self.ts(self.dve, tmp2, gl, best, None, ALU.subtract, None, t)
            t = self.func(tmp2, tmp2, ACT.Exp, t, accum=psel)
            t2 = self.dve.do(lambda e, psel=psel: e.reciprocal(psel, psel), t)
            prod = sb(f"picked{q}", [P, N_EXP])
            v = lambda a: a.rearrange("p (g e) -> p g e", g=N_GRP)
            t = self.tt(self.dve, v(prod[:, :]), v(el), grp.unsqueeze(2).to_broadcast([P, N_GRP, 8]), ALU.mult, t1)
            els = s[:, 32:40]
            t = self.reduce(els, prod[:, :].rearrange("p (g e) -> p e g", g=N_GRP), ALU.add, t)
            m1, m2, e1, e2, g1, g2 = s[:, 2:3], s[:, 3:4], s[:, 40:48], s[:, 48:56], s[:, 4:5], s[:, 5:6]
            t = self.reduce(m1, els, ALU.max, t)
            t = self.first_equal(e1, els, m1, tmp, t)
            rest = s[:, 56:64]
            t = self.stt(rest, e1, NEG, els, ALU.mult, ALU.add, t)
            t = self.reduce(m2, rest, ALU.max, t)
            t = self.first_equal(e2, rest, m2, tmp, t)
            t = self.tt(self.dve, g2, m2, m1, ALU.subtract, t)
            t = self.func(g2, g2, ACT.Exp, t)
            t = self.ts(self.dve, g1, g2, 1.0, None, ALU.add, None, t)
            t = self.dve.do(lambda e, g1=g1: e.reciprocal(g1, g1), t)
            t = self.tt(self.dve, g1, g1, psel, ALU.mult, t, t2)
            t = self.tt(self.dve, g2, g2, g1, ALU.mult, t)
            t = self.ts(self.dve, e1, e1, g1, None, ALU.mult, None, t)
            t = self.stt(e1, e2, g2, e1, ALU.mult, ALU.add, t)
            t = self.tt(self.dve, v(gates[:, 0:N_EXP]), grp.unsqueeze(2).to_broadcast([P, N_GRP, 8]),
                        e1.unsqueeze(1).to_broadcast([P, N_GRP, 8]), ALU.mult, t)
            ps, key, fr = self.half()
            self.pe.wait(fr, t, t0)
            end = self.transposed(ps[0:N_EXP + 1, 0:P], gates[:, :], last=True)
            t = self.copy(self.dve, gates_T[:, q * P:(q + 1) * P], ps[0:N_EXP + 1, 0:P], end)
            self.read_by(key, t)
            done.append(t)
        return gates_T, done

    def moe(self, i):
        self.gated_scope()
        part = lambda n: self.mod[i][:, n * C:(n + 1) * C]
        h_toks = self.norm_x(self.gain[:, i, 2, :], part(3), self.mod_tok)
        gates, g_tok = self.router(i, self.sbs, h_toks)
        y = self.gated_blocks(h_toks, N_EXP + SHARED_BLOCKS, gates[:, :], g_tok, index=lambda b: min(b, N_EXP))
        self.add_back(y, self.gain[:, i, 3, :], 1.0)
        self.scope.close()

    def conv_mixer(self, i):
        st, sb = self.stage()
        part = lambda n: self.mod[i][:, n * C:(n + 1) * C]
        h_toks = self.norm_x(self.gain[:, i, 0, :], part(0), self.mod_tok)
        K = 3
        b_T, u, g_T = sb("conv_b", [P, C, T]), sb("conv_u", [P, C, K - 1 + T]), sb("conv_gate", [P, 2, T])
        out, taps = sb("conv_out", [P, C, T]), sb("conv_taps", [P, 2, T])
        z = self.pool.do(lambda e: e.memset(u[:, :, 0:K - 1], 0.0))
        gate_free, taps_free, toks = [None] * 2, [None] * 2, []
        for j in range(4):
            tok = {}

            def keep(part_no):
                def consume(n, ps, end):
                    c = 2 * j + n
                    if part_no == 0:
                        t = self.copy(self.act, b_T[:, c, :], ps, end)
                    elif part_no == 1:
                        t = self.copy(self.act, g_T[:, n, :], ps, end, gate_free[n])
                    else:
                        t = self.tt(self.dve, u[:, c, K - 1:], g_T[:, n, :], ps, ALU.mult, end, tok[1, n])
                        gate_free[n] = t
                    tok[part_no, n] = t
                    return t
                return consume
            for part_no in range(3):
                self.columns(self.h, h_toks, 1, keep(part_no))
            for n in range(2):
                c = 2 * j + n
                t = self.ts(self.dve, taps[:, n, :], u[:, c, 0:T], self.par("conv0")[:, c:c + 1], None, ALU.mult, None, tok[2, n], z, taps_free[n])
                for k in range(1, K):
                    t = self.stt(taps[:, n, :], u[:, c, k:k + T], self.par(f"conv{k}")[:, c:c + 1], taps[:, n, :], ALU.mult, ALU.add, t)
                t = self.tt(self.pool, out[:, c, :], taps[:, n, :], b_T[:, c, :], ALU.mult, t, tok[0, n])
                taps_free[n] = t
                toks.append(t)
        self.add_back(self.project_columns_out(out, toks), self.gain[:, i, 1, :], 1.0)
        st.close()
    def conv_chunk(self, out, src, taps, bias, c, n_taps, tok, out_free=None):
        w = lambda k: self.par(f"{taps}{k}")[:, c:c + 1]
        if bias is None:
            t = self.ts(self.dve, out, src[:, 0:T], w(0), None, ALU.mult, None, tok, out_free)
        else:
            t = self.ts(self.dve, out, src[:, 0:T], w(0), bias[:, c:c + 1], ALU.mult, ALU.add, tok, out_free)
        for k in range(1, n_taps):
            t = self.stt(out, src[:, k:k + T], w(k), out, ALU.mult, ALU.add, t)
        return t

    def softplus(self, v, tmp, tok):
        t = self.stt(tmp, v, -1.0, v, ALU.mult, ALU.max, tok)
        t = self.func(tmp, tmp, ACT.Exp, t, scale=-1.0)
        t = self.func(tmp, tmp, ACT.Ln, t, bias=self.par("ones", 0, 1))
        return self.stt(v, v, 0.0, tmp, ALU.max, ALU.add, t)

    def rotate(self, dst, src, tok, tmp, tmp_free):
        ps, b, fr = self.half()
        self.pe.wait(fr, tok)
        end = self.mm_end(ps, self.par("turn"), src, True, True)
        t = self.tt(self.dve, tmp, ps, self.par("sin"), ALU.mult, end, tmp_free)
        self.read_by(b, t)
        t2 = self.tt(self.pool, src, src, self.par("cos"), ALU.mult, end)
        return self.tt(self.dve, dst, src, tmp, ALU.add, t, t2)

    def nsa_ssd_mixer(self):
        st, sb = self.stage()
        h_toks = self.norm_x(self.par("a0_gain2"))
        K, G = 4, 2
        mix = sb("mix_in", [P, 12, T])
        silu_z = sb("silu_z", [P, C, T])
        xbc = sb("xbc", [P, 12, T])
        small = sb("gate_dt", [P, TT, 40])
        outer = ExitStack()
        tmp_sb = lambda n, s: outer.enter_context(self.nc.sbuf_tensor(f"{n}_{self.stage_no}", s, F32))
        raw, taps = tmp_sb("xbc_raw", [P, 2, K - 1 + T]), tmp_sb("xbc_taps", [P, 2, T])
        z0 = self.pool.do(lambda e: e.memset(raw[:, :, 0:K - 1], 0.0))
        raw_free, taps_free, xbc_tok = [None] * 2, [None] * 2, [None] * 12

        def conv_in(c, ps, end):
            n = c % 2
            t = self.copy(self.act, raw[:, n, K - 1:], ps, end, raw_free[n])
            v = self.conv_chunk(taps[:, n, :], raw[:, n, :], "ssd_conv", self.par("ssd_conv_b"), c, K, [t, z0], taps_free[n])
            raw_free[n] = v
            xbc_tok[c] = taps_free[n] = self.func(xbc[:, c, :], taps[:, n, :], ACT.Silu, v)
            return t
        self.columns(self.h, h_toks, 6, conv_in)
        z_tok = [None] * C

        def z_in(c, ps, end):
            z_tok[c] = self.func(silu_z[:, c, :], ps, ACT.Silu, end)
            return z_tok[c]
        self.columns(self.h, h_toks, 4, z_in)
        small_tok = []
        for q in range(TT):
            ps, b, fr = self.half()
            self.pe.wait(fr, self.inputs)
            for c in range(C):
                a = (ps[:, 0:40], self.h[:, c, q * P:(q + 1) * P], self.par("w_gl_dt", c * 40, 40), c == 0, c == C - 1)
                end = self.mm_end(*a) if c == C - 1 else self.mm(*a)
            t = self.func(small[:, q, 0:24], ps[:, 0:24], ACT.Sigmoid, end)
            t2 = self.tt(self.dve, small[:, q, 24:40], ps[:, 24:40], self.par("dt_bias"), ALU.add, end, t)
            self.read_by(b, t2)
            small_tok.append([t, t2])
        outer.close()
        self.barrier()
        self.attention(mix, small, h_toks)
        self.barrier()
        self.ssd(mix, small, xbc, silu_z)
        toks = [(self.dve.sem, self.dve.count)] * 12
        self.add_back(self.project_out(lambda c: mix[:, c, :], 12, toks), self.par("a0_gain3"), 1.0)
        st.close()

    def attention(self, mix, small, h_toks):
        st = ExitStack()
        sb = lambda n, s: st.enter_context(self.nc.sbuf_tensor(f"{n}_{self.stage_no}", s, F32))
        qT, kv, v_tok = sb("q_T", [P, 4, T]), sb("kc_vc_ks_kw_T", [P, 4, T]), sb("vs_vw", [P, TT, T])
        tmp = sb("rope_tmp", [P, 2, T])
        tmp_free, rope_tok, n_rope = [None] * 2, {}, [0]

        def rope_into(dst, name):
            def consume(c, ps, end):
                t = self.copy(self.act, dst[:, c, :], ps, end)
                if name == "q" or c != 1:
                    n = n_rope[0] % 2
                    n_rope[0] += 1
                    rope_tok[name, c] = tmp_free[n] = self.rotate(dst[:, c, :], dst[:, c, :], t, tmp[:, n, :], tmp_free[n])
                else:
                    rope_tok[name, c] = t
                return t
            return consume
        self.columns(self.h, h_toks, 2, rope_into(qT, "q"))
        self.columns(self.h, h_toks, 2, rope_into(kv, "kv"))
        i, w, tok = self.slot()
        v_done = []
        self.pe.wait(tok)
        for q in range(TT):
            ps, b, fr = self.half()
            self.pe.wait(fr)
            for c in range(C):
                a = (ps, self.h[:, c, q * P:(q + 1) * P], w[:, c * FB:(c + 1) * FB], c == 0, c == C - 1)
                end = self.mm_end(*a) if c == C - 1 else self.mm(*a)
            v_done.append(self.copy(self.act, v_tok[:, q, :], ps, end))
            self.read_by(b, v_done[-1])
        self.slot_read(i, end)
        n_cmp = 15
        hid = sb("cmp_hidden", [64, 2, 2, n_cmp])
        bias = sb("cmp_bias", [64, 2])
        k_cmp, v_cmp = sb("k_cmp", [P, n_cmp]), sb("v_cmp", [n_cmp, P])
        cmp_tok = []
        for n, (name, chunk) in enumerate((("k", 0), ("v", 1))):
            i, w, tok = self.slot()
            self.pe.wait(tok, rope_tok["kv", chunk], self.inputs)
            parts = []
            for g in range(2):
                base = slice(g * 64, g * 64 + 64)
                ps, b, fr = self.half()
                self.pe.wait(fr)
                for l in range(32):
                    if g == 0:
                        self.mm(ps[0:64, 32:33], w[base, l * 64:(l + 1) * 64], self.par(f"cmp_pe_{name}", l, 1, 64), l == 0, l == 31)
                for l in range(32):
                    a = (ps[0:64, 0:n_cmp], w[base, l * 64:(l + 1) * 64], kv[base, chunk, l:l + 16 * (n_cmp - 1) + 1:16], l == 0, l == 31)
                    end = self.mm_end(*a) if l == 31 else self.mm(*a)
                parts.append((ps, b, end))
            self.slot_read(i, end)
            for g, (ps, b, end) in enumerate(parts):
                if g == 0:
                    t = tb = self.copy(self.dve, bias[:, n:n + 1], ps[0:64, 32:33], end)
                t = self.func(hid[:, n, g, :], ps[0:64, 0:n_cmp], ACT.Silu, end, tb, bias=bias[:, n:n + 1])
                self.read_by(b, t)
            ps, b, fr = self.half()
            self.pe.wait(fr, t)
            w2 = self.par(f"cmp_w2_{name}", rows=64)
            for g in range(2):
                if n == 0:
                    end = self.mm_end(ps[g * 64:g * 64 + 64, 0:n_cmp], w2, hid[:, n, g, :], True, True)
                else:
                    end = self.mm_end(ps[0:n_cmp, g * 64:g * 64 + 64], hid[:, n, g, :], w2, True, True)
            t = self.copy(self.dve, k_cmp[:, :] if n == 0 else v_cmp[:, :], ps[:, 0:n_cmp] if n == 0 else ps[0:n_cmp, 0:P], end)
            self.read_by(b, t)
            cmp_tok.append(t)
        all_rope = [rope_tok["q", c] for c in range(4)] + [rope_tok["kv", 2], rope_tok["kv", 3]]
        scale = 64.0 ** -0.5
        p_buf = sb("probs", [P, 2, 2, T])
        pT = sb("probs_T", [P, 2, 4, P])
        stat = sb("softmax_stats", [P, 2, 8])
        pc, pcT, cs = sb("cmp_probs", [P, 8, n_cmp]), sb("cmp_probs_T", [n_cmp, 8, P]), sb("cmp_stats", [P, 3, 8])
        p_free, pT_free, pc_free, pcT_free = [None] * 2, [None] * 2, None, None
        out_free = None
        for q in range(TT):
            tq = slice(q * P, (q + 1) * P)
            nk = (q + 1) * P
            t = None
            for half in range(2):
                ps, b, fr = self.half()
                self.pe.wait(fr, all_rope, cmp_tok)
                base = slice(half * 64, half * 64 + 64)
                for j in range(4):
                    end = self.mm_end(ps[:, j * 16:j * 16 + n_cmp], qT[base, j, tq], k_cmp[base, :], True, True)
                add = self.par(f"cmp_add{q}").rearrange("p (h c) -> p h c", h=8)[:, 0:4, :]
                t = self.tt(self.dve, pc[:, half * 4:half * 4 + 4, :], ps[:, 0:64].rearrange("p (h c) -> p h c", h=4)[:, :, 0:n_cmp],
                            add, ALU.add, end, pc_free)
                self.read_by(b, t)
            mx, sm, sc = cs[:, 0, :], cs[:, 1, :], cs[:, 2, :]
            bc = lambda a: a.unsqueeze(2).to_broadcast([P, 8, n_cmp])
            t = self.reduce(mx, pc[:, :, :], ALU.max, t)
            t = self.tt(self.dve, pc[:, :, :], pc[:, :, :], bc(mx), ALU.subtract, t)
            t = self.func(pc[:, :, :], pc[:, :, :], ACT.Exp, t, scale=scale)
            t = self.tt(self.dve, pc[:, :, :], pc[:, :, :], self.par(f"cmp_keep{q}").rearrange("p (h c) -> p h c", h=8), ALU.mult, t)
            t = self.reduce(sm, pc[:, :, :], ALU.add, t)
            t = self.ts(self.dve, sm, sm, 1e-30, None, ALU.max, None, t)
            t = self.dve.do(lambda e: e.reciprocal(sc, sm), t)
            t = self.tt(self.dve, sc, sc, small[:, q, 0:24:3], ALU.mult, t)
            t = self.tt(self.dve, pc[:, :, :], pc[:, :, :], bc(sc), ALU.mult, t)
            for n in range(2):
                ps, b, fr = self.full()
                self.pe.wait(fr, t)
                for m in range(4):
                    end = self.transposed(ps[0:n_cmp, m * P:(m + 1) * P], pc[:, 4 * n + m, :], last=m == 3)
                tc = self.copy(self.act, pcT[:, 4 * n:4 * n + 4, :], ps[0:n_cmp, :].rearrange("c (m t) -> c m t", m=4), end, pcT_free)
                self.read_by(b, tc)
            pc_free = end
            o_bank = q
            self.pe.wait(self.free.get(o_bank), out_free)
            for h in range(8):
                j, half, n = h % 4, h // 4, h % 2
                base = slice(half * 64, half * 64 + 64)
                ps, b, fr = self.full()
                self.pe.wait(fr)
                for m in range(2):
                    end = self.mm_end(ps[:, m * T:m * T + nk], qT[base, j, tq], kv[base, 2 + m, 0:nk], True, True)
                view = ps[:, :].rearrange("p (m k) -> p m k", m=2)[:, :, 0:nk]
                pb, s = p_buf[:, n, :, 0:nk], stat[:, n, :]
                mask = self.par(f"causal{q}", 0, nk).unsqueeze(1).to_broadcast([P, 2, nk])
                t = self.tt(self.dve, pb, view, mask, ALU.add, end, p_free[n])
                self.read_by(b, t)
                t = self.reduce(s[:, 0:2], pb, ALU.max, t)
                t = self.ts(self.dve, s[:, 0:2], s[:, 0:2], -scale, None, ALU.mult, None, t)
                for m in range(2):
                    te = self.func(p_buf[:, n, m, 0:nk], p_buf[:, n, m, 0:nk], ACT.Exp, t, scale=scale, bias=s[:, m:m + 1], accum=s[:, 2 + m:3 + m])
                t = self.dve.do(lambda e, s=s: e.reciprocal(s[:, 4:6], s[:, 2:4]), te)
                t = self.tt(self.dve, s[:, 4:6], s[:, 4:6], small[:, q, 3 * h + 1:3 * h + 3], ALU.mult, t)
                t = self.tt(self.dve, pb, pb, s[:, 4:6].unsqueeze(2).to_broadcast([P, 2, nk]), ALU.mult, t)
                ps, b, fr = self.full()
                self.pe.wait(fr, t)
                pairs = [(m, kt) for m in range(2) for kt in range(q + 1)]
                for x, (m, kt) in enumerate(pairs):
                    end = self.transposed(ps[:, x * P:(x + 1) * P], p_buf[:, n, m, kt * P:(kt + 1) * P], last=x == len(pairs) - 1)
                p_free[n] = end
                w = len(pairs) * P
                t = self.copy(self.act, pT[:, n, 0:len(pairs), :], ps[:, 0:w].rearrange("p (x t) -> p x t", t=P), end, pT_free[n])
                self.read_by(b, t)
                o = self.bank[o_bank][base, j * P:(j + 1) * P]
                self.pe.wait(tc, t, v_done)
                self.mm(o, v_cmp[:, half * 64:half * 64 + 64], pcT[:, half * 4 + j, :], True, False)
                for x, (m, kt) in enumerate(pairs):
                    a = (o, v_tok[:, kt, m * P + half * 64:m * P + half * 64 + 64], pT[:, n, x, :], False, x == len(pairs) - 1)
                    end = self.mm_end(*a) if x == len(pairs) - 1 else self.mm(*a)
                pT_free[n] = end
            pcT_free = end
            t = self.copy(self.dve, mix[:, 0:4, tq], self.bank[o_bank][:, :].rearrange("p (j t) -> p j t", j=4), end)
            self.read_by(o_bank, t)
        st.close()

    def ssd(self, mix, small, xbc, silu_z):
        st = ExitStack()
        sb = lambda n, s: st.enter_context(self.nc.sbuf_tensor(f"{n}_{self.stage_no}", s, F32))
        H, N4 = 16, 4
        dt, dA, acs, tmp = small[:, :, 24:40], sb("dA", [P, TT, H]), sb("a_cumsum", [P, TT, H]), sb("dt_tmp", [P, TT, H])
        t = self.softplus(dt, tmp[:, :, :], None)
        tmp2 = sb("a_rate", [P, H])
        ta = self.func(tmp2[:, :], self.par("a_log"), ACT.Exp, self.inputs)
        for q in range(TT):
            t = self.stt(dA[:, q, :], tmp2[:, :], -1.0, small[:, q, 24:40], ALU.mult, ALU.mult, t, ta)
        ps, b, fr = self.half()
        self.pe.wait(fr, t)
        for q in range(TT):
            self.mm(ps[:, q * H:(q + 1) * H], self.par("upto"), dA[:, q, :], True, True)
        end = self.mm_end(ps[:, 32:32 + H], self.par("ones"), dA[:, 0, :], True, True)
        t = self.copy(self.dve, acs[:, :, :], ps[:, 0:32].rearrange("p (q h) -> p q h", q=TT), end)
        dec = sb("decay_to_end", [P, H])
        t = self.tt(self.dve, dec[:, :], ps[:, 32:32 + H], acs[:, 0, :], ALU.subtract, t)
        self.read_by(b, t)
        acs_tok = t
        t_dec = self.func(dec[:, :], dec[:, :], ACT.Exp, t)
        xd, xdd, b_tok = sb("x_dt", [P, TT, D]), sb("x_dt_decayed", [P, D]), sb("B_tokens", [P, 2, P])
        xd_tok = []
        for q in range(TT):
            for n in range(2):
                ps, b, fr = self.full()
                self.pe.wait(fr)
                for m in range(4):
                    end = self.transposed(ps[:, m * P:(m + 1) * P], xbc[:, 4 * n + m, q * P:(q + 1) * P], last=m == 3)
                t = self.tt(self.dve, xd[:, q, 512 * n:512 * n + 512].rearrange("p (h d) -> p h d", h=8), ps[:, :].rearrange("p (h d) -> p h d", h=8),
                            small[:, q, 24 + 8 * n:32 + 8 * n].unsqueeze(2).to_broadcast([P, 8, 64]), ALU.mult, end, acs_tok)
                self.read_by(b, t)
                xd_tok.append(t)
        t_xdd = self.tt(self.dve, xdd[:, :].rearrange("p (h d) -> p h d", h=H), xd[:, 0, :].rearrange("p (h d) -> p h d", h=H),
                        dec[:, :].unsqueeze(2).to_broadcast([P, H, 64]), ALU.mult, xd_tok, t_dec)
        ps, b, fr = self.half()
        self.pe.wait(fr)
        for g in range(2):
            end = self.transposed(ps[:, g * P:(g + 1) * P], xbc[:, 8 + g, 0:P], last=True)
        t_b = self.copy(self.act, b_tok[:, :, :], ps.rearrange("p (g n) -> p g n", g=2), end)
        self.read_by(b, t_b)
        state = sb("state_T", [P, 2, 512])
        for g in range(2):
            ps, b, fr = self.full()
            self.pe.wait(fr, t_b, t_xdd)
            end = self.mm_end(ps[:, :], b_tok[:, g, :], xdd[:, g * 512:(g + 1) * 512], True, True)
            t_state = self.copy(self.act, state[:, g, :], ps[:, :], end)
            self.read_by(b, t_state)
        cb, seg, grow = sb("CB_T", [P, P]), sb("seg_T", [P, 2, N4, P]), sb("C_grown", [P, 2, N4, P])
        cb_free, seg_free, grow_free, n_seg = None, [None] * 2, [None] * 2, 0
        y_tok = []
        for q in range(TT):
            tq = slice(q * P, (q + 1) * P)
            for g in range(2):
                ps, b, fr = self.half()
                self.pe.wait(fr)
                end = self.mm_end(ps[:, 0:P], xbc[:, 8 + g, tq], xbc[:, 10 + g, tq], True, True)
                t_cb = self.tt(self.dve, cb[:, :], ps[:, 0:P], self.par("upto"), ALU.mult, end, cb_free)
                self.read_by(b, t_cb)
                for r4 in range(2):
                    h0, s = 8 * g + 4 * r4, n_seg % 2
                    n_seg += 1
                    ps, b, fr = self.full()
                    self.pe.wait(fr, acs_tok)
                    for m in range(N4):
                        end = self.mm_end(ps[:, m * P:(m + 1) * P], dA[:, q, h0 + m:h0 + m + 1].to_broadcast([P, P]), self.par("upto"), True, True)
                    v = ps[:, :].rearrange("p (m t) -> p m t", m=N4)
                    t = self.tt(self.dve, seg[:, s, :, :], v, acs[:, q, h0:h0 + N4].unsqueeze(2).to_broadcast([P, N4, P]), ALU.subtract, end, seg_free[s], acs_tok)
                    if q > 0:
                        t_g = self.func(grow[:, s, :, :], v, ACT.Exp, end, t, grow_free[s])
                        self.read_by(b, t_g)
                        t_g = self.tt(self.dve, grow[:, s, :, :], grow[:, s, :, :], xbc[:, 10 + g, tq].unsqueeze(1).to_broadcast([P, N4, P]), ALU.mult, t_g)
                    else:
                        t_g = None
                        self.read_by(b, t)
                    t = self.ts(self.pool, seg[:, s, :, :], seg[:, s, :, :], 0.0, None, ALU.min, None, t)
                    t = self.func(seg[:, s, :, :], seg[:, s, :, :], ACT.Exp, t)
                    t = self.tt(self.dve, seg[:, s, :, :], seg[:, s, :, :], cb[:, :].unsqueeze(1).to_broadcast([P, N4, P]), ALU.mult, t, t_cb)
                    cb_free = t
                    yb, b, fr = self.half()
                    self.pe.wait(fr, t, t_g, t_state if q else None, xd_tok)
                    for m in range(N4):
                        h = h0 + m
                        o = yb[(h % 2) * 64:(h % 2) * 64 + 64, (m // 2) * P:(m // 2 + 1) * P]
                        if q:
                            self.mm(o, xd[:, q, h * 64:(h + 1) * 64], seg[:, s, m, :], True, False)
                            end = self.mm_end(o, state[:, g, (h % 8) * 64:(h % 8 + 1) * 64], grow[:, s, m, :], False, True)
                        else:
                            end = self.mm_end(o, xd[:, q, h * 64:(h + 1) * 64], seg[:, s, m, :], True, True)
                    seg_free[s] = grow_free[s] = end
                    for k in range(2):
                        c = h0 // 2 + k
                        t = self.stt(mix[:, 4 + c, tq], xbc[:, c, tq], self.par("d_skip")[:, c:c + 1], yb[:, k * P:(k + 1) * P], ALU.mult, ALU.add, end)
                    self.read_by(b, t)
        sq = self.y
        sq_tok = []
        for c in range(C):
            t1 = self.tt(self.dve, mix[:, 4 + c, :], mix[:, 4 + c, :], silu_z[:, c, :], ALU.mult, t)
            sq_tok.append(self.func(sq[:, c, :], mix[:, 4 + c, :], ACT.Square, t1, self.y_free))
        for g in range(2):
            r = self.inv_rms([sq[:, 4 * g + c, :] for c in range(4)], 512, 1e-5, sq_tok[4 * g:4 * g + 4], out=self.rms[:, g, :])
            for c in range(4 * g, 4 * g + 4):
                t = self.stt(mix[:, 4 + c, :], mix[:, 4 + c, :], self.par("ssd_norm")[:, c:c + 1], self.rms[:, g, :], ALU.mult, ALU.mult, r)
        self.y_free = (self.pe.sem, self.pe.count)
        self.rms_free = t
        self.barrier()
        st.close()

    def invert(self, buf, nt, tok, levels):
        t_, tt, x, nl = buf["t"], buf["tt"], buf["x"], buf["nl"]
        four = lambda a: a.unsqueeze(1).to_broadcast([P, 4, P])
        as4 = lambda ps: ps[:, :].rearrange("p (m t) -> p m t", m=4)
        k = self.tt(self.dve, nl[:, :, :], nt, four(self.par("level1")), ALU.mult, tok, buf["nl_free"])
        t_tt = self.tt(self.dve, tt[:, :, :], four(self.par("ident")), nl[:, :, :], ALU.subtract, k, buf["tt_free"])
        ps, b, fr = self.full()
        self.pe.wait(fr, t_tt)
        for m in range(4):
            end = self.transposed(ps[:, m * P:(m + 1) * P], tt[:, m, :], last=m == 3)
        t_t = self.copy(self.act, t_[:, :, :], as4(ps), end, buf["x_free"])
        self.read_by(b, t_t)
        x_free, nl_free = buf["x_free"], t_tt
        for l in levels[1:]:
            t_nl = self.tt(self.pool, nl[:, :, :], nt, four(self.par(f"level{l}")), ALU.mult, nl_free, tok)
            yield
            ps, b, fr = self.full()
            self.pe.wait(fr, t_nl, t_t)
            for m in range(4):
                a = (ps[:, m * P:(m + 1) * P], nl[:, m, :], t_[:, m, :], True, True)
                end = self.mm_end(*a) if m == 3 else self.mm(*a)
            nl_free = end
            t_x = self.copy(self.act, x[:, :, :], as4(ps), end, x_free)
            self.read_by(b, t_x)
            yield
            last = l == levels[-1]
            ps, b, fr = self.full()
            self.pe.wait(fr, t_x, t_tt)
            for m in range(4):
                a = (ps[:, m * P:(m + 1) * P], x[:, m, :], tt[:, m, :], True, True)
                end = self.mm_end(*a) if m == 3 else self.mm(*a)
            if not last:
                ps2, b2, fr = self.full()
                self.pe.wait(fr)
                for m in range(4):
                    a = (ps2[:, m * P:(m + 1) * P], tt[:, m, :], x[:, m, :], True, True)
                    end2 = self.mm_end(*a) if m == 3 else self.mm(*a)
                t_t = self.tt(self.dve, t_[:, :, :], t_[:, :, :], as4(ps2), ALU.subtract, end2, t_t)
                self.read_by(b2, t_t)
                end = end2
            t_tt = self.tt(self.dve, tt[:, :, :], tt[:, :, :], as4(ps), ALU.subtract, end)
            self.read_by(b, t_tt)
            x_free = end
        buf["x_free"] = buf["nl_free"] = (self.pe.sem, self.pe.count)
        buf["done"] = t_tt

    @staticmethod
    def interleave(*generators):
        left = list(generators)
        while left:
            for g in list(left):
                try:
                    next(g)
                except StopIteration:
                    left.remove(g)

    def rwkv_mixer(self):
        st, sb = self.stage()
        h_toks = self.norm_x(self.par("a1_gain2"))
        r, k, v, sg, a, g = (sb(n, [P, C, T]) for n in ("r", "k", "v", "decay", "a", "g"))
        pend = sb("chunk_decay", [P, C, 4])
        inner = ExitStack()
        isb = lambda n, s: inner.enter_context(self.nc.sbuf_tensor(f"{n}_{self.stage_no}", s, F32))
        xx, m0, m1 = isb("x_shifted", [P, C, T]), isb("mixed0", [P, C, T]), isb("mixed1", [P, C, T])
        hw = isb("lora_hidden", [P, 4, T])
        h, y = self.h, self.y
        t = self.tt(self.dve, xx[:, :, 1:], h[:, :, 0:T - 1], h[:, :, 1:], ALU.subtract, h_toks)
        t = self.ts(self.dve, xx[:, :, 0:1], h[:, :, 0:1], -1.0, None, ALU.mult, None, t)
        mixed, m_free = [m0, m1], [None, None]
        turn = [0]

        def mix(n):
            i = turn[0] % 2
            turn[0] += 1
            toks = [self.stt(mixed[i][:, c, :], xx[:, c, :], self.par(f"mu{n}")[:, c:c + 1], h[:, c, :], ALU.mult, ALU.add, t, m_free[i])
                    for c in range(C)]
            return i, mixed[i], toks

        s1, w1, tok1 = self.slot()
        s2, g1, tok2 = self.slot()
        hid_tok = []
        for n, (mu, w, tok, lo, m, fn) in enumerate(((1, w1, tok1, 0, 64, ACT.Tanh), (4, w1, tok1, 64, 64, ACT.Copy),
                                                     (5, g1, tok2, 0, 128, ACT.Sigmoid), (5, g1, tok2, 128, 32, ACT.Sigmoid))):
            if n < 3:
                i, src, toks = mix(mu)
            ps, b, fr = self.half()
            self.pe.wait(fr, tok, toks)
            for c in range(C):
                args = (ps[0:m, :], w[:, c * FB + lo:c * FB + lo + m], src[:, c, :], c == 0, c == C - 1)
                end = self.mm_end(*args) if c == C - 1 else self.mm(*args)
            m_free[i] = end
            hid_tok.append(self.func(hw[0:m, n, :], ps[0:m, :], fn, end))
            self.read_by(b, hid_tok[-1])
            if n in (1, 3):
                self.slot_read(s1 if n == 1 else s2, end)
        for n, (dst, bias) in enumerate(((sg, "w0"), (a, "a0"))):
            if n == 0:
                s1, w, tok = self.slot()
            for c in range(C):
                ps, b, fr = self.half()
                self.pe.wait(fr, tok, hid_tok[n])
                end = self.mm_end(ps, w[0:64, n * D + c * P:n * D + (c + 1) * P], hw[0:64, n, :], True, True)
                t2 = self.func(dst[:, c, :], ps, ACT.Sigmoid, end, bias=self.par(bias)[:, c:c + 1])
                self.read_by(b, t2)
        self.slot_read(s1, end)
        s1, w, tok = self.slot()
        for c in range(C):
            ps, b, fr = self.half()
            self.pe.wait(fr, tok, hid_tok[2], hid_tok[3])
            self.mm(ps, w[:, c * P:(c + 1) * P], hw[:, 2, :], True, False)
            end = self.mm_end(ps, w[0:32, D + c * P:D + (c + 1) * P], hw[0:32, 3, :], False, True)
            t2 = self.copy(self.act, g[:, c, :], ps, end)
            self.read_by(b, t2)
        self.slot_read(s1, end)
        for mu, dst in ((0, r), (2, k), (3, v)):
            i, src, toks = mix(mu)

            def consume(c, ps, end, dst=dst):
                return self.copy(self.act, dst[:, c, :], ps, end)
            self.columns(src, toks, 4, consume)
            m_free[i] = (self.pe.sem, self.pe.count)
        self.barrier()
        kappa = float(np.exp(-0.5))
        gs, kk, t3, t4 = m0, m1, xx, y
        for c in range(C):
            t_gs = self.dve.do(lambda e, c=c: e.tensor_tensor_scan(gs[:, c, :], self.par("not_first64"), sg[:, c, :], 0.0, ALU.mult, ALU.add))
            t_kk = self.ts(self.dve, kk[:, c, :], k[:, c, :], self.par("k_k")[:, c:c + 1], None, ALU.mult, None)
        al = lambda x: x[:, :, :]
        t = self.tt(self.pool, al(t4), al(gs), al(sg), ALU.subtract, t_gs)
        t_pprev = self.func(al(t4), al(t4), ACT.Exp, t, scale=-kappa)
        t = self.func(al(t3), al(kk), ACT.Square, t_kk)

        def head_sums(src, tok, use):
            out = []
            for n in range(4):
                ps, b, fr = self.full()
                self.pe.wait(fr, tok)
                end = self.mm_end(ps[:, :], self.par("half_ones"), src[:, 2 * n:2 * n + 2, :], True, True)
                t = use(n, ps[:, :].rearrange("p (c t) -> p c t", c=2), end)
                self.read_by(b, t)
                out.append(t)
            return out
        t = head_sums(t3, t, lambda n, ps, end: self.ts(self.dve, t3[:, 2 * n:2 * n + 2, :], ps, 1e-24, None, ALU.max, None, end))
        t = self.func(al(t3), al(t3), ACT.Ln, t, scale=65536.0)
        t = self.func(al(t3), al(t3), ACT.Exp, t, scale=-0.5)
        t_kk = self.stt(al(kk), al(kk), 256.0, al(t3), ALU.mult, ALU.mult, t, t_kk)
        t_A = self.stt(al(sg), al(kk), -1.0, al(t4), ALU.mult, ALU.mult, t_kk, t_pprev)
        one_less = isb("one_less_ka", [P, C])
        t = self.ts(self.dve, one_less[:, :], self.par("k_a"), -1.0, 1.0, ALU.mult, ALU.add)
        for c in range(C):
            t1 = self.ts(self.dve, t3[:, c, :], a[:, c, :], self.par("k_a")[:, c:c + 1], one_less[:, c:c + 1], ALU.mult, ALU.add, t, t_kk)
        t_k = self.tt(self.dve, al(k), al(k), al(t3), ALU.mult, t1)
        t_b = self.tt(self.pool, al(a), al(kk), al(a), ALU.mult, t1, t_kk)
        t = self.tt(self.dve, al(t3), al(r), al(k), ALU.mult, t_k)
        for c in range(C):
            t1 = self.ts(self.dve, t3[:, c, :], t3[:, c, :], self.par("r_k")[:, c:c + 1], None, ALU.mult, None, t)
        t_bonus = head_sums(t3, t1, lambda n, ps, end: self.tt(self.dve, h[:, 2 * n:2 * n + 2, :], v[:, 2 * n:2 * n + 2, :], ps, ALU.mult, end))
        t = self.func(al(t4), al(gs), ACT.Exp, t_A, scale=kappa)
        t_B = self.tt(self.pool, al(a), al(a), al(t4), ALU.mult, t, t_b)
        t_K = self.tt(self.dve, al(k), al(k), al(t4), ALU.mult, t, t_bonus)
        t = self.func(al(t3), al(gs), ACT.Exp, t_bonus, t_K, scale=-kappa)
        t_R = self.tt(self.dve, al(r), al(r), al(t3), ALU.mult, t)
        self.copy(self.dve, pend[:, :, :], t3[:, :, 63:T:64], t)
        self.barrier()
        inner.close()
        A, B, K, R = sg, a, k, r
        inner = ExitStack()
        isb = lambda n, s: inner.enter_context(self.nc.sbuf_tensor(f"{n}_{self.stage_no}", s, F32))
        tokT = {n: isb(f"{n}_tokens", [P, 4, P]) for n in "BKV"}
        bufs = []
        for par in range(2):
            bufs.append({n: isb(f"{n}{par}", [P, 4, P]) for n in ("nt", "rb", "rk", "t", "tt", "x", "nl")})
            bufs[par].update(x_free=None, nl_free=None, tt_free=None)
        lv, S = isb("LakV", [P, 4, P]), [isb(f"state{i}", [P, 4, P]) for i in range(2)]
        U = isb("U", [P, 4, P])
        W, Stmp = bufs[0]["x"], bufs[1]["x"]
        as4 = lambda ps: ps[:, :].rearrange("p (m t) -> p m t", m=4)
        four = lambda m: m.unsqueeze(1).to_broadcast([P, 4, P])
        for sg_ in range(2):
            ch = lambda m: 4 * sg_ + m
            for q in range(TT):
                tq = slice(q * P, (q + 1) * P)
                self.barrier()
                for n, src in (("B", B), ("K", K), ("V", v)):
                    ps, b, fr = self.full()
                    self.pe.wait(fr)
                    for m in range(4):
                        end = self.transposed(ps[:, m * P:(m + 1) * P], src[:, ch(m), tq], last=m == 3)
                    t_tok = self.copy(self.act, tokT[n][:, :, :], as4(ps), end)
                    self.read_by(b, t_tok)
                lak_tok = []
                for par in range(2):
                    bf, base = bufs[par], slice(par * 64, par * 64 + 64)
                    for dst, L, Rh, mask, sign in (("nt", B, A, "before64", -1.0), ("nl", K, A, "before64", 1.0),
                                                   ("rb", B, R, "upto64", 1.0), ("rk", K, R, "upto64", 1.0)):
                        ps, b, fr = self.full()
                        self.pe.wait(fr)
                        for m in range(4):
                            end = self.mm_end(ps[:, m * P:(m + 1) * P], L[base, ch(m), tq], Rh[base, ch(m), tq], True, True)
                        t = self.stt(bf[dst][:, :, :], as4(ps), sign, four(self.par(mask)), ALU.mult, ALU.mult, end)
                        self.read_by(b, t)
                        if dst == "nt":
                            bf["nt_tok"] = t
                        if dst == "nl":
                            lak_tok.append(t)
                ps, b, fr = self.full()
                self.pe.wait(fr, lak_tok, t_tok)
                for m in range(4):
                    for par in range(2):
                        o = slice(m * P + par * 64, m * P + par * 64 + 64)
                        end = self.mm_end(ps[:, o], bufs[par]["nl"][:, m, :], tokT["V"][:, m, par * 64:par * 64 + 64], True, True)
                t_lv = self.copy(self.act, lv[:, :, :], as4(ps), end)
                self.read_by(b, t_lv)
                for bf in bufs:
                    bf["nl_free"] = end
                    bf["x_free"] = bf["tt_free"] = None
                self.interleave(*(self.invert(bf, bf["nt"][:, :, :], bf["nt_tok"], (1, 2, 4, 8, 16, 32)) for bf in bufs))
                inv = [bf["done"] for bf in bufs] + [bufs[0]["x_free"], bufs[1]["x_free"]]
                for j in (2 * q, 2 * q + 1):
                    rows = slice((j % 2) * 64, (j % 2) * 64 + 64)
                    s_now, s_next = S[j % 2], S[(j + 1) % 2]
                    if j == 0:
                        w_src, t_w = lv, t_lv
                    else:
                        ps, b, fr = self.full()
                        self.pe.wait(fr, t_s, inv)
                        for m in range(4):
                            end = self.mm_end(ps[:, m * P:(m + 1) * P], A[:, ch(m), tq], s_now[:, m, :], True, True)
                        w_src = W
                        t_w = self.tt(self.dve, W[:, :, :], lv[:, :, :], as4(ps), ALU.add, end, inv, t_lv)
                        self.read_by(b, t_w)
                    ps, b, fr = self.full()
                    self.pe.wait(fr, t_w, inv)
                    for m in range(4):
                        for par in range(2):
                            o = slice(par * 64, par * 64 + 64)
                            end = self.mm_end(ps[:, m * P + par * 64:m * P + par * 64 + 64], bufs[par]["tt"][:, m, :], w_src[:, m, o], True, True)
                    t_u = self.copy(self.act, U[rows, :, :], as4(ps)[rows], end)
                    self.read_by(b, t_u)
                    if j < 3:
                        ps, b, fr = self.full()
                        self.pe.wait(fr, t_u)
                        for m in range(4):
                            o = ps[:, m * P:(m + 1) * P]
                            self.mm(o, tokT["B"][rows, m, :], U[rows, m, :], True, False)
                            end = self.mm_end(o, tokT["K"][rows, m, :], tokT["V"][rows, m, :], False, True)
                        t = self.tt(self.dve, Stmp[:, :, :], as4(ps), four(self.par("half_ones")), ALU.mult, end, inv)
                        self.read_by(b, t)
                        if j > 0:
                            t = self.tt(self.dve, Stmp[:, :, :], Stmp[:, :, :], s_now[:, :, :], ALU.add, t, t_s)
                        t_new = (t, j)
                    if j % 2:
                        ps, b, fr = self.full()
                        self.pe.wait(fr, t_u)
                        for m in range(4):
                            o = ps[:, m * P:(m + 1) * P]
                            first = True
                            for i in (2 * q, j):
                                if i:
                                    cols = slice((i % 2) * 64, (i % 2) * 64 + 64)
                                    self.mm(o[:, cols], S[i % 2][:, m, :], R[:, ch(m), q * P + cols.start:q * P + cols.stop], first, False, True)
                                    first = False
                            for par in range(2):
                                f = slice(par * 64, par * 64 + 64)
                                self.mm(o[f], U[:, m, f], bufs[par]["rb"][:, m, :], False, False, True)
                                end = self.mm_end(o[f], tokT["V"][:, m, f], bufs[par]["rk"][:, m, :], False, par == 1, True)
                        t_y = self.copy(self.act, y[:, 4 * sg_:4 * sg_ + 4, tq], as4(ps), end)
                        self.read_by(b, t_y)
                    if j < 3:
                        t_s = self.tt(self.dve, s_next[:, :, :], Stmp[:, :, :],
                                      pend[:, 4 * sg_:4 * sg_ + 4, j:j + 1].to_broadcast([P, 4, P]), ALU.mult, t_new[0],
                                      (self.pe.sem, self.pe.count))
        self.barrier()
        inner.close()
        d, sq = A, B
        head_sums_w = lambda src, tok, use: head_sums(src, tok, use)
        t = head_sums_w(y, None, lambda n, ps, end: self.stt(d[:, 2 * n:2 * n + 2, :], ps, -1.0 / 64, y[:, 2 * n:2 * n + 2, :], ALU.mult, ALU.add, end))
        t2 = self.func(al(sq), al(d), ACT.Square, t)
        t2 = head_sums_w(sq, t2, lambda n, ps, end: self.ts(self.dve, sq[:, 2 * n:2 * n + 2, :], ps, 1.0 / 64, 64e-5, ALU.mult, ALU.add, end))
        t2 = self.func(al(sq), al(sq), ACT.Ln, t2)
        t2 = self.func(al(sq), al(sq), ACT.Exp, t2, scale=-0.5)
        t = self.tt(self.dve, al(d), al(d), al(sq), ALU.mult, t2)
        toks = []
        for c in range(C):
            t1 = self.ts(self.dve, d[:, c, :], d[:, c, :], self.par("ln_g")[:, c:c + 1], self.par("ln_b")[:, c:c + 1], ALU.mult, ALU.add, t)
            t1 = self.tt(self.pool, d[:, c, :], d[:, c, :], h[:, c, :], ALU.add, t1)
            toks.append(self.tt(self.dve, d[:, c, :], d[:, c, :], g[:, c, :], ALU.mult, t1))
        self.h_free = self.y_free = toks[-1]
        self.add_back(self.project_columns_out(d, toks), self.par("a1_gain3"), 1.0)
        st.close()

    def delta_mixer(self):
        i, H, K = 1, 8, 4
        st, sb = self.stage()
        part = lambda n: self.mod[i][:, n * C:(n + 1) * C]
        h_toks = self.norm_x(self.gain[:, i, 0, :], part(0), self.mod_tok)
        q_T, k_T, v_T, z = (sb(n, [P, C, T]) for n in ("q", "k", "v", "silu_z"))
        ba = sb("beta_g", [P, TT, 16])
        inner = ExitStack()
        isb = lambda n, s: inner.enter_context(self.nc.sbuf_tensor(f"{n}_{self.stage_no}", s, F32))
        raw, taps = isb("qkv_raw", [P, 2, K - 1 + T]), isb("qkv_taps", [P, 2, T])
        z0 = self.pool.do(lambda e: e.memset(raw[:, :, 0:K - 1], 0.0))
        raw_free, taps_free = [None] * 2, [None] * 2

        def conv_in(c, ps, end):
            n = c % 2
            dst = (q_T, k_T, v_T)[c // C][:, c % C, :]
            t = self.copy(self.act, raw[:, n, K - 1:], ps, end, raw_free[n])
            v = self.conv_chunk(taps[:, n, :], raw[:, n, :], "gdn_conv", None, c, K, [t, z0], taps_free[n])
            raw_free[n] = v
            taps_free[n] = self.func(dst, taps[:, n, :], ACT.Silu, v)
            return t
        self.columns(self.h, h_toks, 12, conv_in)
        self.columns(self.h, h_toks, 4, lambda c, ps, end: self.func(z[:, c, :], ps, ACT.Silu, end))
        for q in range(TT):
            ps, b, fr = self.half()
            self.pe.wait(fr, self.inputs)
            for c in range(C):
                a = (ps[:, 0:16], self.h[:, c, q * P:(q + 1) * P], self.par("w_ba", c * 16, 16), c == 0, c == C - 1)
                end = self.mm_end(*a) if c == C - 1 else self.mm(*a)
            t = self.func(ba[:, q, 0:8], ps[:, 0:8], ACT.Sigmoid, end)
            t = self.tt(self.dve, ba[:, q, 8:16], ps[:, 8:16], self.par("gdn_dt_bias"), ALU.add, end, t)
            self.read_by(b, t)
        self.barrier()
        inner.close()
        tmp = sb("g_tmp", [P, TT, H])
        rate = sb("g_rate", [P, H])
        t = self.softplus(ba[:, :, 8:16], tmp[:, :, :], None)
        ta = self.func(rate[:, :], self.par("gdn_a_log"), ACT.Exp, t)
        for q in range(TT):
            t = self.stt(ba[:, q, 8:16], rate[:, :], -1.0, ba[:, q, 8:16], ALU.mult, ALU.mult, t, ta)
        gc, kdec = sb("g_cumsum", [P, TT, H]), sb("decay_to_end", [P, H])
        ps, b, fr = self.half()
        self.pe.wait(fr, t)
        for q in range(TT):
            self.mm(ps[:, q * H:(q + 1) * H], self.par("upto"), ba[:, q, 8:16], True, True)
        end = self.mm_end(ps[:, 16:24], self.par("ones"), ba[:, 0, 8:16], True, True)
        t = self.copy(self.dve, gc[:, :, :], ps[:, 0:16].rearrange("p (q h) -> p q h", q=TT), end)
        t = self.tt(self.dve, kdec[:, :], ps[:, 16:24], gc[:, 0, :], ALU.subtract, t)
        self.read_by(b, t)
        t_kd = self.func(kdec[:, :], kdec[:, :], ACT.Exp, t)
        sq = self.y
        for dst, s2 in ((q_T, float(P)), (k_T, 1.0)):
            t = self.func(sq[:, :, :], dst[:, :, :], ACT.Square, self.y_free)
            for n in range(4):
                ps, b, fr = self.full()
                self.pe.wait(fr, t)
                end = self.mm_end(ps[:, :], self.par("ones"), sq[:, 2 * n:2 * n + 2, :], True, True)
                t1 = self.ts(self.dve, sq[:, 2 * n:2 * n + 2, :], ps[:, :].rearrange("p (c t) -> p c t", c=2), s2, s2 * NORM_EPS, ALU.mult, ALU.add, end)
                self.read_by(b, t1)
            t1 = self.func(sq[:, :, :], sq[:, :, :], ACT.Ln, t1)
            t1 = self.func(sq[:, :, :], sq[:, :, :], ACT.Exp, t1, scale=-0.5)
            self.y_free = self.tt(self.dve, dst[:, :, :], dst[:, :, :], sq[:, :, :], ALU.mult, t1)
        self.barrier()
        o_T = self.h
        names = ("nt", "attn", "t", "tt", "x", "nl", "dec", "k_tok", "vb", "kg", "qd")
        bufs = [{n: sb(f"{n}{x}", [P, 4, P]) for n in (names[:5] + names[6:10] if x < 0 else names)} for x in range(1)]
        S = sb("state", [P, 4, P])
        bf = bufs[0]
        as4 = lambda ps: ps[:, :].rearrange("p (m t) -> p m t", m=4)
        four = lambda m: m.unsqueeze(1).to_broadcast([P, 4, P])
        col = lambda x: x.unsqueeze(2).to_broadcast([P, 4, P])
        for hg in range(2):
            h0 = 4 * hg
            for q in range(TT):
                tq = slice(q * P, (q + 1) * P)
                self.barrier()
                pg, b, fr = self.full()
                self.pe.wait(fr)
                for m in range(4):
                    end = self.mm_end(pg[:, m * P:(m + 1) * P], ba[:, q, 8 + h0 + m:9 + h0 + m].to_broadcast([P, P]), self.par("upto"), True, True)
                dec = bf["dec"][:, :, :]
                t = self.tt(self.dve, dec, as4(pg), col(gc[:, q, h0:h0 + 4]), ALU.subtract, end)
                t = self.ts(self.dve, dec, dec, 0.0, None, ALU.min, None, t)
                t_dec = self.func(dec, dec, ACT.Exp, t)
                t_kg = self.func(bf["kg"][:, :, :], as4(pg), ACT.Exp, end, t)
                self.read_by(b, t_kg)
                t_qd = self.tt(self.pool, bf["qd"][:, :, :], q_T[:, h0:h0 + 4, tq], bf["kg"][:, :, :], ALU.mult, t_kg)
                t_kg = self.tt(self.pool, bf["kg"][:, :, :], k_T[:, h0:h0 + 4, tq], bf["kg"][:, :, :], ALU.mult, t_qd)
                ps, b, fr = self.full()
                self.pe.wait(fr)
                for m in range(4):
                    end = self.mm_end(ps[:, m * P:(m + 1) * P], k_T[:, h0 + m, tq], k_T[:, h0 + m, tq], True, True)
                t_nt = self.tt(self.dve, bf["nt"][:, :, :], as4(ps), dec, ALU.mult, end, t_dec)
                self.read_by(b, t_nt)
                ps, b, fr = self.full()
                self.pe.wait(fr)
                for m in range(4):
                    end = self.mm_end(ps[:, m * P:(m + 1) * P], ba[:, q, h0 + m:h0 + m + 1].to_broadcast([P, P]), self.par("ident"), True, True)
                t_nt = self.tt(self.dve, bf["nt"][:, :, :], bf["nt"][:, :, :], as4(ps), ALU.mult, end, t_nt)
                self.read_by(b, t_nt)
                t_nt = self.tt(self.pool, bf["nt"][:, :, :], bf["nt"][:, :, :], four(self.par("before")), ALU.mult, t_nt)
                ps, b, fr = self.full()
                self.pe.wait(fr)
                for m in range(4):
                    end = self.mm_end(ps[:, m * P:(m + 1) * P], k_T[:, h0 + m, tq], q_T[:, h0 + m, tq], True, True)
                t_at = self.tt(self.dve, bf["attn"][:, :, :], as4(ps), dec, ALU.mult, end, t_dec)
                self.read_by(b, t_at)
                t_at = self.tt(self.pool, bf["attn"][:, :, :], bf["attn"][:, :, :], four(self.par("upto")), ALU.mult, t_at)
                ps, b, fr = self.full()
                self.pe.wait(fr)
                for m in range(4):
                    end = self.transposed(ps[:, m * P:(m + 1) * P], v_T[:, h0 + m, tq], last=m == 3)
                t_vb = self.tt(self.dve, bf["vb"][:, :, :], as4(ps), col(ba[:, q, h0:h0 + 4]), ALU.mult, end)
                self.read_by(b, t_vb)
                t_kt = None
                if q == 0:
                    ps, b, fr = self.full()
                    self.pe.wait(fr)
                    for m in range(4):
                        end = self.transposed(ps[:, m * P:(m + 1) * P], k_T[:, h0 + m, tq], last=m == 3)
                    t_kt = self.tt(self.dve, bf["k_tok"][:, :, :], as4(ps), col(kdec[:, h0:h0 + 4]), ALU.mult, end, t_kd)
                    self.read_by(b, t_kt)
                bf.update(x_free=None, nl_free=None, tt_free=None)
                self.interleave(self.invert(bf, bf["nt"][:, :, :], t_nt, (1, 2, 4, 8, 16, 32, 64)))
                inv = [bf["done"], bf["x_free"]]
                w = bf["vb"]
                if q:
                    ps, b, fr = self.full()
                    self.pe.wait(fr, t_s, t_kg)
                    for m in range(4):
                        end = self.mm_end(ps[:, m * P:(m + 1) * P], bf["kg"][:, m, :], S[:, m, :], True, True)
                    w = bf["x"]
                    t = self.tt(self.dve, w[:, :, :], as4(ps), col(ba[:, q, h0:h0 + 4]), ALU.mult, end, inv)
                    self.read_by(b, t)
                    t_vb = self.tt(self.dve, w[:, :, :], bf["vb"][:, :, :], w[:, :, :], ALU.subtract, t, t_vb)
                ps, b, fr = self.full()
                self.pe.wait(fr, t_vb, inv)
                for m in range(4):
                    end = self.mm_end(ps[:, m * P:(m + 1) * P], bf["tt"][:, m, :], w[:, m, :], True, True)
                U = bf["nl"]
                t_u = self.copy(self.act, U[:, :, :], as4(ps), end, inv)
                self.read_by(b, t_u)
                ps, b, fr = self.full()
                self.pe.wait(fr, t_u, t_at, t_qd)
                for m in range(4):
                    o = ps[:, m * P:(m + 1) * P]
                    if q:
                        self.mm(o, S[:, m, :], bf["qd"][:, m, :], True, False)
                    end = self.mm_end(o, U[:, m, :], bf["attn"][:, m, :], not q, True)
                t = self.copy(self.dve, o_T[:, h0:h0 + 4, tq], as4(ps), end, self.h_free)
                self.read_by(b, t)
                if q == 0:
                    ps, b, fr = self.full()
                    self.pe.wait(fr, t_u, t_kt)
                    for m in range(4):
                        end = self.mm_end(ps[:, m * P:(m + 1) * P], bf["k_tok"][:, m, :], U[:, m, :], True, True)
                    t_s = self.copy(self.act, S[:, :, :], as4(ps), end)
                    self.read_by(b, t_s)
        self.barrier()
        t = self.func(sq[:, :, :], o_T[:, :, :], ACT.Square)
        for n in range(4):
            ps, b, fr = self.full()
            self.pe.wait(fr, t)
            end = self.mm_end(ps[:, :], self.par("ones"), sq[:, 2 * n:2 * n + 2, :], True, True)
            t1 = self.ts(self.dve, sq[:, 2 * n:2 * n + 2, :], ps[:, :].rearrange("p (c t) -> p c t", c=2), 1.0 / P, NORM_EPS, ALU.mult, ALU.add, end)
            self.read_by(b, t1)
        t1 = self.func(sq[:, :, :], sq[:, :, :], ACT.Ln, t1)
        t1 = self.func(sq[:, :, :], sq[:, :, :], ACT.Exp, t1, scale=-0.5)
        t1 = self.stt(q_T[:, :, :], o_T[:, :, :], self.par("gdn_norm"), sq[:, :, :], ALU.mult, ALU.mult, t1)
        t1 = self.tt(self.dve, q_T[:, :, :], q_T[:, :, :], z[:, :, :], ALU.mult, t1)
        self.h_free = self.y_free = t1
        self.add_back(self.project_columns_out(q_T, [t1] * C), self.gain[:, i, 1, :], 1.0)
        st.close()


def program(nc, x_in, w_in, pack_in, out, n_slots, at, stages=None):
    k = Kernel(nc, x_in, w_in, pack_in, out, n_slots, at)
    for name, fn in STAGES:
        if stages is None or name in stages:
            fn(k)
    k.finish()


STAGES = [
    ("a0_ffn1", lambda k: k.ffn("a0_gain0", "a0_gain1")),
    ("a0_mix", lambda k: k.nsa_ssd_mixer()),
    ("a0_ffn2", lambda k: k.ffn("a0_gain4", "a0_gain5")),
    ("a1_ffn1", lambda k: k.ffn("a1_gain0", "a1_gain1")),
    ("a1_mix", lambda k: k.rwkv_mixer()),
    ("a1_ffn2", lambda k: k.ffn("a1_gain4", "a1_gain5")),
    ("b0_ada", lambda k: k.modulation(0)),
    ("b0_mix", lambda k: k.conv_mixer(0)),
    ("b0_moe", lambda k: k.moe(0)),
    ("b1_ada", lambda k: k.modulation(1)),
    ("b1_mix", lambda k: k.delta_mixer()),
    ("b1_moe", lambda k: k.moe(1)),
]


def kernel(**inputs):
    from concourse import bacc
    from concourse.bass_utils import run_bass_kernel_spmd

    xT, slots, pk = lay_out(inputs)
    weights = np.stack(slots)
    small = np.concatenate(pk.parts, axis=1)
    nc = bacc.Bacc("TRN2", target_bir_lowering=False, num_devices=1)
    args = []
    arrays = {"x_T": xT, "weight_slots": weights, "small_params": small}
    for name, arr in arrays.items():
        args.append(nc.dram_tensor(name, arr.shape, F32, kind="ExternalInput").ap())
    out = nc.dram_tensor("out_T", xT.shape, F32, kind="ExternalOutput").ap()
    program(nc, *args, out, len(slots), pk.at)
    got = run_bass_kernel_spmd(nc, [arrays], core_ids=[0]).results[0]["out_T"]
    return np.ascontiguousarray(got.transpose(2, 1, 0).reshape(1, T, D))
```

```python
from contextlib import ExitStack

import numpy as np
import concourse.bass as bass
import concourse.mybir as mybir
from concourse.alu_op_type import AluOpType as ALU

F32 = mybir.dt.float32
F32R = mybir.dt.float32r
ACT = mybir.ActivationFunctionType
AX = mybir.AxisListType.X

P = 128
D = 1024
T = 256
C = D // P
TT = T // P
SLOT = 2048
RING = 8
MOE_EXTRA = 5
CAP = 64
FB = 256
FFN_BLOCKS = 2816 // FB
N_EXP = 64
N_GRP = 8
SHARED_BLOCKS = 512 // FB
NORM_EPS = 1e-6
NEG = -1e30


class Pack:

    def __init__(self):
        self.at, self.parts, self.n = {}, [], 0

    def add(self, name, a):
        a = np.asarray(a)
        full = np.zeros((P, a.shape[1]), np.float32)
        full[:a.shape[0]] = a
        self.at[name] = (self.n, a.shape[1])
        self.parts.append(full)
        self.n += a.shape[1]

    def features(self, name, a):
        self.add(name, np.asarray(a).reshape(-1, P).T)

    def rows(self, name, a):
        a = np.asarray(a).reshape(1, -1)
        self.add(name, np.broadcast_to(a, (P, a.shape[1])))


def columns_slot(w):
    out = np.zeros((P, C, FB), np.float32)
    out[:, :, :w.shape[1]] = w.reshape(C, P, w.shape[1]).transpose(1, 0, 2)
    return out.reshape(P, SLOT)


def rows_slot(w):
    return w.reshape(2, P, D).transpose(1, 0, 2).reshape(P, SLOT)


def shape_constants(pk):
    i = np.arange(P)
    s, t = i[:, None], i[None, :]
    pk.add("ident", (s == t).astype(np.float32))
    pk.add("ones", np.ones((P, P), np.float32))
    pk.add("half_ones", (s // 64 == t // 64).astype(np.float32))
    pk.add("upto", (s <= t).astype(np.float32))
    pk.add("before", (s < t).astype(np.float32))
    same = s // 64 == t // 64
    pk.add("upto64", (same & (s <= t)).astype(np.float32))
    pk.add("before64", (same & (s < t)).astype(np.float32))
    for l in (1, 2, 4, 8, 16, 32, 64):
        pk.add(f"level{l}", ((s // (2 * l) == t // (2 * l)) & (s % (2 * l) < l) & (t % (2 * l) >= l)).astype(np.float32))
    inv = (10000.0 ** (-np.arange(0, 64, 2, dtype=np.float32) / np.float32(64))).astype(np.float32)
    ang = np.arange(T, dtype=np.float32)[:, None] * inv[None, :]
    pk.add("cos", np.cos(ang).astype(np.float32).T[np.arange(P) % 32])
    pk.add("sin", np.sin(ang).astype(np.float32).T[np.arange(P) % 32])
    turn = np.zeros((P, P), np.float32)
    for m in range(P):
        turn[m + 32 if m % 64 < 32 else m - 32, m] = -1.0 if m % 64 < 32 else 1.0
    pk.add("turn", turn)
    for q in range(TT):
        tok = q * P + i[:, None]
        pk.add(f"causal{q}", np.where(np.arange(T)[None, :] <= tok, 0.0, NEG).astype(np.float32))
        keep = (np.arange(15)[None, :] * 16 + 31 <= tok)
        pk.add(f"cmp_keep{q}", np.broadcast_to(keep[:, None, :], (P, 8, 15)).reshape(P, 120).astype(np.float32))
        pk.add(f"cmp_add{q}", np.broadcast_to(np.where(keep, 0.0, NEG)[:, None, :], (P, 8, 15)).reshape(P, 120).astype(np.float32))
    seg = np.ones(T, np.float32)
    seg[::64] = 0.0
    pk.rows("not_first64", seg)
    pk.add("one_32nd", np.full((P, 1), 1 / 32, np.float32))
    pk.rows("places", np.arange(1, CAP + 1).astype(np.float32))
    pk.rows("rank8", np.arange(8, 0, -1).astype(np.float32))


def lay_out(a):
    a = {k: np.asarray(v) for k, v in a.items()}
    pk, slots = Pack(), []
    shape_constants(pk)

    def by_columns(w):
        for n in range(0, w.shape[1], FB):
            slots.append(columns_slot(w[:, n:n + FB]))

    def by_rows(w):
        for n in range(0, w.shape[0], FB):
            slots.append(rows_slot(w[n:n + FB]))

    def gated(g, u, d):
        for n in range(0, g.shape[1], FB):
            slots.append(columns_slot(g[:, n:n + FB]))
            slots.append(columns_slot(u[:, n:n + FB]))
            slots.append(rows_slot(d[n:n + FB]))

    for layer in range(2):
        for n in range(6):
            pk.features(f"a{layer}_gain{n}", a["norm_gains"][layer, n])
        gated(a["ffn1_w_gate"][layer], a["ffn1_w_up"][layer], a["ffn1_w_down"][layer])
        if layer == 0:
            w = a["ab_w_in"][0]
            q, kc, vc, ks, vs, kw, vw, gl, z, xbc, dt = np.split(
                w, np.cumsum([512, 128, 128, 128, 128, 128, 128, 24, 1024, 1536])[:].tolist(), axis=1)
            by_columns(xbc)
            by_columns(z)
            pair = [h for j in range(4) for h in (j, j + 4)]
            by_columns(np.concatenate([q[:, h * 64:h * 64 + 64] for h in pair], 1))
            by_columns(np.concatenate([kc, vc, ks, kw], 1))
            by_columns(np.concatenate([vs, vw], 1))
            for w1 in (a["a_cmp_w1_k"][0], a["a_cmp_w1_v"][0]):
                w1 = w1.reshape(32, 64, 64).transpose(1, 0, 2).reshape(64, SLOT)
                slots.append(np.concatenate([w1, w1], 0))
            wo = a["ab_w_out"][0]
            by_rows(np.concatenate([wo[h * 64:h * 64 + 64] for h in pair] + [wo[512:]], 0))
            pk.add("w_gl_dt", np.concatenate([gl, dt], 1).reshape(C, P, 40).transpose(1, 0, 2).reshape(P, C * 40))
            for n in ("k", "v"):
                pe = a[f"a_cmp_pe_{n}"][0].T
                pk.add(f"cmp_pe_{n}", np.concatenate([pe, pe], 0))
                pk.add(f"cmp_w2_{n}", a[f"a_cmp_w2_{n}"][0])
            for k in range(4):
                pk.features(f"ssd_conv{k}", a["b_conv_w"][0, k, 0])
            pk.features("ssd_conv_b", a["b_conv_b"][0])
            pk.rows("dt_bias", a["b_dt_bias"][0])
            pk.rows("a_log", a["b_a_log"][0])
            pk.features("d_skip", np.repeat(a["b_d_skip"][0], 64))
            pk.features("ssd_norm", a["b_norm_w"][0])
        else:
            for n in range(6):
                pk.features(f"mu{n}", a["c_mu"][0, n])
            by_columns(np.concatenate([a["c_w1"][0], a["c_a1"][0]], 1))
            by_columns(a["c_g1"][0])
            lora = np.zeros((P, 2, D), np.float32)
            lora[:64, 0], lora[:64, 1] = a["c_w2"][0], a["c_a2"][0]
            slots.append(lora.reshape(P, SLOT))
            lora = np.zeros((P, 2, D), np.float32)
            lora[:, 0], lora[:32, 1] = a["c_g2"][0][:P], a["c_g2"][0][P:]
            slots.append(lora.reshape(P, SLOT))
            for n in ("r", "k", "v"):
                by_columns(a[f"c_w_{n}"][0])
            for i in range(2):
                by_columns(a["ada_w_2"][i])
            by_columns(a["c_w_o"][0])
            for n in ("w0", "a0", "k_k", "k_a", "r_k", "ln_g", "ln_b"):
                pk.features(n, a[f"c_{n}"][0].reshape(-1))
        gated(a["ffn2_w_gate"][layer], a["ffn2_w_up"][layer], a["ffn2_w_down"][layer])

    pk.features("c", a["c_2"][0])
    for i in range(2):
        pk.features(f"ada_b{i}", a["ada_b_2"][i])
        for n in range(4):
            pk.features(f"b{i}_norm{n}", a["norm_w_2"][i, n])
        if i == 0:
            for j in range(4):
                for part in range(3):
                    by_columns(a["conv_in_w_2"][0][:, part * D + j * FB:part * D + (j + 1) * FB])
            for k in range(3):
                pk.features(f"conv{k}", a["conv_w_2"][0, k])
            by_columns(a["conv_out_w_2"][0])
        else:
            by_columns(a["gdn_in_w_2"][0][:, :4096])
            pk.add("w_ba", a["gdn_in_w_2"][0][:, 4096:].reshape(C, P, 16).transpose(1, 0, 2).reshape(P, C * 16))
            for k in range(4):
                pk.features(f"gdn_conv{k}", a["gdn_conv_w_2"][0, k])
            pk.rows("gdn_a_log", a["gdn_a_log_2"][0])
            pk.rows("gdn_dt_bias", a["gdn_dt_bias_2"][0])
            pk.features("gdn_norm", a["gdn_norm_w_2"][0])
            by_columns(a["gdn_out_w_2"][0])
        router = np.concatenate([a["moe_group_w_2"][i], a["moe_expert_w_2"][i], a["shared_gate_w_2"][i]], 1)
        pk.add(f"router{i}", router.reshape(C, P, 73).transpose(1, 0, 2).reshape(P, C * 73))
        pk.rows(f"router_b{i}", np.concatenate([a["moe_group_b_2"][i], a["moe_expert_b_2"][i]]))
        gated(a["shared_w_gate_2"][i], a["shared_w_up_2"][i], a["shared_w_down_2"][i])
        for e in range(0, N_EXP, 2):
            for n, cut in (("gate", columns_slot), ("up", columns_slot), ("down", rows_slot)):
                slots += [cut(a[f"moe_w_{n}_2"][i, e + k]) for k in range(2)]
    xT = a["x"][0].T.reshape(C, P, T).transpose(1, 0, 2)
    return np.ascontiguousarray(xT), slots, pk


class Queue:

    def __init__(self, sem):
        self.sem, self.count, self.todo, self.seen = sem, 0, [], {}

    def wait(self, *tokens):
        for tok in tokens:
            if tok is None:
                continue
            if isinstance(tok, list):
                self.wait(*tok)
            elif self.seen.get(id(tok[0]), 0) < tok[1]:
                self.seen[id(tok[0])] = tok[1]
                self.todo.append(lambda e, s=tok[0], v=tok[1]: e.wait_ge(s, v))

    def silent(self, fn):
        self.todo.append(fn)

    def do(self, fn, *tokens):
        self.wait(*tokens)
        self.count += 1
        self.todo.append(lambda e, sem=self.sem: fn(e).then_inc(sem, 1))
        return (self.sem, self.count)

    def enter_branch(self, flag):
        def begin(e):
            self.branch = e.If(e.value_load(flag, min_val=0, max_val=1) > 0)
            self.branch.__enter__()
        self.todo.append(begin)

    def leave_branch(self):
        self.todo.append(lambda e: self.branch.__exit__(None, None, None))

    def play(self, e):
        for fn in self.todo:
            fn(e)


class Kernel:
    def __init__(self, nc, x_in, w_in, pack_in, out, n_slots, at):
        self.nc, self.x_in, self.w_in, self.pack_in, self.out = nc, x_in, w_in, pack_in, out
        self.n_slots, self.at = n_slots, at
        self.ctx = ExitStack()
        c = self.ctx
        sem = lambda n: c.enter_context(nc.semaphore(n))
        self.pe, self.dve = Queue(sem("pe_done")), Queue(sem("dve_done"))
        self.act, self.pool = Queue(sem("act_done")), Queue(sem("pool_done"))
        self.sp = Queue(None)
        self.in_sem, self.out_sem = sem("inputs_in"), sem("output_out")
        self.slot_sem = [sem(f"slot_in{i}") for i in range(RING + MOE_EXTRA)]
        self.slot_loads = [0] * (RING + MOE_EXTRA)
        self.where = {}
        self.next_load, self.extra_end = 0, 0
        sb = lambda n, s: c.enter_context(nc.sbuf_tensor(n, s, F32))
        self.ring = sb("weight_ring", [P, RING, SLOT])
        self.pk = sb("params_sb", [P, pack_in.shape[1]])
        self.x = sb("x_sb", [P, C, T])
        self.h = sb("h_sb", [P, C, T])
        self.y = sb("y_sb", [P, C, T])
        self.rms = sb("inv_rms", [P, 2, T])
        self.bank = [c.enter_context(nc.psum_tensor(f"bank{i}", [P, 512], F32)) for i in range(8)]
        self.free = {}
        self.turn = 0
        self.next_slot = 0
        self.stage_no = 0
        self.sp.silent(lambda e: e.dma_start(self.pk[:, :], pack_in).then_inc(self.in_sem, 16))
        self.sp.silent(lambda e: e.dma_start(self.x[:, :, :], x_in).then_inc(self.in_sem, 16))
        self.inputs = (self.in_sem, 32)
        for i in range(RING):
            self.load_next(i, self.ring[:, i, :])
        self.x_tok = self.inputs
        self.silu_c()
        self.h_free = self.y_free = self.rms_free = None
        self.filler = None

    def par(self, name, lo=0, n=None, rows=P):
        o, w = self.at[name]
        return self.pk[0:rows, o + lo:o + (w if n is None else lo + n)]

    def load_next(self, loc, mem, *after):
        i = self.next_load
        if i >= self.n_slots or (loc >= RING and i >= self.extra_end):
            return
        self.next_load += 1
        self.slot_loads[loc] += 1
        self.where[i] = (loc, mem, (self.slot_sem[loc], 16 * self.slot_loads[loc]))
        self.sp.wait(*after)
        self.sp.silent(lambda e: e.dma_start(mem, self.w_in[i]).then_inc(self.slot_sem[loc], 16))

    def more_slots(self, extra, stage_slots):
        self.extra_end = self.next_slot + stage_slots
        toks = [(q.sem, q.count) for q in (self.pe, self.dve, self.act, self.pool) if q.count]
        for n in range(extra.shape[1]):
            self.load_next(RING + n, extra[:, n, :], toks)

    def slot(self):
        i = self.next_slot
        self.next_slot += 1
        return (i, *self.where[i][1:])

    def slot_read(self, i, tok):
        self.load_next(*self.where[i][:2], tok)

    def half(self, banks=(4, 5, 6, 7)):
        ps, b, fr = self.full(banks)
        return ps[:, 0:T], b, fr

    def full(self, banks=(4, 5, 6, 7)):
        b = banks[self.turn % len(banks)]
        self.turn += 1
        return self.bank[b], b, self.free.get(b)

    def read_by(self, b, *toks):
        self.free[b] = list(toks)

    def mm(self, out, lhsT, rhs, start, stop, shared=False):
        self.pe.silent(lambda e: e.matmul(out, lhsT, rhs, start=start, stop=stop, skip_group_check=shared))

    def mm_end(self, out, lhsT, rhs, start, stop, shared=False):
        return self.pe.do(lambda e: e.matmul(out, lhsT, rhs, start=start, stop=stop, skip_group_check=shared))

    def transposed(self, out, in_, last=False):
        n = in_.shape[0]
        ident = self.par("ident", 0, n, n)
        if last:
            return self.pe.do(lambda e: e.transpose(out, in_, ident))
        self.pe.silent(lambda e: e.transpose(out, in_, ident))

    def tt(self, q, out, a, b, op, *tok):
        return q.do(lambda e: e.tensor_tensor(out, a, b, op), *tok)

    def ts(self, q, out, a, s1, s2, op0, op1, *tok):
        if op1 is None:
            return q.do(lambda e: e.tensor_scalar(out, a, s1, None, op0), *tok)
        return q.do(lambda e: e.tensor_scalar(out, a, s1, s2, op0, op1), *tok)

    def stt(self, out, a, s, b, op0, op1, *tok):
        return self.dve.do(lambda e: e.scalar_tensor_tensor(out=out, in0=a, scalar=s, in1=b, op0=op0, op1=op1), *tok)

    def func(self, out, a, f, *tok, scale=1.0, bias=0.0, accum=None):
        if accum is None:
            return self.act.do(lambda e: e.activation(out, a, f, scale=scale, bias=bias), *tok)
        return self.act.do(lambda e: e.activation(out, a, f, scale=scale, bias=bias, accum_out=accum), *tok)

    def copy(self, q, out, a, *tok):
        if q is self.act:
            return self.func(out, a, ACT.Copy, *tok)
        return q.do(lambda e: e.tensor_copy(out, a), *tok)

    def reduce(self, out, a, op, *tok):
        return self.dve.do(lambda e: e.tensor_reduce(out, a, AX, op), *tok)

    def barrier(self):
        toks = [(q.sem, q.count) for q in (self.pe, self.dve, self.act, self.pool) if q.count]
        for q in (self.pe, self.dve, self.act, self.pool):
            q.wait(*toks)

    def stage(self):
        self.barrier()
        self.stage_no += 1
        st = ExitStack()
        no, nc = self.stage_no, self.nc

        def sb(name, shape):
            return st.enter_context(nc.sbuf_tensor(f"{name}_{no}", shape, F32))
        return st, sb

    def inv_rms(self, squares, n, eps, toks, lhs="ones", scale=1.0, out=None):
        ps, key, fr = self.half()
        self.pe.wait(fr, self.inputs)
        for c, s in enumerate(squares):
            self.pe.wait(toks[c])
            if c == len(squares) - 1:
                tok = self.mm_end(ps[:, 0:s.shape[-1]], self.par(lhs), s, c == 0, True)
            else:
                self.mm(ps[:, 0:s.shape[-1]], self.par(lhs), s, c == 0, False)
        w = squares[0].shape[-1]
        out = self.rms[:, 0, :] if out is None else out
        s2 = 1.0 / (scale * scale)
        t = self.ts(self.dve, out, ps[:, 0:w], s2 / n, s2 * eps, ALU.mult, ALU.add, tok, self.rms_free)
        self.read_by(key, t)
        t = self.func(out, out, ACT.Ln, t)
        return self.func(out, out, ACT.Exp, t, scale=-0.5)

    def norm_x(self, gain, shift=None, tok=None):
        sq = self.y
        toks = []
        for n in range(4):
            t = self.func(sq[:, 2 * n:2 * n + 2, :], self.x[:, 2 * n:2 * n + 2, :], ACT.Square, self.x_tok, self.y_free)
            toks += [t, t]
        r = self.inv_rms([sq[:, c, :] for c in range(C)], D, NORM_EPS, toks)
        self.y_free = (self.pe.sem, self.pe.count)
        out = []
        for c in range(C):
            t = self.stt(self.h[:, c, :], self.x[:, c, :], gain[:, c:c + 1], self.rms[:, 0, :], ALU.mult, ALU.mult,
                         r, self.h_free, tok)
            if shift is not None:
                t = self.func(self.h[:, c, :], self.h[:, c, :], ACT.Identity, t, bias=shift[:, c:c + 1])
            out.append(t)
        self.rms_free = (self.dve.sem, self.dve.count)
        return out

    def add_back(self, y_toks, gain, scale, tok=None):
        toks, ysb = [], []
        sq = self.h
        for b in range(4):
            t = self.func(sq[:, 2 * b:2 * b + 2, :], self.bank[b][:, :].rearrange("p (c t) -> p c t", c=2), ACT.Square, y_toks[b])
            toks += [t, t]
            v = self.copy(self.dve, self.y[:, 2 * b:2 * b + 2, :], self.bank[b][:, :].rearrange("p (c t) -> p c t", c=2), y_toks[b], self.y_free, t)
            self.read_by(b, t, v)
            ysb.append(v)
        r = self.inv_rms([sq[:, c, :] for c in range(C)], D, NORM_EPS, toks, scale=scale)
        self.h_free = (self.pe.sem, self.pe.count)
        xt = []
        for c in range(C):
            t = self.stt(self.y[:, c, :], self.y[:, c, :], gain[:, c:c + 1], self.rms[:, 0, :], ALU.mult, ALU.mult, r, ysb[c // 2], tok)
            t = self.tt(self.pool, self.x[:, c, :], self.x[:, c, :], self.y[:, c, :], ALU.add, t, self.x_tok)
            xt.append(t)
        self.rms_free = (self.dve.sem, self.dve.count)
        self.x_tok = xt[-1]
        self.y_free = xt[-1]

    def gated_blocks(self, h_toks, n_blocks, gates=None, gate_tok=None, first=True, last=True, index=lambda b: b):
        st, sb = (self.scope, self.sbs)
        silu, hid = self.silu, self.hid
        pend = []

        def down():
            u, i_d, wd, d_tok, hid_tok = pend.pop(0)
            fc = u % 2
            self.pe.wait(hid_tok, d_tok)
            if u == 0:
                for b in range(4):
                    self.pe.wait(self.free.get(b))
            end = last and u == 2 * n_blocks - 1
            toks = []
            for c in range(C):
                args = (self.bank[c // 2][:, (c % 2) * T:(c % 2 + 1) * T], wd[:, fc * D + c * P:fc * D + (c + 1) * P],
                        hid[:, u % 4, :], first and u == 0 and c % 2 == 0, end and c % 2 == 1, True)
                if c == C - 1 or (end and c % 2):
                    toks.append(self.mm_end(*args))
                else:
                    self.mm(*args)
            self.hid_free[u % 4] = toks[-1]
            if fc == 1:
                self.slot_read(i_d, toks[-1])
            return toks

        for b in range(n_blocks):
            i_g, wg, g_tok = self.slot()
            i_u, wu, u_tok = self.slot()
            i_d, wd, d_tok = self.slot()
            for fc in range(2):
                u = 2 * b + fc
                bk = 4 + u % 3
                ps = self.bank[bk]
                self.pe.wait(self.free.get(bk))
                self.pe.wait(g_tok)
                for c in range(C):
                    if u == 0:
                        self.pe.wait(h_toks[c])
                    self.mm(ps[:, 0:T], wg[:, c * FB + fc * P:c * FB + (fc + 1) * P], self.h[:, c, :], c == 0, c == C - 1)
                self.pe.wait(u_tok)
                for c in range(C):
                    a = (ps[:, T:2 * T], wu[:, c * FB + fc * P:c * FB + (fc + 1) * P], self.h[:, c, :], c == 0, c == C - 1)
                    if c < C - 1:
                        self.mm(*a)
                    else:
                        up = self.mm_end(*a)
                if fc == 1:
                    self.slot_read(i_g, up)
                    self.slot_read(i_u, up)
                if gates is not None and fc == 0:
                    self.pe.wait(gate_tok, self.free.get(7))
                    gp = self.bank[7][:, 0:T]
                    n = gates.shape[0]
                    e = index(b)
                    gb = self.mm_end(gp, self.par("ident", e, 1, n).to_broadcast([n, P]), gates, True, True)
                    g_sb = self.gate_sb[:, b % 2, :]
                    gc = self.copy(self.act, g_sb, gp, gb, self.gate_free[b % 2])
                    self.read_by(7, gc)
                s = self.func(silu[:, u % 4, :], ps[:, 0:T], ACT.Silu, up, self.silu_free[u % 4])
                m = self.tt(self.dve, hid[:, u % 4, :], silu[:, u % 4, :], ps[:, T:2 * T], ALU.mult, s, up, self.hid_free[u % 4])
                self.silu_free[u % 4] = m
                self.read_by(bk, s, m)
                if gates is not None:
                    m = self.tt(self.dve, hid[:, u % 4, :], hid[:, u % 4, :], g_sb, ALU.mult, m, gc)
                    self.gate_free[b % 2] = m
                pend.append((u, i_d, wd, d_tok, m))
                if len(pend) > 2:
                    toks = down()
        while pend:
            toks = down()
        return toks

    def gated_scope(self):
        self.scope, sb = self.stage()
        self.sbs = sb
        self.silu, self.hid, self.gate_sb = sb("silu", [P, 4, T]), sb("hid", [P, 4, T]), sb("gate_rows", [P, 2, T])
        self.silu_free, self.hid_free, self.gate_free = [None] * 4, [None] * 4, [None] * 2

    def split(self, hi, lo, a, *tok):
        t1 = self.func(hi, a, ACT.Copy, *tok)
        t2 = self.tt(self.dve, lo, a, hi.bitcast(F32), ALU.subtract, t1, *tok)
        return [t1, t2]

    def mm3(self, out, w, x, start, stop, shared=False, signal=False):
        self.mm(out, w[0], x[0], start, False, shared)
        self.mm(out, w[0], x[1], False, False, shared)
        return (self.mm_end if signal else self.mm)(out, w[1], x[0], False, stop, shared)

    def ffn(self, g_in, g_out):
        st, sb = self.stage()
        sbr = lambda n, shape: st.enter_context(self.nc.sbuf_tensor(f"{n}_{self.stage_no}", shape, F32R))
        units, NB = 2 * FFN_BLOCKS, 3
        h_r = sbr("h_hi_lo", [P, 2, C, T])
        gu_r = sbr("gate_up_hi_lo", [P, NB, 2, 2, C, P])
        d_r = sbr("down_hi_lo", [P, 2, 2, D])
        hid_r = sbr("hidden_hi_lo", [P, 2, 2, T])
        silu, hid = sb("silu", [P, 2, T]), sb("hidden", [P, 2, T])
        gu_free, d_free, silu_free, hid_free, hr_free = [None] * NB, [None] * 2, [None] * 2, [None] * 2, [None] * 2
        blocks, gu_tok, d_tok = {}, {}, {}

        def split_gate_up(u):
            if u >= units:
                return
            b, fc, k = u // 2, u % 2, u % NB
            if fc == 0:
                blocks[b] = [self.slot() for _ in range(3)]
            toks = []
            for n in range(2):
                i, w, tok = blocks[b][n]
                half = w.rearrange("p (c f) -> p c f", c=C)[:, :, fc * P:(fc + 1) * P]
                t = self.split(gu_r[:, k, n, 0, :, :], gu_r[:, k, n, 1, :, :], half, tok, gu_free[k])
                toks += t
                if fc:
                    self.slot_read(i, t)
            gu_tok[u] = toks

        def split_down(u):
            if u >= units:
                return
            b, fc, k = u // 2, u % 2, u % 2
            i, w, tok = blocks[b][2]
            d_tok[u] = self.split(d_r[:, k, 0, :], d_r[:, k, 1, :], w[:, fc * D:(fc + 1) * D], tok, d_free[k])
            if fc:
                self.slot_read(i, d_tok[u])

        split_gate_up(0)
        h_toks = self.norm_x(self.par(g_in))
        hr_toks = [self.split(h_r[:, 0, c, :], h_r[:, 1, c, :], self.h[:, c, :], h_toks[c]) for c in range(C)]
        split_down(0)
        split_gate_up(1)
        self.h_free = hr_toks[-1]

        def gate_up(u):
            bk, k = 4 + u % 4, u % NB
            ps = self.bank[bk]
            self.pe.wait(self.free.get(bk), gu_tok[u])
            for n in range(2):
                for c in range(C):
                    if u == 0:
                        self.pe.wait(hr_toks[c])
                    end = self.mm3(ps[:, n * T:(n + 1) * T], (gu_r[:, k, n, 0, c, :], gu_r[:, k, n, 1, c, :]),
                                   (h_r[:, 0, c, :], h_r[:, 1, c, :]), c == 0, c == C - 1, signal=n and c == C - 1)
            gu_free[k] = end
            k = u % 2
            s = self.func(silu[:, k, :], ps[:, 0:T], ACT.Silu, end, silu_free[k])
            m = self.tt(self.dve, hid[:, k, :], silu[:, k, :], ps[:, T:2 * T], ALU.mult, s, hid_free[k])
            silu_free[k] = m
            self.read_by(bk, m)
            hid_free[k] = self.split(hid_r[:, k, 0, :], hid_r[:, k, 1, :], hid[:, k, :], m, hr_free[k])

        def down(u):
            k, out = u % 2, []
            self.pe.wait(d_tok[u], hid_free[k])
            for c in range(C):
                if u == 0 and c % 2 == 0:
                    self.pe.wait(self.free.get(c // 2))
                end = u == units - 1 and c % 2 == 1
                t = self.mm3(self.bank[c // 2][:, (c % 2) * T:(c % 2 + 1) * T], (d_r[:, k, 0, c * P:(c + 1) * P], d_r[:, k, 1, c * P:(c + 1) * P]),
                             (hid_r[:, k, 0, :], hid_r[:, k, 1, :]), u == 0 and c % 2 == 0, end, True, signal=end or c == C - 1)
                if end:
                    out.append(t)
            d_free[k] = hr_free[k] = t
            return out

        for u in range(units):
            split_gate_up(u + 2)
            if u:
                split_down(u)
            gate_up(u)
            if u:
                down(u - 1)
        self.add_back(down(units - 1), self.par(g_out), 0.5)
        st.close()

    def columns(self, act_in, toks, n_slots, consume, tiles=2):
        for n in range(n_slots):
            i, w, tok = self.slot()
            for fc in range(tiles):
                ps, key, fr = self.half()
                self.pe.wait(fr, tok)
                for c in range(C):
                    self.pe.wait(toks[c])
                    a = (ps, w[:, c * FB + fc * P:c * FB + (fc + 1) * P], act_in[:, c, :], c == 0, c == C - 1)
                    if c < C - 1:
                        self.mm(*a)
                    else:
                        end = self.mm_end(*a)
                self.read_by(key, consume(2 * n + fc, ps, end))
            self.slot_read(i, end)

    def project_out(self, src, n_chunks, toks):
        for b in range(4):
            self.pe.wait(self.free.get(b))
        out = []
        for n in range(n_chunks // 2):
            i, w, tok = self.slot()
            self.pe.wait(tok)
            for k in range(2):
                kc = 2 * n + k
                self.pe.wait(toks[kc])
                end = kc == n_chunks - 1
                for c in range(C):
                    a = (self.bank[c // 2][:, (c % 2) * T:(c % 2 + 1) * T], w[:, k * D + c * P:k * D + (c + 1) * P],
                         src(kc), kc == 0 and c % 2 == 0, end and c % 2 == 1, True)
                    if (end and c % 2) or (k == 1 and c == C - 1):
                        t = self.mm_end(*a)
                        if end:
                            out.append(t)
                    else:
                        self.mm(*a)
            self.slot_read(i, t)
        return out

    def project_columns_out(self, src, toks):
        out = []
        for n in range(4):
            i, w, tok = self.slot()
            self.pe.wait(tok, self.free.get(n))
            for fc in range(2):
                for c in range(C):
                    self.pe.wait(toks[c])
                    a = (self.bank[n][:, fc * T:(fc + 1) * T], w[:, c * FB + fc * P:c * FB + (fc + 1) * P], src[:, c, :], c == 0, c == C - 1)
                    if c < C - 1:
                        self.mm(*a)
                    else:
                        t = self.mm_end(*a)
            self.slot_read(i, t)
            out.append(t)
        return out

    def finish(self):
        self.sp.wait(self.x_tok)
        self.sp.silent(lambda e: e.dma_start(self.out, self.x[:, :, :]).then_inc(self.out_sem, 16))
        self.sp.silent(lambda e: e.wait_ge(self.out_sem, 16))
        block = self.ctx.enter_context(self.nc.Block())

        @block.sync
        def _(e):
            self.sp.play(e)

        @block.tensor
        def _(e):
            self.pe.play(e)

        @block.vector
        def _(e):
            self.dve.play(e)

        @block.scalar
        def _(e):
            self.act.play(e)

        @block.gpsimd
        def _(e):
            self.pool.play(e)
        self.ctx.close()

    def silu_c(self):
        self.cs = self.ctx.enter_context(self.nc.sbuf_tensor("silu_c", [P, C], F32))
        self.mod = [self.ctx.enter_context(self.nc.sbuf_tensor(f"mod{i}", [P, 6 * C], F32)) for i in range(2)]
        self.mod_rows = self.ctx.enter_context(self.nc.sbuf_tensor("mod_rows", [P, 2, FB], F32))
        self.mod_rows_free = [None, None]
        self.gain = self.ctx.enter_context(self.nc.sbuf_tensor("mod_gain", [P, 2, 4, C], F32))
        self.cs_tok = self.func(self.cs[:, :], self.par("c"), ACT.Silu, self.inputs)

    def modulation(self, i):
        self.pe.wait(self.cs_tok)
        ps = self.bank[0]
        self.pe.wait(self.free.get(0))
        for n in range(6 * D // FB):
            s, w, tok = self.slot()
            k = 1 + n % 2
            self.pe.wait(tok, self.free.get(k))
            for c in range(C):
                o = self.bank[k][32 * (c % 4):32 * (c % 4) + 32, 0:FB]
                a = (o, self.cs[:, c:c + 1].to_broadcast([P, 32]), w[:, c * FB:(c + 1) * FB], c < 4, c >= 4)
                end = self.mm_end(*a) if c == C - 1 else self.mm(*a)
            self.slot_read(s, end)
            t = self.copy(self.act, self.mod_rows[:, n % 2, :], self.bank[k][:, 0:FB], end, self.mod_rows_free[n % 2])
            self.read_by(k, t)
            yield
            self.pe.wait(t)
            for fc in range(2):
                a = (ps[:, 2 * n + fc:2 * n + fc + 1], self.mod_rows[:, n % 2, fc * P:(fc + 1) * P], self.par("one_32nd"), True, True)
                end = self.mm_end(*a) if fc else self.mm(*a)
            self.mod_rows_free[n % 2] = end
        b = 0
        mod, g = self.mod[i], self.gain
        t = self.tt(self.dve, mod[:, :], ps[:, 0:6 * C], self.par(f"ada_b{i}"), ALU.add, end, self.inputs)
        self.read_by(b, t)
        part = lambda n: mod[:, n * C:(n + 1) * C]
        toks = []
        for n, (m, w) in enumerate(((1, 0), (4, 2))):
            toks.append(self.stt(g[:, i, w, :], part(m), 1.0, self.par(f"b{i}_norm{w}"), ALU.add, ALU.mult, t))
        for m, w in ((2, 1), (5, 3)):
            toks.append(self.tt(self.dve, g[:, i, w, :], part(m), self.par(f"b{i}_norm{w}"), ALU.mult, t))
        self.mod_tok = toks[-1]

    def both_modulations(self):
        for i in range(2):
            yield from self.modulation(i)

    def background(self, n=1):
        for _ in range(n):
            if self.filler is not None and next(self.filler, True):
                self.filler = None

    def first_equal(self, out, vals, best, tmp, tok):
        t = self.ts(self.dve, tmp, vals, best, None, ALU.is_equal, None, tok)
        t = self.tt(self.dve, tmp, tmp, self.par("rank8"), ALU.mult, t)
        t = self.reduce(out[:, 0:1], tmp, ALU.max, t)
        t = self.ts(self.dve, tmp, tmp, out[:, 0:1], None, ALU.is_equal, None, t)
        return self.copy(self.dve, out, tmp, t)

    def router(self, i, sb, h_toks):
        gates, picks, shared, rank = [], [], sb("shared_gate", [P, TT]), sb("ranks", [P, TT, N_EXP])
        g_tok, m_tok = [], []
        for q in range(TT):
            ps, key, fr = self.half()
            self.pe.wait(fr, self.inputs)
            for c in range(C):
                self.pe.wait(h_toks[c])
                a = (ps[:, 0:73], self.h[:, c, q * P:(q + 1) * P], self.par(f"router{i}", c * 73, 73), c == 0, c == C - 1)
                end = self.mm_end(*a) if c == C - 1 else self.mm(*a)
            lg, s = sb(f"logits{q}", [P, 73]), sb(f"route{q}", [P, 96])
            t = self.tt(self.dve, lg[:, 0:72], ps[:, 0:72], self.par(f"router_b{i}"), ALU.add, end)
            t_sh = self.func(shared[:, q:q + 1], ps[:, 72:73], ACT.Sigmoid, end, t)
            self.read_by(key, t_sh)
            gl, el = lg[:, 0:8], lg[:, 8:72]
            best, psel, tmp, grp, tmp2 = s[:, 0:1], s[:, 1:2], s[:, 8:16], s[:, 16:24], s[:, 24:32]
            t = self.reduce(best, gl, ALU.max, t)
            t1 = self.first_equal(grp, gl, best, tmp, t)
            t = self.ts(self.dve, tmp2, gl, best, None, ALU.subtract, None, t)
            t = self.func(tmp2, tmp2, ACT.Exp, t, accum=psel)
            t2 = self.dve.do(lambda e, psel=psel: e.reciprocal(psel, psel), t)
            prod = sb(f"picked{q}", [P, N_EXP])
            v = lambda a: a.rearrange("p (g e) -> p g e", g=N_GRP)
            t = self.tt(self.dve, v(prod[:, :]), v(el), grp.unsqueeze(2).to_broadcast([P, N_GRP, 8]), ALU.mult, t1)
            els = s[:, 32:40]
            t = self.reduce(els, prod[:, :].rearrange("p (g e) -> p e g", g=N_GRP), ALU.add, t)
            m1, m2, e1, e2, g1, g2 = s[:, 2:3], s[:, 3:4], s[:, 40:48], s[:, 48:56], s[:, 4:5], s[:, 5:6]
            t = self.reduce(m1, els, ALU.max, t)
            t = self.first_equal(e1, els, m1, tmp, t)
            rest, both = s[:, 56:64], s[:, 64:72]
            t = self.stt(rest, e1, NEG, els, ALU.mult, ALU.add, t)
            t = self.reduce(m2, rest, ALU.max, t)
            t = self.first_equal(e2, rest, m2, tmp, t)
            spread = lambda out, x, *tok: self.tt(self.dve, v(out), grp.unsqueeze(2).to_broadcast([P, N_GRP, 8]),
                                                  x.unsqueeze(1).to_broadcast([P, N_GRP, 8]), ALU.mult, *tok)
            t = self.tt(self.dve, both, e1, e2, ALU.add, t)
            t = spread(prod[:, :], both, t)
            picks.append(prod)
            m_tok.append(t)
            t = self.tt(self.dve, g2, m2, m1, ALU.subtract, t)
            t = self.func(g2, g2, ACT.Exp, t)
            t = self.ts(self.dve, g1, g2, 1.0, None, ALU.add, None, t)
            t = self.dve.do(lambda e, g1=g1: e.reciprocal(g1, g1), t)
            t = self.tt(self.dve, g1, g1, psel, ALU.mult, t, t2)
            t = self.tt(self.dve, g2, g2, g1, ALU.mult, t)
            t = self.ts(self.dve, e1, e1, g1, None, ALU.mult, None, t)
            t = self.stt(e1, e2, g2, e1, ALU.mult, ALU.add, t)
            gates.append(sb(f"gates{q}", [P, N_EXP]))
            g_tok.append(spread(gates[q][:, :], e1, t))
        ps, key, fr = self.half()
        self.pe.wait(fr, m_tok)
        self.mm(ps[:, 0:64], self.par("upto"), picks[0][:, :], True, True)
        self.mm(ps[:, 64:128], self.par("ones"), picks[0][:, :], True, False)
        self.mm(ps[:, 64:128], self.par("upto"), picks[1][:, :], False, True)
        self.mm(ps[:, 128:192], self.par("ones"), picks[0][:, :], True, False)
        end = self.mm_end(ps[:, 128:192], self.par("ones"), picks[1][:, :], False, True)
        for q in range(TT):
            r_tok = self.tt(self.dve, rank[:, q, :], ps[:, q * 64:(q + 1) * 64], picks[q][:, :], ALU.mult, end)
        most = sb("most_tokens", [P, 1])
        t = self.reduce(most[:, :], ps[:, 128:192], ALU.max, end)
        self.read_by(key, t)
        flag = self.scope.enter_context(self.nc.sbuf_tensor(f"overflows_{self.stage_no}", [P, 1], mybir.dt.int32))
        f_tok = self.ts(self.dve, flag[:, :], most[:, :], float(CAP), None, ALU.is_gt, None, t)
        row = sb("shared_gate_row", [1, T])
        ps, key, fr = self.half()
        self.pe.wait(fr, t_sh)
        for q in range(TT):
            end = self.transposed(ps[0:1, q * P:(q + 1) * P], shared[:, q:q + 1], last=True)
        t = self.copy(self.act, row[:, :], ps[0:1, 0:T], end)
        self.read_by(key, t)
        return gates, g_tok, rank, r_tok, row, t, flag, f_tok

    def moe(self, i):
        self.gated_scope()
        sb = self.sbs
        extra = sb("more_slots", [P, MOE_EXTRA, SLOT])
        self.more_slots(extra, 3 * (SHARED_BLOCKS + N_EXP))
        part = lambda n: self.mod[i][:, n * C:(n + 1) * C]
        h_toks = self.norm_x(self.gain[:, i, 2, :], part(3), self.mod_tok)
        gates, g_tok, rank, r_tok, row, row_tok, flag, f_tok = self.router(i, sb, h_toks)
        h_tok = self.y[:, :, :].rearrange("p c t -> p (c t)").rearrange("p (q d) -> p q d", q=TT)
        for q in range(TT):
            for n in range(2):
                ps, b, fr = self.full()
                self.pe.wait(fr)
                for m in range(4):
                    end = self.transposed(ps[:, m * P:(m + 1) * P], self.h[:, 4 * n + m, q * P:(q + 1) * P], last=m == 3)
                ht = self.copy(self.act, h_tok[:, q, n * 512:(n + 1) * 512], ps[:, :], end, self.y_free)
                self.read_by(b, ht)
        self.gated_blocks(h_toks, SHARED_BLOCKS, row[:, :], row_tok, last=False, index=lambda b: 0)
        first_expert = self.next_slot
        self.packed_experts(sb, gates, g_tok, rank, r_tok, h_tok, ht)
        y = self.experts_end
        self.y_free = y
        self.overflow(i, sb, flag, f_tok, gates, rank, extra, first_expert)
        self.add_back([y] * 4, self.gain[:, i, 3, :], 1.0)
        self.scope.close()

    def packed_experts(self, sb, gates, g_tok, rank, r_tok, h_tok, ht):
        two = lambda n, shape: [sb(f"{n}{k}", shape) for k in range(2)]
        sel, selg = two("places", [P, TT, 4, CAP]), two("gated_places", [P, TT, 4, CAP])
        hc, out, turned = two("packed_h", [P, C, P]), two("down", [P, D]), two("hidden_and_scatter_T", [P, 2 * T])
        silu, hid = two("packed_silu", [P, FB]), two("packed_hidden", [P, FB])
        free = {n: [None, None] for n in ("sel", "selg", "hc", "out", "turned", "silu", "hid")}
        done = {}
        PAIRS = N_EXP // 2

        def select(g):
            k = g % 2
            for q in range(TT):
                r = rank[:, q, 4 * g:4 * g + 4].unsqueeze(2).to_broadcast([P, 4, CAP])
                t = self.tt(self.dve, sel[k][:, q, :, :], self.par("places").unsqueeze(1).to_broadcast([P, 4, CAP]), r, ALU.is_equal, r_tok, free["sel"][k])
                done["sel", g, q] = t
                done["selg", g, q] = self.tt(self.dve, selg[k][:, q, :, :], sel[k][:, q, :, :],
                                             gates[q][:, 4 * g:4 * g + 4].unsqueeze(2).to_broadcast([P, 4, CAP]), ALU.mult, t, g_tok[q], free["selg"][k])

        def places(buf, p, q):
            return buf[(p // 2) % 2][:, q, 2 * (p % 2):2 * (p % 2) + 2, :]

        def gather(p, n):
            ps, b, fr = self.full()
            self.pe.wait(fr, ht, done["sel", p // 2, 0], done["sel", p // 2, 1])
            for m in range(4):
                c = 4 * n + m
                self.mm(ps[:, m * P:(m + 1) * P], h_tok[:, 0, c * P:(c + 1) * P], places(sel, p, 0), True, False)
                a = (ps[:, m * P:(m + 1) * P], h_tok[:, 1, c * P:(c + 1) * P], places(sel, p, 1), False, True)
                end = self.mm_end(*a) if m == 3 else self.mm(*a)
            if p % 2 == 1 and n == 1:
                free["sel"][(p // 2) % 2] = end
            t = self.copy(self.act, hc[p % 2][:, 4 * n:4 * n + 4, :], ps[:, :].rearrange("p (m t) -> p m t", m=4), end, free["hc"][p % 2])
            self.read_by(b, t)
            done["hc", p, n] = t

        def gate_up(p):
            w = [self.slot() for _ in range(6)]
            done["wd", p] = w[4:]
            ps, b, fr = self.full()
            self.pe.wait(fr, done["hc", p, 0], done["hc", p, 1])
            for n in range(2):
                for c in range(C):
                    for e in range(2):
                        self.pe.wait(w[2 * n + e][2])
                        a = (ps[e * CAP:(e + 1) * CAP, n * FB:(n + 1) * FB], hc[p % 2][:, c, e * CAP:(e + 1) * CAP],
                             w[2 * n + e][1][:, c * FB:(c + 1) * FB], c == 0, c == C - 1)
                        end = self.mm_end(*a) if e and c == C - 1 else self.mm(*a)
                for e in range(2):
                    self.slot_read(w[2 * n + e][0], end)
            free["hc"][p % 2] = end
            k = p % 2
            t = self.func(silu[k][:, :], ps[:, 0:FB], ACT.Silu, end, free["silu"][k])
            t = self.tt(self.dve, hid[k][:, :], silu[k][:, :], ps[:, FB:2 * FB], ALU.mult, t, free["hid"][k])
            free["silu"][k] = t
            self.read_by(b, t)
            done["hid", p] = t

        def turn(p):
            ps, b, fr = self.full()
            self.pe.wait(fr, done["hid", p], done["selg", p // 2, 0], done["selg", p // 2, 1])
            for fc in range(2):
                self.transposed(ps[:, fc * P:(fc + 1) * P], hid[p % 2][:, fc * P:(fc + 1) * P])
            for q in range(TT):
                end = self.transposed(ps[:, T + q * P:T + (q + 1) * P], places(selg, p, q).rearrange("p e s -> p (e s)"), last=q == 1)
            if p % 2 == 1:
                free["selg"][(p // 2) % 2] = end
            free["hid"][p % 2] = end
            t = self.copy(self.act, turned[p % 2][:, :], ps[:, :], end, free["turned"][p % 2])
            self.read_by(b, t)
            done["turned", p] = t

        def down(p, n):
            ps, b, fr = self.full()
            self.pe.wait(fr, done["turned", p])
            for fc in range(2):
                for e in range(2):
                    i, wd, tok = done["wd", p][e]
                    self.pe.wait(tok)
                    a = (ps[e * CAP:(e + 1) * CAP, :], turned[p % 2][:, fc * P + e * CAP:fc * P + (e + 1) * CAP],
                         wd[:, fc * D + n * 512:fc * D + (n + 1) * 512], fc == 0, fc == 1)
                    end = self.mm_end(*a) if fc and e else self.mm(*a)
            if n == 1:
                for e in range(2):
                    self.slot_read(done["wd", p][e][0], end)
            t = self.copy(self.dve, out[p % 2][:, n * 512:(n + 1) * 512], ps[:, :], end, free["out"][p % 2])
            self.read_by(b, t)
            done["out", p, n] = t

        def scatter(p):
            self.pe.wait(done["out", p, 0], done["out", p, 1])
            for c in range(C):
                a = (self.bank[c // 2][:, (c % 2) * T:(c % 2 + 1) * T], out[p % 2][:, c * P:(c + 1) * P], turned[p % 2][:, T:2 * T],
                     False, p == PAIRS - 1 and c % 2 == 1, True)
                end = self.mm_end(*a) if c == C - 1 else self.mm(*a)
            free["out"][p % 2] = free["turned"][p % 2] = end
            return end

        select(0)
        gather(0, 0)
        gather(0, 1)
        for p in range(PAIRS):
            more = p + 1 < PAIRS
            gate_up(p)
            if p % 2 == 0 and more:
                select(p // 2 + 1) if p // 2 + 1 < N_EXP // 4 else None
            if more:
                gather(p + 1, 0)
            if p:
                scatter(p - 1)
            turn(p)
            if more:
                gather(p + 1, 1)
            down(p, 0)
            down(p, 1)
        self.experts_end = scatter(PAIRS - 1)

    def overflow(self, i, sb, flag, f_tok, gates, rank, buf, first_expert):
        nc = self.nc
        queues = (self.sp, self.pe, self.dve, self.act, self.pool)
        ready = [f_tok, self.experts_end]
        saved, banks = [], dict(self.free)
        load = self.ctx.enter_context(nc.semaphore(f"overflow_load{i}"))
        for n, q in enumerate(queues):
            q.wait(*ready)
            saved.append((q.sem, q.count, dict(q.seen)))
            q.enter_branch(flag[0:1, 0:1])
            q.sem = self.ctx.enter_context(nc.semaphore(f"overflow_{n}_{i}")) if n else None
            q.count = 0
        late, gates_T = sb("late_gates", [P, N_EXP]), sb("late_gates_T", [N_EXP, T])
        t = None
        for q in range(TT):
            t = self.stt(late[:, :], rank[:, q, :], float(CAP), gates[q][:, :], ALU.is_gt, ALU.mult, t)
            self.pe.wait(t)
            end = self.transposed(self.bank[4][0:N_EXP, 0:P], late[:, :], last=True)
            t = self.copy(self.dve, gates_T[:, q * P:(q + 1) * P], self.bank[4][0:N_EXP, 0:P], end)
        grow, act_, hid = self.gate_sb, self.silu, self.hid
        end = None
        for e in range(N_EXP):
            for n in range(3):
                self.sp.wait(end)
                self.sp.silent(lambda q, n=n, e=e: q.dma_start(buf[:, n, :], self.w_in[first_expert + 6 * (e // 2) + 2 * n + e % 2]).then_inc(load, 16))
            self.pe.wait(t, (load, 48 * (e + 1)))
            gb = self.mm_end(self.bank[6][:, 0:T], self.par("ident", e, 1, N_EXP).to_broadcast([N_EXP, P]), gates_T[:, :], True, True)
            t_g = self.copy(self.act, grow[:, 0, :], self.bank[6][:, 0:T], gb)
            for fc in range(2):
                ps = self.bank[4 + fc]
                for n in range(2):
                    for c in range(C):
                        a = (ps[:, n * T:(n + 1) * T], buf[:, n, c * FB + fc * P:c * FB + (fc + 1) * P], self.h[:, c, :], c == 0, c == C - 1)
                        up = self.mm_end(*a) if n and c == C - 1 else self.mm(*a)
                t = self.func(act_[:, fc, :], ps[:, 0:T], ACT.Silu, up, t_g)
                t = self.tt(self.dve, hid[:, fc, :], act_[:, fc, :], ps[:, T:2 * T], ALU.mult, t)
                t = self.tt(self.dve, hid[:, fc, :], hid[:, fc, :], grow[:, 0, :], ALU.mult, t)
                self.pe.wait(t)
                for c in range(C):
                    a = (self.bank[c // 2][:, (c % 2) * T:(c % 2 + 1) * T], buf[:, 2, fc * D + c * P:fc * D + (c + 1) * P], hid[:, fc, :], False, False, True)
                    end = self.mm_end(*a) if c == C - 1 else self.mm(*a)
        ends = [(q.sem, q.count) for q in queues[1:] if q.count]
        for q, (sem, count, seen) in zip(queues, saved):
            q.wait(*ends)
            q.leave_branch()
            q.sem, q.count, q.seen = sem, count, seen
        self.free = banks

    def conv_mixer(self, i):
        st, sb = self.stage()
        part = lambda n: self.mod[i][:, n * C:(n + 1) * C]
        h_toks = self.norm_x(self.gain[:, i, 0, :], part(0), self.mod_tok)
        K = 3
        b_T, u, g_T = sb("conv_b", [P, C, T]), sb("conv_u", [P, C, K - 1 + T]), sb("conv_gate", [P, 2, T])
        out, taps = sb("conv_out", [P, C, T]), sb("conv_taps", [P, 2, T])
        z = self.pool.do(lambda e: e.memset(u[:, :, 0:K - 1], 0.0))
        gate_free, taps_free, toks = [None] * 2, [None] * 2, []
        for j in range(4):
            tok = {}

            def keep(part_no):
                def consume(n, ps, end):
                    c = 2 * j + n
                    if part_no == 0:
                        t = self.copy(self.act, b_T[:, c, :], ps, end)
                    elif part_no == 1:
                        t = self.copy(self.act, g_T[:, n, :], ps, end, gate_free[n])
                    else:
                        t = self.tt(self.dve, u[:, c, K - 1:], g_T[:, n, :], ps, ALU.mult, end, tok[1, n])
                        gate_free[n] = t
                    tok[part_no, n] = t
                    return t
                return consume
            for part_no in range(3):
                self.columns(self.h, h_toks, 1, keep(part_no))
            for n in range(2):
                c = 2 * j + n
                t = self.ts(self.dve, taps[:, n, :], u[:, c, 0:T], self.par("conv0")[:, c:c + 1], None, ALU.mult, None, tok[2, n], z, taps_free[n])
                for k in range(1, K):
                    t = self.stt(taps[:, n, :], u[:, c, k:k + T], self.par(f"conv{k}")[:, c:c + 1], taps[:, n, :], ALU.mult, ALU.add, t)
                t = self.tt(self.pool, out[:, c, :], taps[:, n, :], b_T[:, c, :], ALU.mult, t, tok[0, n])
                taps_free[n] = t
                toks.append(t)
        self.add_back(self.project_columns_out(out, toks), self.gain[:, i, 1, :], 1.0)
        st.close()
    def conv_chunk(self, out, src, taps, bias, c, n_taps, tok, out_free=None):
        w = lambda k: self.par(f"{taps}{k}")[:, c:c + 1]
        if bias is None:
            t = self.ts(self.dve, out, src[:, 0:T], w(0), None, ALU.mult, None, tok, out_free)
        else:
            t = self.ts(self.dve, out, src[:, 0:T], w(0), bias[:, c:c + 1], ALU.mult, ALU.add, tok, out_free)
        for k in range(1, n_taps):
            t = self.stt(out, src[:, k:k + T], w(k), out, ALU.mult, ALU.add, t)
        return t

    def softplus(self, v, tmp, tok):
        t = self.stt(tmp, v, -1.0, v, ALU.mult, ALU.max, tok)
        t = self.func(tmp, tmp, ACT.Exp, t, scale=-1.0)
        t = self.func(tmp, tmp, ACT.Ln, t, bias=self.par("ones", 0, 1))
        return self.stt(v, v, 0.0, tmp, ALU.max, ALU.add, t)

    def rotate(self, dst, src, tok, tmp, tmp_free):
        ps, b, fr = self.half()
        self.pe.wait(fr, tok)
        end = self.mm_end(ps, self.par("turn"), src, True, True)
        t = self.tt(self.dve, tmp, ps, self.par("sin"), ALU.mult, end, tmp_free)
        self.read_by(b, t)
        t2 = self.tt(self.pool, src, src, self.par("cos"), ALU.mult, end)
        return self.tt(self.dve, dst, src, tmp, ALU.add, t, t2)

    def nsa_ssd_mixer(self):
        st, sb = self.stage()
        h_toks = self.norm_x(self.par("a0_gain2"))
        K, G = 4, 2
        mix = sb("mix_in", [P, 12, T])
        silu_z = sb("silu_z", [P, C, T])
        xbc = sb("xbc", [P, 12, T])
        small = sb("gate_dt", [P, TT, 40])
        outer = ExitStack()
        tmp_sb = lambda n, s: outer.enter_context(self.nc.sbuf_tensor(f"{n}_{self.stage_no}", s, F32))
        raw, taps = tmp_sb("xbc_raw", [P, 2, K - 1 + T]), tmp_sb("xbc_taps", [P, 2, T])
        z0 = self.pool.do(lambda e: e.memset(raw[:, :, 0:K - 1], 0.0))
        raw_free, taps_free, xbc_tok = [None] * 2, [None] * 2, [None] * 12

        def conv_in(c, ps, end):
            n = c % 2
            t = self.copy(self.act, raw[:, n, K - 1:], ps, end, raw_free[n])
            v = self.conv_chunk(taps[:, n, :], raw[:, n, :], "ssd_conv", self.par("ssd_conv_b"), c, K, [t, z0], taps_free[n])
            raw_free[n] = v
            xbc_tok[c] = taps_free[n] = self.func(xbc[:, c, :], taps[:, n, :], ACT.Silu, v)
            return t
        self.columns(self.h, h_toks, 6, conv_in)
        z_tok = [None] * C

        def z_in(c, ps, end):
            z_tok[c] = self.func(silu_z[:, c, :], ps, ACT.Silu, end)
            return z_tok[c]
        self.columns(self.h, h_toks, 4, z_in)
        small_tok = []
        for q in range(TT):
            ps, b, fr = self.half()
            self.pe.wait(fr, self.inputs)
            for c in range(C):
                a = (ps[:, 0:40], self.h[:, c, q * P:(q + 1) * P], self.par("w_gl_dt", c * 40, 40), c == 0, c == C - 1)
                end = self.mm_end(*a) if c == C - 1 else self.mm(*a)
            t = self.func(small[:, q, 0:24], ps[:, 0:24], ACT.Sigmoid, end)
            t2 = self.tt(self.dve, small[:, q, 24:40], ps[:, 24:40], self.par("dt_bias"), ALU.add, end, t)
            self.read_by(b, t2)
            small_tok.append([t, t2])
        outer.close()
        self.barrier()
        self.attention(mix, small, h_toks)
        self.barrier()
        self.ssd(mix, small, xbc, silu_z)
        toks = [(self.dve.sem, self.dve.count)] * 12
        self.add_back(self.project_out(lambda c: mix[:, c, :], 12, toks), self.par("a0_gain3"), 1.0)
        st.close()

    def attention(self, mix, small, h_toks):
        st = ExitStack()
        sb = lambda n, s: st.enter_context(self.nc.sbuf_tensor(f"{n}_{self.stage_no}", s, F32))
        qT, kv, v_tok = sb("q_T", [P, 4, T]), sb("kc_vc_ks_kw_T", [P, 4, T]), sb("vs_vw", [P, TT, T])
        tmp = sb("rope_tmp", [P, 2, T])
        tmp_free, rope_tok, n_rope = [None] * 2, {}, [0]

        def rope_into(dst, name):
            def consume(c, ps, end):
                t = self.copy(self.act, dst[:, c, :], ps, end)
                if name == "q" or c != 1:
                    n = n_rope[0] % 2
                    n_rope[0] += 1
                    rope_tok[name, c] = tmp_free[n] = self.rotate(dst[:, c, :], dst[:, c, :], t, tmp[:, n, :], tmp_free[n])
                else:
                    rope_tok[name, c] = t
                return t
            return consume
        self.columns(self.h, h_toks, 2, rope_into(qT, "q"))
        self.columns(self.h, h_toks, 2, rope_into(kv, "kv"))
        i, w, tok = self.slot()
        v_done = []
        self.pe.wait(tok)
        for q in range(TT):
            ps, b, fr = self.half()
            self.pe.wait(fr)
            for c in range(C):
                a = (ps, self.h[:, c, q * P:(q + 1) * P], w[:, c * FB:(c + 1) * FB], c == 0, c == C - 1)
                end = self.mm_end(*a) if c == C - 1 else self.mm(*a)
            v_done.append(self.copy(self.act, v_tok[:, q, :], ps, end))
            self.read_by(b, v_done[-1])
        self.slot_read(i, end)
        n_cmp = 15
        hid = sb("cmp_hidden", [64, 2, 2, n_cmp])
        bias = sb("cmp_bias", [64, 2])
        k_cmp, v_cmp = sb("k_cmp", [P, n_cmp]), sb("v_cmp", [n_cmp, P])
        cmp_tok = []
        for n, (name, chunk) in enumerate((("k", 0), ("v", 1))):
            i, w, tok = self.slot()
            self.pe.wait(tok, rope_tok["kv", chunk], self.inputs)
            parts = []
            for g in range(2):
                base = slice(g * 64, g * 64 + 64)
                ps, b, fr = self.half()
                self.pe.wait(fr)
                for l in range(32):
                    if g == 0:
                        self.mm(ps[0:64, 32:33], w[base, l * 64:(l + 1) * 64], self.par(f"cmp_pe_{name}", l, 1, 64), l == 0, l == 31)
                for l in range(32):
                    a = (ps[0:64, 0:n_cmp], w[base, l * 64:(l + 1) * 64], kv[base, chunk, l:l + 16 * (n_cmp - 1) + 1:16], l == 0, l == 31)
                    end = self.mm_end(*a) if l == 31 else self.mm(*a)
                parts.append((ps, b, end))
            self.slot_read(i, end)
            for g, (ps, b, end) in enumerate(parts):
                if g == 0:
                    t = tb = self.copy(self.dve, bias[:, n:n + 1], ps[0:64, 32:33], end)
                t = self.func(hid[:, n, g, :], ps[0:64, 0:n_cmp], ACT.Silu, end, tb, bias=bias[:, n:n + 1])
                self.read_by(b, t)
            ps, b, fr = self.half()
            self.pe.wait(fr, t)
            w2 = self.par(f"cmp_w2_{name}", rows=64)
            for g in range(2):
                if n == 0:
                    end = self.mm_end(ps[g * 64:g * 64 + 64, 0:n_cmp], w2, hid[:, n, g, :], True, True)
                else:
                    end = self.mm_end(ps[0:n_cmp, g * 64:g * 64 + 64], hid[:, n, g, :], w2, True, True)
            t = self.copy(self.dve, k_cmp[:, :] if n == 0 else v_cmp[:, :], ps[:, 0:n_cmp] if n == 0 else ps[0:n_cmp, 0:P], end)
            self.read_by(b, t)
            cmp_tok.append(t)
        all_rope = [rope_tok["q", c] for c in range(4)] + [rope_tok["kv", 2], rope_tok["kv", 3]]
        scale = 64.0 ** -0.5
        p_buf = sb("probs", [P, 2, 2, T])
        pT = sb("probs_T", [P, 2, 4, P])
        stat = sb("softmax_stats", [P, 2, 8])
        pc, pcT, cs = sb("cmp_probs", [P, 8, n_cmp]), sb("cmp_probs_T", [n_cmp, 8, P]), sb("cmp_stats", [P, 3, 8])
        p_free, pT_free, pc_free, pcT_free = [None] * 2, [None] * 2, None, None
        out_free = None
        for q in range(TT):
            tq = slice(q * P, (q + 1) * P)
            nk = (q + 1) * P
            t = None
            for half in range(2):
                ps, b, fr = self.half()
                self.pe.wait(fr, all_rope, cmp_tok)
                base = slice(half * 64, half * 64 + 64)
                for j in range(4):
                    end = self.mm_end(ps[:, j * 16:j * 16 + n_cmp], qT[base, j, tq], k_cmp[base, :], True, True)
                add = self.par(f"cmp_add{q}").rearrange("p (h c) -> p h c", h=8)[:, 0:4, :]
                t = self.tt(self.dve, pc[:, half * 4:half * 4 + 4, :], ps[:, 0:64].rearrange("p (h c) -> p h c", h=4)[:, :, 0:n_cmp],
                            add, ALU.add, end, pc_free)
                self.read_by(b, t)
            mx, sm, sc = cs[:, 0, :], cs[:, 1, :], cs[:, 2, :]
            bc = lambda a: a.unsqueeze(2).to_broadcast([P, 8, n_cmp])
            t = self.reduce(mx, pc[:, :, :], ALU.max, t)
            t = self.tt(self.dve, pc[:, :, :], pc[:, :, :], bc(mx), ALU.subtract, t)
            t = self.func(pc[:, :, :], pc[:, :, :], ACT.Exp, t, scale=scale)
            t = self.tt(self.dve, pc[:, :, :], pc[:, :, :], self.par(f"cmp_keep{q}").rearrange("p (h c) -> p h c", h=8), ALU.mult, t)
            t = self.reduce(sm, pc[:, :, :], ALU.add, t)
            t = self.ts(self.dve, sm, sm, 1e-30, None, ALU.max, None, t)
            t = self.dve.do(lambda e: e.reciprocal(sc, sm), t)
            t = self.tt(self.dve, sc, sc, small[:, q, 0:24:3], ALU.mult, t)
            t = self.tt(self.dve, pc[:, :, :], pc[:, :, :], bc(sc), ALU.mult, t)
            for n in range(2):
                ps, b, fr = self.full()
                self.pe.wait(fr, t)
                for m in range(4):
                    end = self.transposed(ps[0:n_cmp, m * P:(m + 1) * P], pc[:, 4 * n + m, :], last=m == 3)
                tc = self.copy(self.act, pcT[:, 4 * n:4 * n + 4, :], ps[0:n_cmp, :].rearrange("c (m t) -> c m t", m=4), end, pcT_free)
                self.read_by(b, tc)
            pc_free = end
            o_bank = q
            self.pe.wait(self.free.get(o_bank), out_free)
            for h in range(8):
                j, half, n = h % 4, h // 4, h % 2
                base = slice(half * 64, half * 64 + 64)
                ps, b, fr = self.full()
                self.pe.wait(fr)
                for m in range(2):
                    end = self.mm_end(ps[:, m * T:m * T + nk], qT[base, j, tq], kv[base, 2 + m, 0:nk], True, True)
                view = ps[:, :].rearrange("p (m k) -> p m k", m=2)[:, :, 0:nk]
                pb, s = p_buf[:, n, :, 0:nk], stat[:, n, :]
                mask = self.par(f"causal{q}", 0, nk).unsqueeze(1).to_broadcast([P, 2, nk])
                t = self.tt(self.dve, pb, view, mask, ALU.add, end, p_free[n])
                self.read_by(b, t)
                t = self.reduce(s[:, 0:2], pb, ALU.max, t)
                t = self.ts(self.dve, s[:, 0:2], s[:, 0:2], -scale, None, ALU.mult, None, t)
                for m in range(2):
                    te = self.func(p_buf[:, n, m, 0:nk], p_buf[:, n, m, 0:nk], ACT.Exp, t, scale=scale, bias=s[:, m:m + 1], accum=s[:, 2 + m:3 + m])
                t = self.dve.do(lambda e, s=s: e.reciprocal(s[:, 4:6], s[:, 2:4]), te)
                t = self.tt(self.dve, s[:, 4:6], s[:, 4:6], small[:, q, 3 * h + 1:3 * h + 3], ALU.mult, t)
                t = self.tt(self.dve, pb, pb, s[:, 4:6].unsqueeze(2).to_broadcast([P, 2, nk]), ALU.mult, t)
                ps, b, fr = self.full()
                self.pe.wait(fr, t)
                pairs = [(m, kt) for m in range(2) for kt in range(q + 1)]
                for x, (m, kt) in enumerate(pairs):
                    end = self.transposed(ps[:, x * P:(x + 1) * P], p_buf[:, n, m, kt * P:(kt + 1) * P], last=x == len(pairs) - 1)
                p_free[n] = end
                w = len(pairs) * P
                t = self.copy(self.act, pT[:, n, 0:len(pairs), :], ps[:, 0:w].rearrange("p (x t) -> p x t", t=P), end, pT_free[n])
                self.read_by(b, t)
                o = self.bank[o_bank][base, j * P:(j + 1) * P]
                self.pe.wait(tc, t, v_done)
                self.mm(o, v_cmp[:, half * 64:half * 64 + 64], pcT[:, half * 4 + j, :], True, False)
                for x, (m, kt) in enumerate(pairs):
                    a = (o, v_tok[:, kt, m * P + half * 64:m * P + half * 64 + 64], pT[:, n, x, :], False, x == len(pairs) - 1)
                    end = self.mm_end(*a) if x == len(pairs) - 1 else self.mm(*a)
                pT_free[n] = end
            pcT_free = end
            t = self.copy(self.dve, mix[:, 0:4, tq], self.bank[o_bank][:, :].rearrange("p (j t) -> p j t", j=4), end)
            self.read_by(o_bank, t)
        st.close()

    def ssd(self, mix, small, xbc, silu_z):
        st = ExitStack()
        sb = lambda n, s: st.enter_context(self.nc.sbuf_tensor(f"{n}_{self.stage_no}", s, F32))
        H, N4 = 16, 4
        dt, dA, acs, tmp = small[:, :, 24:40], sb("dA", [P, TT, H]), sb("a_cumsum", [P, TT, H]), sb("dt_tmp", [P, TT, H])
        t = self.softplus(dt, tmp[:, :, :], None)
        tmp2 = sb("a_rate", [P, H])
        ta = self.func(tmp2[:, :], self.par("a_log"), ACT.Exp, self.inputs)
        for q in range(TT):
            t = self.stt(dA[:, q, :], tmp2[:, :], -1.0, small[:, q, 24:40], ALU.mult, ALU.mult, t, ta)
        ps, b, fr = self.half()
        self.pe.wait(fr, t)
        for q in range(TT):
            self.mm(ps[:, q * H:(q + 1) * H], self.par("upto"), dA[:, q, :], True, True)
        end = self.mm_end(ps[:, 32:32 + H], self.par("ones"), dA[:, 0, :], True, True)
        t = self.copy(self.dve, acs[:, :, :], ps[:, 0:32].rearrange("p (q h) -> p q h", q=TT), end)
        dec = sb("decay_to_end", [P, H])
        t = self.tt(self.dve, dec[:, :], ps[:, 32:32 + H], acs[:, 0, :], ALU.subtract, t)
        self.read_by(b, t)
        acs_tok = t
        t_dec = self.func(dec[:, :], dec[:, :], ACT.Exp, t)
        xd, xdd, b_tok = sb("x_dt", [P, TT, D]), sb("x_dt_decayed", [P, D]), sb("B_tokens", [P, 2, P])
        xd_tok = []
        for q in range(TT):
            for n in range(2):
                ps, b, fr = self.full()
                self.pe.wait(fr)
                for m in range(4):
                    end = self.transposed(ps[:, m * P:(m + 1) * P], xbc[:, 4 * n + m, q * P:(q + 1) * P], last=m == 3)
                t = self.tt(self.dve, xd[:, q, 512 * n:512 * n + 512].rearrange("p (h d) -> p h d", h=8), ps[:, :].rearrange("p (h d) -> p h d", h=8),
                            small[:, q, 24 + 8 * n:32 + 8 * n].unsqueeze(2).to_broadcast([P, 8, 64]), ALU.mult, end, acs_tok)
                self.read_by(b, t)
                xd_tok.append(t)
        t_xdd = self.tt(self.dve, xdd[:, :].rearrange("p (h d) -> p h d", h=H), xd[:, 0, :].rearrange("p (h d) -> p h d", h=H),
                        dec[:, :].unsqueeze(2).to_broadcast([P, H, 64]), ALU.mult, xd_tok, t_dec)
        ps, b, fr = self.half()
        self.pe.wait(fr)
        for g in range(2):
            end = self.transposed(ps[:, g * P:(g + 1) * P], xbc[:, 8 + g, 0:P], last=True)
        t_b = self.copy(self.act, b_tok[:, :, :], ps.rearrange("p (g n) -> p g n", g=2), end)
        self.read_by(b, t_b)
        state = sb("state_T", [P, 2, 512])
        for g in range(2):
            ps, b, fr = self.full()
            self.pe.wait(fr, t_b, t_xdd)
            end = self.mm_end(ps[:, :], b_tok[:, g, :], xdd[:, g * 512:(g + 1) * 512], True, True)
            t_state = self.copy(self.act, state[:, g, :], ps[:, :], end)
            self.read_by(b, t_state)
        cb, seg, grow = sb("CB_T", [P, P]), sb("seg_T", [P, 2, N4, P]), sb("C_grown", [P, 2, N4, P])
        cb_free, seg_free, grow_free, n_seg = None, [None] * 2, [None] * 2, 0
        y_tok = []
        for q in range(TT):
            tq = slice(q * P, (q + 1) * P)
            for g in range(2):
                ps, b, fr = self.half()
                self.pe.wait(fr)
                end = self.mm_end(ps[:, 0:P], xbc[:, 8 + g, tq], xbc[:, 10 + g, tq], True, True)
                t_cb = self.tt(self.dve, cb[:, :], ps[:, 0:P], self.par("upto"), ALU.mult, end, cb_free)
                self.read_by(b, t_cb)
                for r4 in range(2):
                    h0, s = 8 * g + 4 * r4, n_seg % 2
                    n_seg += 1
                    ps, b, fr = self.full()
                    self.pe.wait(fr, acs_tok)
                    for m in range(N4):
                        end = self.mm_end(ps[:, m * P:(m + 1) * P], dA[:, q, h0 + m:h0 + m + 1].to_broadcast([P, P]), self.par("upto"), True, True)
                    v = ps[:, :].rearrange("p (m t) -> p m t", m=N4)
                    t = self.tt(self.dve, seg[:, s, :, :], v, acs[:, q, h0:h0 + N4].unsqueeze(2).to_broadcast([P, N4, P]), ALU.subtract, end, seg_free[s], acs_tok)
                    if q > 0:
                        t_g = self.func(grow[:, s, :, :], v, ACT.Exp, end, t, grow_free[s])
                        self.read_by(b, t_g)
                        t_g = self.tt(self.dve, grow[:, s, :, :], grow[:, s, :, :], xbc[:, 10 + g, tq].unsqueeze(1).to_broadcast([P, N4, P]), ALU.mult, t_g)
                    else:
                        t_g = None
                        self.read_by(b, t)
                    t = self.ts(self.pool, seg[:, s, :, :], seg[:, s, :, :], 0.0, None, ALU.min, None, t)
                    t = self.func(seg[:, s, :, :], seg[:, s, :, :], ACT.Exp, t)
                    t = self.tt(self.dve, seg[:, s, :, :], seg[:, s, :, :], cb[:, :].unsqueeze(1).to_broadcast([P, N4, P]), ALU.mult, t, t_cb)
                    cb_free = t
                    yb, b, fr = self.half()
                    self.pe.wait(fr, t, t_g, t_state if q else None, xd_tok)
                    for m in range(N4):
                        h = h0 + m
                        o = yb[(h % 2) * 64:(h % 2) * 64 + 64, (m // 2) * P:(m // 2 + 1) * P]
                        if q:
                            self.mm(o, xd[:, q, h * 64:(h + 1) * 64], seg[:, s, m, :], True, False)
                            end = self.mm_end(o, state[:, g, (h % 8) * 64:(h % 8 + 1) * 64], grow[:, s, m, :], False, True)
                        else:
                            end = self.mm_end(o, xd[:, q, h * 64:(h + 1) * 64], seg[:, s, m, :], True, True)
                    seg_free[s] = grow_free[s] = end
                    for k in range(2):
                        c = h0 // 2 + k
                        t = self.stt(mix[:, 4 + c, tq], xbc[:, c, tq], self.par("d_skip")[:, c:c + 1], yb[:, k * P:(k + 1) * P], ALU.mult, ALU.add, end)
                    self.read_by(b, t)
        sq = self.y
        sq_tok = []
        for c in range(C):
            t1 = self.tt(self.dve, mix[:, 4 + c, :], mix[:, 4 + c, :], silu_z[:, c, :], ALU.mult, t)
            sq_tok.append(self.func(sq[:, c, :], mix[:, 4 + c, :], ACT.Square, t1, self.y_free))
        for g in range(2):
            r = self.inv_rms([sq[:, 4 * g + c, :] for c in range(4)], 512, 1e-5, sq_tok[4 * g:4 * g + 4], out=self.rms[:, g, :])
            for c in range(4 * g, 4 * g + 4):
                t = self.stt(mix[:, 4 + c, :], mix[:, 4 + c, :], self.par("ssd_norm")[:, c:c + 1], self.rms[:, g, :], ALU.mult, ALU.mult, r)
        self.y_free = (self.pe.sem, self.pe.count)
        self.rms_free = t
        self.barrier()
        st.close()

    def invert(self, buf, nt, tok, levels):
        t_, tt, x, nl = buf["t"], buf["tt"], buf["x"], buf["nl"]
        four = lambda a: a.unsqueeze(1).to_broadcast([P, 4, P])
        as4 = lambda ps: ps[:, :].rearrange("p (m t) -> p m t", m=4)
        k = self.tt(self.dve, nl[:, :, :], nt, four(self.par("level1")), ALU.mult, tok, buf["nl_free"])
        t_tt = self.tt(self.dve, tt[:, :, :], four(self.par("ident")), nl[:, :, :], ALU.subtract, k, buf["tt_free"])
        ps, b, fr = self.full()
        self.pe.wait(fr, t_tt)
        for m in range(4):
            end = self.transposed(ps[:, m * P:(m + 1) * P], tt[:, m, :], last=m == 3)
        t_t = self.copy(self.act, t_[:, :, :], as4(ps), end, buf["x_free"])
        self.read_by(b, t_t)
        x_free, nl_free = buf["x_free"], t_tt
        for l in levels[1:]:
            t_nl = self.tt(self.pool, nl[:, :, :], nt, four(self.par(f"level{l}")), ALU.mult, nl_free, tok)
            yield
            ps, b, fr = self.full()
            self.pe.wait(fr, t_nl, t_t)
            for m in range(4):
                a = (ps[:, m * P:(m + 1) * P], nl[:, m, :], t_[:, m, :], True, True)
                end = self.mm_end(*a) if m == 3 else self.mm(*a)
            nl_free = end
            t_x = self.copy(self.act, x[:, :, :], as4(ps), end, x_free)
            self.read_by(b, t_x)
            yield
            last = l == levels[-1]
            ps, b, fr = self.full()
            self.pe.wait(fr, t_x, t_tt)
            for m in range(4):
                a = (ps[:, m * P:(m + 1) * P], x[:, m, :], tt[:, m, :], True, True)
                end = self.mm_end(*a) if m == 3 else self.mm(*a)
            if not last:
                ps2, b2, fr = self.full()
                self.pe.wait(fr)
                for m in range(4):
                    a = (ps2[:, m * P:(m + 1) * P], tt[:, m, :], x[:, m, :], True, True)
                    end2 = self.mm_end(*a) if m == 3 else self.mm(*a)
                t_t = self.tt(self.dve, t_[:, :, :], t_[:, :, :], as4(ps2), ALU.subtract, end2, t_t)
                self.read_by(b2, t_t)
                end = end2
            t_tt = self.tt(self.dve, tt[:, :, :], tt[:, :, :], as4(ps), ALU.subtract, end)
            self.read_by(b, t_tt)
            x_free = end
        buf["x_free"] = buf["nl_free"] = (self.pe.sem, self.pe.count)
        buf["done"] = t_tt

    def interleave(self, *generators):
        left = list(generators)
        while left:
            self.background()
            for g in list(left):
                if next(g, True):
                    left.remove(g)

    def rwkv_mixer(self):
        st, sb = self.stage()
        h_toks = self.norm_x(self.par("a1_gain2"))
        r, k, v, sg, a, g = (sb(n, [P, C, T]) for n in ("r", "k", "v", "decay", "a", "g"))
        pend = sb("chunk_decay", [P, C, 4])
        inner = ExitStack()
        isb = lambda n, s: inner.enter_context(self.nc.sbuf_tensor(f"{n}_{self.stage_no}", s, F32))
        xx, m0, m1 = isb("x_shifted", [P, C, T]), isb("mixed0", [P, C, T]), isb("mixed1", [P, C, T])
        hw = isb("lora_hidden", [P, 4, T])
        h, y = self.h, self.y
        t = self.tt(self.dve, xx[:, :, 1:], h[:, :, 0:T - 1], h[:, :, 1:], ALU.subtract, h_toks)
        t = self.ts(self.dve, xx[:, :, 0:1], h[:, :, 0:1], -1.0, None, ALU.mult, None, t)
        mixed, m_free = [m0, m1], [None, None]
        turn = [0]

        def mix(n):
            i = turn[0] % 2
            turn[0] += 1
            toks = [self.stt(mixed[i][:, c, :], xx[:, c, :], self.par(f"mu{n}")[:, c:c + 1], h[:, c, :], ALU.mult, ALU.add, t, m_free[i])
                    for c in range(C)]
            return i, mixed[i], toks

        s1, w1, tok1 = self.slot()
        s2, g1, tok2 = self.slot()
        hid_tok = []
        for n, (mu, w, tok, lo, m, fn) in enumerate(((1, w1, tok1, 0, 64, ACT.Tanh), (4, w1, tok1, 64, 64, ACT.Copy),
                                                     (5, g1, tok2, 0, 128, ACT.Sigmoid), (5, g1, tok2, 128, 32, ACT.Sigmoid))):
            if n < 3:
                i, src, toks = mix(mu)
            ps, b, fr = self.half()
            self.pe.wait(fr, tok, toks)
            for c in range(C):
                args = (ps[0:m, :], w[:, c * FB + lo:c * FB + lo + m], src[:, c, :], c == 0, c == C - 1)
                end = self.mm_end(*args) if c == C - 1 else self.mm(*args)
            m_free[i] = end
            hid_tok.append(self.func(hw[0:m, n, :], ps[0:m, :], fn, end))
            self.read_by(b, hid_tok[-1])
            if n in (1, 3):
                self.slot_read(s1 if n == 1 else s2, end)
        for n, (dst, bias) in enumerate(((sg, "w0"), (a, "a0"))):
            if n == 0:
                s1, w, tok = self.slot()
            for c in range(C):
                ps, b, fr = self.half()
                self.pe.wait(fr, tok, hid_tok[n])
                end = self.mm_end(ps, w[0:64, n * D + c * P:n * D + (c + 1) * P], hw[0:64, n, :], True, True)
                t2 = self.func(dst[:, c, :], ps, ACT.Sigmoid, end, bias=self.par(bias)[:, c:c + 1])
                self.read_by(b, t2)
        self.slot_read(s1, end)
        s1, w, tok = self.slot()
        for c in range(C):
            ps, b, fr = self.half()
            self.pe.wait(fr, tok, hid_tok[2], hid_tok[3])
            self.mm(ps, w[:, c * P:(c + 1) * P], hw[:, 2, :], True, False)
            end = self.mm_end(ps, w[0:32, D + c * P:D + (c + 1) * P], hw[0:32, 3, :], False, True)
            t2 = self.copy(self.act, g[:, c, :], ps, end)
            self.read_by(b, t2)
        self.slot_read(s1, end)
        for mu, dst in ((0, r), (2, k), (3, v)):
            i, src, toks = mix(mu)

            def consume(c, ps, end, dst=dst):
                return self.copy(self.act, dst[:, c, :], ps, end)
            self.columns(src, toks, 4, consume)
            m_free[i] = (self.pe.sem, self.pe.count)
        self.barrier()
        kappa = float(np.exp(-0.5))
        gs, kk, t3, t4 = m0, m1, xx, y
        for c in range(C):
            t_gs = self.dve.do(lambda e, c=c: e.tensor_tensor_scan(gs[:, c, :], self.par("not_first64"), sg[:, c, :], 0.0, ALU.mult, ALU.add))
            t_kk = self.ts(self.dve, kk[:, c, :], k[:, c, :], self.par("k_k")[:, c:c + 1], None, ALU.mult, None)
        al = lambda x: x[:, :, :]
        t = self.tt(self.pool, al(t4), al(gs), al(sg), ALU.subtract, t_gs)
        t_pprev = self.func(al(t4), al(t4), ACT.Exp, t, scale=-kappa)
        t = self.func(al(t3), al(kk), ACT.Square, t_kk)

        def head_sums(src, tok, use):
            out = []
            for n in range(4):
                ps, b, fr = self.full()
                self.pe.wait(fr, tok)
                end = self.mm_end(ps[:, :], self.par("half_ones"), src[:, 2 * n:2 * n + 2, :], True, True)
                t = use(n, ps[:, :].rearrange("p (c t) -> p c t", c=2), end)
                self.read_by(b, t)
                out.append(t)
            return out
        t = head_sums(t3, t, lambda n, ps, end: self.ts(self.dve, t3[:, 2 * n:2 * n + 2, :], ps, 1e-24, None, ALU.max, None, end))
        t = self.func(al(t3), al(t3), ACT.Ln, t, scale=65536.0)
        t = self.func(al(t3), al(t3), ACT.Exp, t, scale=-0.5)
        t_kk = self.stt(al(kk), al(kk), 256.0, al(t3), ALU.mult, ALU.mult, t, t_kk)
        t_A = self.stt(al(sg), al(kk), -1.0, al(t4), ALU.mult, ALU.mult, t_kk, t_pprev)
        one_less = isb("one_less_ka", [P, C])
        t = self.ts(self.dve, one_less[:, :], self.par("k_a"), -1.0, 1.0, ALU.mult, ALU.add)
        for c in range(C):
            t1 = self.ts(self.dve, t3[:, c, :], a[:, c, :], self.par("k_a")[:, c:c + 1], one_less[:, c:c + 1], ALU.mult, ALU.add, t, t_kk)
        t_k = self.tt(self.dve, al(k), al(k), al(t3), ALU.mult, t1)
        t_b = self.tt(self.pool, al(a), al(kk), al(a), ALU.mult, t1, t_kk)
        t = self.tt(self.dve, al(t3), al(r), al(k), ALU.mult, t_k)
        for c in range(C):
            t1 = self.ts(self.dve, t3[:, c, :], t3[:, c, :], self.par("r_k")[:, c:c + 1], None, ALU.mult, None, t)
        t_bonus = head_sums(t3, t1, lambda n, ps, end: self.tt(self.dve, h[:, 2 * n:2 * n + 2, :], v[:, 2 * n:2 * n + 2, :], ps, ALU.mult, end))
        t = self.func(al(t4), al(gs), ACT.Exp, t_A, scale=kappa)
        t_B = self.tt(self.pool, al(a), al(a), al(t4), ALU.mult, t, t_b)
        t_K = self.tt(self.dve, al(k), al(k), al(t4), ALU.mult, t, t_bonus)
        t = self.func(al(t3), al(gs), ACT.Exp, t_bonus, t_K, scale=-kappa)
        t_R = self.tt(self.dve, al(r), al(r), al(t3), ALU.mult, t)
        self.copy(self.dve, pend[:, :, :], t3[:, :, 63:T:64], t)
        self.barrier()
        inner.close()
        A, B, K, R = sg, a, k, r
        self.filler = self.both_modulations()
        inner = ExitStack()
        isb = lambda n, s: inner.enter_context(self.nc.sbuf_tensor(f"{n}_{self.stage_no}", s, F32))
        tokT = {n: isb(f"{n}_tokens", [P, 4, P]) for n in "BKV"}
        bufs = []
        for par in range(2):
            bufs.append({n: isb(f"{n}{par}", [P, 4, P]) for n in ("nt", "rb", "rk", "t", "tt", "x", "nl")})
            bufs[par].update(x_free=None, nl_free=None, tt_free=None)
        lv, S = isb("LakV", [P, 4, P]), [isb(f"state{i}", [P, 4, P]) for i in range(2)]
        U = isb("U", [P, 4, P])
        W, Stmp = bufs[0]["x"], bufs[1]["x"]
        as4 = lambda ps: ps[:, :].rearrange("p (m t) -> p m t", m=4)
        four = lambda m: m.unsqueeze(1).to_broadcast([P, 4, P])
        for sg_ in range(2):
            ch = lambda m: 4 * sg_ + m
            for q in range(TT):
                tq = slice(q * P, (q + 1) * P)
                self.barrier()
                for n, src in (("B", B), ("K", K), ("V", v)):
                    ps, b, fr = self.full()
                    self.pe.wait(fr)
                    for m in range(4):
                        end = self.transposed(ps[:, m * P:(m + 1) * P], src[:, ch(m), tq], last=m == 3)
                    t_tok = self.copy(self.act, tokT[n][:, :, :], as4(ps), end)
                    self.read_by(b, t_tok)
                lak_tok = []
                for par in range(2):
                    bf, base = bufs[par], slice(par * 64, par * 64 + 64)
                    for dst, L, Rh, mask, sign in (("nt", B, A, "before64", -1.0), ("nl", K, A, "before64", 1.0),
                                                   ("rb", B, R, "upto64", 1.0), ("rk", K, R, "upto64", 1.0)):
                        ps, b, fr = self.full()
                        self.pe.wait(fr)
                        for m in range(4):
                            end = self.mm_end(ps[:, m * P:(m + 1) * P], L[base, ch(m), tq], Rh[base, ch(m), tq], True, True)
                        t = self.stt(bf[dst][:, :, :], as4(ps), sign, four(self.par(mask)), ALU.mult, ALU.mult, end)
                        self.read_by(b, t)
                        if dst == "nt":
                            bf["nt_tok"] = t
                        if dst == "nl":
                            lak_tok.append(t)
                ps, b, fr = self.full()
                self.pe.wait(fr, lak_tok, t_tok)
                for m in range(4):
                    for par in range(2):
                        o = slice(m * P + par * 64, m * P + par * 64 + 64)
                        end = self.mm_end(ps[:, o], bufs[par]["nl"][:, m, :], tokT["V"][:, m, par * 64:par * 64 + 64], True, True)
                t_lv = self.copy(self.act, lv[:, :, :], as4(ps), end)
                self.read_by(b, t_lv)
                for bf in bufs:
                    bf["nl_free"] = end
                    bf["x_free"] = bf["tt_free"] = None
                self.interleave(*(self.invert(bf, bf["nt"][:, :, :], bf["nt_tok"], (1, 2, 4, 8, 16, 32)) for bf in bufs))
                inv = [bf["done"] for bf in bufs] + [bufs[0]["x_free"], bufs[1]["x_free"]]
                for j in (2 * q, 2 * q + 1):
                    self.background(2)
                    rows = slice((j % 2) * 64, (j % 2) * 64 + 64)
                    s_now, s_next = S[j % 2], S[(j + 1) % 2]
                    if j == 0:
                        w_src, t_w = lv, t_lv
                    else:
                        ps, b, fr = self.full()
                        self.pe.wait(fr, t_s, inv)
                        for m in range(4):
                            end = self.mm_end(ps[:, m * P:(m + 1) * P], A[:, ch(m), tq], s_now[:, m, :], True, True)
                        w_src = W
                        t_w = self.tt(self.dve, W[:, :, :], lv[:, :, :], as4(ps), ALU.add, end, inv, t_lv)
                        self.read_by(b, t_w)
                    ps, b, fr = self.full()
                    self.pe.wait(fr, t_w, inv)
                    for m in range(4):
                        for par in range(2):
                            o = slice(par * 64, par * 64 + 64)
                            end = self.mm_end(ps[:, m * P + par * 64:m * P + par * 64 + 64], bufs[par]["tt"][:, m, :], w_src[:, m, o], True, True)
                    t_u = self.copy(self.act, U[rows, :, :], as4(ps)[rows], end)
                    self.read_by(b, t_u)
                    if j < 3:
                        ps, b, fr = self.full()
                        self.pe.wait(fr, t_u)
                        for m in range(4):
                            o = ps[:, m * P:(m + 1) * P]
                            self.mm(o, tokT["B"][rows, m, :], U[rows, m, :], True, False)
                            end = self.mm_end(o, tokT["K"][rows, m, :], tokT["V"][rows, m, :], False, True)
                        t = self.tt(self.dve, Stmp[:, :, :], as4(ps), four(self.par("half_ones")), ALU.mult, end, inv)
                        self.read_by(b, t)
                        if j > 0:
                            t = self.tt(self.dve, Stmp[:, :, :], Stmp[:, :, :], s_now[:, :, :], ALU.add, t, t_s)
                        t_new = (t, j)
                    if j % 2:
                        ps, b, fr = self.full()
                        self.pe.wait(fr, t_u)
                        for m in range(4):
                            o = ps[:, m * P:(m + 1) * P]
                            first = True
                            for i in (2 * q, j):
                                if i:
                                    cols = slice((i % 2) * 64, (i % 2) * 64 + 64)
                                    self.mm(o[:, cols], S[i % 2][:, m, :], R[:, ch(m), q * P + cols.start:q * P + cols.stop], first, False, True)
                                    first = False
                            for par in range(2):
                                f = slice(par * 64, par * 64 + 64)
                                self.mm(o[f], U[:, m, f], bufs[par]["rb"][:, m, :], False, False, True)
                                end = self.mm_end(o[f], tokT["V"][:, m, f], bufs[par]["rk"][:, m, :], False, par == 1, True)
                        t_y = self.copy(self.act, y[:, 4 * sg_:4 * sg_ + 4, tq], as4(ps), end)
                        self.read_by(b, t_y)
                    if j < 3:
                        t_s = self.tt(self.dve, s_next[:, :, :], Stmp[:, :, :],
                                      pend[:, 4 * sg_:4 * sg_ + 4, j:j + 1].to_broadcast([P, 4, P]), ALU.mult, t_new[0],
                                      (self.pe.sem, self.pe.count))
        self.background(99)
        self.barrier()
        inner.close()
        d, sq = A, B
        head_sums_w = lambda src, tok, use: head_sums(src, tok, use)
        t = head_sums_w(y, None, lambda n, ps, end: self.stt(d[:, 2 * n:2 * n + 2, :], ps, -1.0 / 64, y[:, 2 * n:2 * n + 2, :], ALU.mult, ALU.add, end))
        t2 = self.func(al(sq), al(d), ACT.Square, t)
        t2 = head_sums_w(sq, t2, lambda n, ps, end: self.ts(self.dve, sq[:, 2 * n:2 * n + 2, :], ps, 1.0 / 64, 64e-5, ALU.mult, ALU.add, end))
        t2 = self.func(al(sq), al(sq), ACT.Ln, t2)
        t2 = self.func(al(sq), al(sq), ACT.Exp, t2, scale=-0.5)
        t = self.tt(self.dve, al(d), al(d), al(sq), ALU.mult, t2)
        toks = []
        for c in range(C):
            t1 = self.ts(self.dve, d[:, c, :], d[:, c, :], self.par("ln_g")[:, c:c + 1], self.par("ln_b")[:, c:c + 1], ALU.mult, ALU.add, t)
            t1 = self.tt(self.pool, d[:, c, :], d[:, c, :], h[:, c, :], ALU.add, t1)
            toks.append(self.tt(self.dve, d[:, c, :], d[:, c, :], g[:, c, :], ALU.mult, t1))
        self.h_free = self.y_free = toks[-1]
        self.add_back(self.project_columns_out(d, toks), self.par("a1_gain3"), 1.0)
        st.close()

    def delta_mixer(self):
        i, H, K = 1, 8, 4
        st, sb = self.stage()
        part = lambda n: self.mod[i][:, n * C:(n + 1) * C]
        h_toks = self.norm_x(self.gain[:, i, 0, :], part(0), self.mod_tok)
        q_T, k_T, v_T, z = (sb(n, [P, C, T]) for n in ("q", "k", "v", "silu_z"))
        ba = sb("beta_g", [P, TT, 16])
        inner = ExitStack()
        isb = lambda n, s: inner.enter_context(self.nc.sbuf_tensor(f"{n}_{self.stage_no}", s, F32))
        raw, taps = isb("qkv_raw", [P, 2, K - 1 + T]), isb("qkv_taps", [P, 2, T])
        z0 = self.pool.do(lambda e: e.memset(raw[:, :, 0:K - 1], 0.0))
        raw_free, taps_free = [None] * 2, [None] * 2

        def conv_in(c, ps, end):
            n = c % 2
            dst = (q_T, k_T, v_T)[c // C][:, c % C, :]
            t = self.copy(self.act, raw[:, n, K - 1:], ps, end, raw_free[n])
            v = self.conv_chunk(taps[:, n, :], raw[:, n, :], "gdn_conv", None, c, K, [t, z0], taps_free[n])
            raw_free[n] = v
            taps_free[n] = self.func(dst, taps[:, n, :], ACT.Silu, v)
            return t
        self.columns(self.h, h_toks, 12, conv_in)
        self.columns(self.h, h_toks, 4, lambda c, ps, end: self.func(z[:, c, :], ps, ACT.Silu, end))
        for q in range(TT):
            ps, b, fr = self.half()
            self.pe.wait(fr, self.inputs)
            for c in range(C):
                a = (ps[:, 0:16], self.h[:, c, q * P:(q + 1) * P], self.par("w_ba", c * 16, 16), c == 0, c == C - 1)
                end = self.mm_end(*a) if c == C - 1 else self.mm(*a)
            t = self.func(ba[:, q, 0:8], ps[:, 0:8], ACT.Sigmoid, end)
            t = self.tt(self.dve, ba[:, q, 8:16], ps[:, 8:16], self.par("gdn_dt_bias"), ALU.add, end, t)
            self.read_by(b, t)
        self.barrier()
        inner.close()
        tmp = sb("g_tmp", [P, TT, H])
        rate = sb("g_rate", [P, H])
        t = self.softplus(ba[:, :, 8:16], tmp[:, :, :], None)
        ta = self.func(rate[:, :], self.par("gdn_a_log"), ACT.Exp, t)
        for q in range(TT):
            t = self.stt(ba[:, q, 8:16], rate[:, :], -1.0, ba[:, q, 8:16], ALU.mult, ALU.mult, t, ta)
        gc, kdec = sb("g_cumsum", [P, TT, H]), sb("decay_to_end", [P, H])
        ps, b, fr = self.half()
        self.pe.wait(fr, t)
        for q in range(TT):
            self.mm(ps[:, q * H:(q + 1) * H], self.par("upto"), ba[:, q, 8:16], True, True)
        end = self.mm_end(ps[:, 16:24], self.par("ones"), ba[:, 0, 8:16], True, True)
        t = self.copy(self.dve, gc[:, :, :], ps[:, 0:16].rearrange("p (q h) -> p q h", q=TT), end)
        t = self.tt(self.dve, kdec[:, :], ps[:, 16:24], gc[:, 0, :], ALU.subtract, t)
        self.read_by(b, t)
        t_kd = self.func(kdec[:, :], kdec[:, :], ACT.Exp, t)
        sq = self.y
        for dst, s2 in ((q_T, float(P)), (k_T, 1.0)):
            t = self.func(sq[:, :, :], dst[:, :, :], ACT.Square, self.y_free)
            for n in range(4):
                ps, b, fr = self.full()
                self.pe.wait(fr, t)
                end = self.mm_end(ps[:, :], self.par("ones"), sq[:, 2 * n:2 * n + 2, :], True, True)
                t1 = self.ts(self.dve, sq[:, 2 * n:2 * n + 2, :], ps[:, :].rearrange("p (c t) -> p c t", c=2), s2, s2 * NORM_EPS, ALU.mult, ALU.add, end)
                self.read_by(b, t1)
            t1 = self.func(sq[:, :, :], sq[:, :, :], ACT.Ln, t1)
            t1 = self.func(sq[:, :, :], sq[:, :, :], ACT.Exp, t1, scale=-0.5)
            self.y_free = self.tt(self.dve, dst[:, :, :], dst[:, :, :], sq[:, :, :], ALU.mult, t1)
        self.barrier()
        o_T = self.h
        names = ("nt", "attn", "t", "tt", "x", "nl", "dec", "k_tok", "vb", "kg", "qd")
        bufs = [{n: sb(f"{n}{x}", [P, 4, P]) for n in (names[:5] + names[6:10] if x < 0 else names)} for x in range(1)]
        S = sb("state", [P, 4, P])
        bf = bufs[0]
        as4 = lambda ps: ps[:, :].rearrange("p (m t) -> p m t", m=4)
        four = lambda m: m.unsqueeze(1).to_broadcast([P, 4, P])
        col = lambda x: x.unsqueeze(2).to_broadcast([P, 4, P])
        for hg in range(2):
            h0 = 4 * hg
            for q in range(TT):
                tq = slice(q * P, (q + 1) * P)
                self.barrier()
                pg, b, fr = self.full()
                self.pe.wait(fr)
                for m in range(4):
                    end = self.mm_end(pg[:, m * P:(m + 1) * P], ba[:, q, 8 + h0 + m:9 + h0 + m].to_broadcast([P, P]), self.par("upto"), True, True)
                dec = bf["dec"][:, :, :]
                t = self.tt(self.dve, dec, as4(pg), col(gc[:, q, h0:h0 + 4]), ALU.subtract, end)
                t = self.ts(self.dve, dec, dec, 0.0, None, ALU.min, None, t)
                t_dec = self.func(dec, dec, ACT.Exp, t)
                t_kg = self.func(bf["kg"][:, :, :], as4(pg), ACT.Exp, end, t)
                self.read_by(b, t_kg)
                t_qd = self.tt(self.pool, bf["qd"][:, :, :], q_T[:, h0:h0 + 4, tq], bf["kg"][:, :, :], ALU.mult, t_kg)
                t_kg = self.tt(self.pool, bf["kg"][:, :, :], k_T[:, h0:h0 + 4, tq], bf["kg"][:, :, :], ALU.mult, t_qd)
                ps, b, fr = self.full()
                self.pe.wait(fr)
                for m in range(4):
                    end = self.mm_end(ps[:, m * P:(m + 1) * P], k_T[:, h0 + m, tq], k_T[:, h0 + m, tq], True, True)
                t_nt = self.tt(self.dve, bf["nt"][:, :, :], as4(ps), dec, ALU.mult, end, t_dec)
                self.read_by(b, t_nt)
                ps, b, fr = self.full()
                self.pe.wait(fr)
                for m in range(4):
                    end = self.mm_end(ps[:, m * P:(m + 1) * P], ba[:, q, h0 + m:h0 + m + 1].to_broadcast([P, P]), self.par("ident"), True, True)
                t_nt = self.tt(self.dve, bf["nt"][:, :, :], bf["nt"][:, :, :], as4(ps), ALU.mult, end, t_nt)
                self.read_by(b, t_nt)
                t_nt = self.tt(self.pool, bf["nt"][:, :, :], bf["nt"][:, :, :], four(self.par("before")), ALU.mult, t_nt)
                ps, b, fr = self.full()
                self.pe.wait(fr)
                for m in range(4):
                    end = self.mm_end(ps[:, m * P:(m + 1) * P], k_T[:, h0 + m, tq], q_T[:, h0 + m, tq], True, True)
                t_at = self.tt(self.dve, bf["attn"][:, :, :], as4(ps), dec, ALU.mult, end, t_dec)
                self.read_by(b, t_at)
                t_at = self.tt(self.pool, bf["attn"][:, :, :], bf["attn"][:, :, :], four(self.par("upto")), ALU.mult, t_at)
                ps, b, fr = self.full()
                self.pe.wait(fr)
                for m in range(4):
                    end = self.transposed(ps[:, m * P:(m + 1) * P], v_T[:, h0 + m, tq], last=m == 3)
                t_vb = self.tt(self.dve, bf["vb"][:, :, :], as4(ps), col(ba[:, q, h0:h0 + 4]), ALU.mult, end)
                self.read_by(b, t_vb)
                t_kt = None
                if q == 0:
                    ps, b, fr = self.full()
                    self.pe.wait(fr)
                    for m in range(4):
                        end = self.transposed(ps[:, m * P:(m + 1) * P], k_T[:, h0 + m, tq], last=m == 3)
                    t_kt = self.tt(self.dve, bf["k_tok"][:, :, :], as4(ps), col(kdec[:, h0:h0 + 4]), ALU.mult, end, t_kd)
                    self.read_by(b, t_kt)
                bf.update(x_free=None, nl_free=None, tt_free=None)
                self.interleave(self.invert(bf, bf["nt"][:, :, :], t_nt, (1, 2, 4, 8, 16, 32, 64)))
                inv = [bf["done"], bf["x_free"]]
                w = bf["vb"]
                if q:
                    ps, b, fr = self.full()
                    self.pe.wait(fr, t_s, t_kg)
                    for m in range(4):
                        end = self.mm_end(ps[:, m * P:(m + 1) * P], bf["kg"][:, m, :], S[:, m, :], True, True)
                    w = bf["x"]
                    t = self.tt(self.dve, w[:, :, :], as4(ps), col(ba[:, q, h0:h0 + 4]), ALU.mult, end, inv)
                    self.read_by(b, t)
                    t_vb = self.tt(self.dve, w[:, :, :], bf["vb"][:, :, :], w[:, :, :], ALU.subtract, t, t_vb)
                ps, b, fr = self.full()
                self.pe.wait(fr, t_vb, inv)
                for m in range(4):
                    end = self.mm_end(ps[:, m * P:(m + 1) * P], bf["tt"][:, m, :], w[:, m, :], True, True)
                U = bf["nl"]
                t_u = self.copy(self.act, U[:, :, :], as4(ps), end, inv)
                self.read_by(b, t_u)
                ps, b, fr = self.full()
                self.pe.wait(fr, t_u, t_at, t_qd)
                for m in range(4):
                    o = ps[:, m * P:(m + 1) * P]
                    if q:
                        self.mm(o, S[:, m, :], bf["qd"][:, m, :], True, False)
                    end = self.mm_end(o, U[:, m, :], bf["attn"][:, m, :], not q, True)
                t = self.copy(self.dve, o_T[:, h0:h0 + 4, tq], as4(ps), end, self.h_free)
                self.read_by(b, t)
                if q == 0:
                    ps, b, fr = self.full()
                    self.pe.wait(fr, t_u, t_kt)
                    for m in range(4):
                        end = self.mm_end(ps[:, m * P:(m + 1) * P], bf["k_tok"][:, m, :], U[:, m, :], True, True)
                    t_s = self.copy(self.act, S[:, :, :], as4(ps), end)
                    self.read_by(b, t_s)
        self.barrier()
        t = self.func(sq[:, :, :], o_T[:, :, :], ACT.Square)
        for n in range(4):
            ps, b, fr = self.full()
            self.pe.wait(fr, t)
            end = self.mm_end(ps[:, :], self.par("ones"), sq[:, 2 * n:2 * n + 2, :], True, True)
            t1 = self.ts(self.dve, sq[:, 2 * n:2 * n + 2, :], ps[:, :].rearrange("p (c t) -> p c t", c=2), 1.0 / P, NORM_EPS, ALU.mult, ALU.add, end)
            self.read_by(b, t1)
        t1 = self.func(sq[:, :, :], sq[:, :, :], ACT.Ln, t1)
        t1 = self.func(sq[:, :, :], sq[:, :, :], ACT.Exp, t1, scale=-0.5)
        t1 = self.stt(q_T[:, :, :], o_T[:, :, :], self.par("gdn_norm"), sq[:, :, :], ALU.mult, ALU.mult, t1)
        t1 = self.tt(self.dve, q_T[:, :, :], q_T[:, :, :], z[:, :, :], ALU.mult, t1)
        self.h_free = self.y_free = t1
        self.add_back(self.project_columns_out(q_T, [t1] * C), self.gain[:, i, 1, :], 1.0)
        st.close()


def program(nc, x_in, w_in, pack_in, out, n_slots, at, stages=None):
    k = Kernel(nc, x_in, w_in, pack_in, out, n_slots, at)
    if stages is not None and "ada" in stages:
        k.filler = k.both_modulations()
        k.background(99)
    for name, fn in STAGES:
        if stages is None or name in stages:
            fn(k)
    k.finish()


STAGES = [
    ("a0_ffn1", lambda k: k.ffn("a0_gain0", "a0_gain1")),
    ("a0_mix", lambda k: k.nsa_ssd_mixer()),
    ("a0_ffn2", lambda k: k.ffn("a0_gain4", "a0_gain5")),
    ("a1_ffn1", lambda k: k.ffn("a1_gain0", "a1_gain1")),
    ("a1_mix", lambda k: k.rwkv_mixer()),
    ("a1_ffn2", lambda k: k.ffn("a1_gain4", "a1_gain5")),
    ("b0_mix", lambda k: k.conv_mixer(0)),
    ("b0_moe", lambda k: k.moe(0)),
    ("b1_mix", lambda k: k.delta_mixer()),
    ("b1_moe", lambda k: k.moe(1)),
]


def kernel(**inputs):
    from concourse import bacc
    from concourse.bass_utils import run_bass_kernel_spmd

    xT, slots, pk = lay_out(inputs)
    weights = np.stack(slots)
    small = np.concatenate(pk.parts, axis=1)
    nc = bacc.Bacc("TRN2", target_bir_lowering=False, num_devices=1)
    args = []
    arrays = {"x_T": xT, "weight_slots": weights, "small_params": small}
    for name, arr in arrays.items():
        args.append(nc.dram_tensor(name, arr.shape, F32, kind="ExternalInput").ap())
    out = nc.dram_tensor("out_T", xT.shape, F32, kind="ExternalOutput").ap()
    program(nc, *args, out, len(slots), pk.at)
    got = run_bass_kernel_spmd(nc, [arrays], core_ids=[0]).results[0]["out_T"]
    return np.ascontiguousarray(got.transpose(2, 1, 0).reshape(1, T, D))
```

```python
from contextlib import ExitStack

import numpy as np
import concourse.bass as bass
import concourse.mybir as mybir
from concourse.alu_op_type import AluOpType as ALU

F32 = mybir.dt.float32
F32R = mybir.dt.float32r
ACT = mybir.ActivationFunctionType
AX = mybir.AxisListType.X

P = 128
D = 1024
T = 256
C = D // P
TT = T // P
SLOT = 2048
RING = 6
FFN_EXTRA = 2
MOE_EXTRA = 5
CAP = 64
FB = 256
FFN_BLOCKS = 2816 // FB
N_EXP = 64
N_GRP = 8
SHARED_BLOCKS = 512 // FB
NORM_EPS = 1e-6
NEG = -1e30


class Pack:

    def __init__(self):
        self.at, self.parts, self.n = {}, [], 0

    def add(self, name, a):
        a = np.asarray(a)
        full = np.zeros((P, a.shape[1]), np.float32)
        full[:a.shape[0]] = a
        self.at[name] = (self.n, a.shape[1])
        self.parts.append(full)
        self.n += a.shape[1]

    def features(self, name, a):
        self.add(name, np.asarray(a).reshape(-1, P).T)

    def rows(self, name, a):
        a = np.asarray(a).reshape(1, -1)
        self.add(name, np.broadcast_to(a, (P, a.shape[1])))


def columns_slot(w):
    out = np.zeros((P, C, FB), np.float32)
    out[:, :, :w.shape[1]] = w.reshape(C, P, w.shape[1]).transpose(1, 0, 2)
    return out.reshape(P, SLOT)


def rows_slot(w):
    return w.reshape(2, P, D).transpose(1, 0, 2).reshape(P, SLOT)


def shape_constants(pk):
    i = np.arange(P)
    s, t = i[:, None], i[None, :]
    pk.add("ident", (s == t).astype(np.float32))
    pk.add("ones", np.ones((P, P), np.float32))
    pk.add("half_ones", (s // 64 == t // 64).astype(np.float32))
    pk.add("upto", (s <= t).astype(np.float32))
    pk.add("before", (s < t).astype(np.float32))
    same = s // 64 == t // 64
    pk.add("upto64", (same & (s <= t)).astype(np.float32))
    pk.add("before64", (same & (s < t)).astype(np.float32))
    for l in (1, 2, 4, 8, 16, 32, 64):
        pk.add(f"level{l}", ((s // (2 * l) == t // (2 * l)) & (s % (2 * l) < l) & (t % (2 * l) >= l)).astype(np.float32))
    inv = (10000.0 ** (-np.arange(0, 64, 2, dtype=np.float32) / np.float32(64))).astype(np.float32)
    ang = np.arange(T, dtype=np.float32)[:, None] * inv[None, :]
    pk.add("cos", np.cos(ang).astype(np.float32).T[np.arange(P) % 32])
    pk.add("sin", np.sin(ang).astype(np.float32).T[np.arange(P) % 32])
    turn = np.zeros((P, P), np.float32)
    for m in range(P):
        turn[m + 32 if m % 64 < 32 else m - 32, m] = -1.0 if m % 64 < 32 else 1.0
    pk.add("turn", turn)
    for q in range(TT):
        tok = q * P + i[:, None]
        pk.add(f"causal{q}", np.where(np.arange(T)[None, :] <= tok, 0.0, NEG).astype(np.float32))
        keep = (np.arange(15)[None, :] * 16 + 31 <= tok)
        pk.add(f"cmp_keep{q}", np.broadcast_to(keep[:, None, :], (P, 8, 15)).reshape(P, 120).astype(np.float32))
        pk.add(f"cmp_add{q}", np.broadcast_to(np.where(keep, 0.0, NEG)[:, None, :], (P, 8, 15)).reshape(P, 120).astype(np.float32))
    pk.rows("cols_half", np.concatenate([np.arange(P) < 64, np.arange(P) >= 64]).astype(np.float32))
    seg = np.ones(T, np.float32)
    seg[::64] = 0.0
    pk.rows("not_first64", seg)
    pk.add("one_32nd", np.full((P, 1), 1 / 32, np.float32))
    pk.rows("places", np.arange(1, CAP + 1).astype(np.float32))
    pk.rows("rank8", np.arange(8, 0, -1).astype(np.float32))


def lay_out(a):
    a = {k: np.asarray(v) for k, v in a.items()}
    pk, slots = Pack(), []
    shape_constants(pk)

    def by_columns(w):
        for n in range(0, w.shape[1], FB):
            slots.append(columns_slot(w[:, n:n + FB]))

    def by_rows(w):
        for n in range(0, w.shape[0], FB):
            slots.append(rows_slot(w[n:n + FB]))

    def gated(g, u, d):
        for n in range(0, g.shape[1], FB):
            slots.append(columns_slot(g[:, n:n + FB]))
            slots.append(columns_slot(u[:, n:n + FB]))
            slots.append(rows_slot(d[n:n + FB]))

    for layer in range(2):
        for n in range(6):
            pk.features(f"a{layer}_gain{n}", a["norm_gains"][layer, n])
        gated(a["ffn1_w_gate"][layer], a["ffn1_w_up"][layer], a["ffn1_w_down"][layer])
        if layer == 0:
            w = a["ab_w_in"][0]
            q, kc, vc, ks, vs, kw, vw, gl, z, xbc, dt = np.split(
                w, np.cumsum([512, 128, 128, 128, 128, 128, 128, 24, 1024, 1536])[:].tolist(), axis=1)
            by_columns(xbc)
            by_columns(z)
            pair = [h for j in range(4) for h in (j, j + 4)]
            by_columns(np.concatenate([q[:, h * 64:h * 64 + 64] for h in pair], 1))
            by_columns(np.concatenate([kc, vc, ks, kw], 1))
            by_columns(np.concatenate([vs, vw], 1))
            for w1 in (a["a_cmp_w1_k"][0], a["a_cmp_w1_v"][0]):
                w1 = w1.reshape(32, 64, 64).transpose(1, 0, 2).reshape(64, SLOT)
                slots.append(np.concatenate([w1, w1], 0))
            wo = a["ab_w_out"][0]
            by_rows(np.concatenate([wo[h * 64:h * 64 + 64] for h in pair] + [wo[512:]], 0))
            pk.add("w_gl_dt", np.concatenate([gl, dt], 1).reshape(C, P, 40).transpose(1, 0, 2).reshape(P, C * 40))
            for n in ("k", "v"):
                pe = a[f"a_cmp_pe_{n}"][0].T
                pk.add(f"cmp_pe_{n}", np.concatenate([pe, pe], 0))
                pk.add(f"cmp_w2_{n}", a[f"a_cmp_w2_{n}"][0])
            for k in range(4):
                pk.features(f"ssd_conv{k}", a["b_conv_w"][0, k, 0])
            pk.features("ssd_conv_b", a["b_conv_b"][0])
            pk.rows("dt_bias", a["b_dt_bias"][0])
            pk.rows("a_log", a["b_a_log"][0])
            pk.features("d_skip", np.repeat(a["b_d_skip"][0], 64))
            pk.features("ssd_norm", a["b_norm_w"][0])
        else:
            for n in range(6):
                pk.features(f"mu{n}", a["c_mu"][0, n])
            by_columns(np.concatenate([a["c_w1"][0], a["c_a1"][0]], 1))
            by_columns(a["c_g1"][0])
            lora = np.zeros((P, 2, D), np.float32)
            lora[:64, 0], lora[:64, 1] = a["c_w2"][0], a["c_a2"][0]
            slots.append(lora.reshape(P, SLOT))
            for n in ("r", "k", "v"):
                by_columns(a[f"c_w_{n}"][0])
            for i in range(2):
                by_columns(a["ada_w_2"][i])
            lora = np.zeros((P, 2, D), np.float32)
            lora[:, 0], lora[:32, 1] = a["c_g2"][0][:P], a["c_g2"][0][P:]
            slots.append(lora.reshape(P, SLOT))
            by_columns(a["c_w_o"][0])
            for n in ("w0", "a0", "k_k", "k_a", "r_k", "ln_g", "ln_b"):
                pk.features(n, a[f"c_{n}"][0].reshape(-1))
        gated(a["ffn2_w_gate"][layer], a["ffn2_w_up"][layer], a["ffn2_w_down"][layer])

    pk.features("c", a["c_2"][0])
    for i in range(2):
        pk.features(f"ada_b{i}", a["ada_b_2"][i])
        for n in range(4):
            pk.features(f"b{i}_norm{n}", a["norm_w_2"][i, n])
        if i == 0:
            for j in range(4):
                for part in range(3):
                    by_columns(a["conv_in_w_2"][0][:, part * D + j * FB:part * D + (j + 1) * FB])
            for k in range(3):
                pk.features(f"conv{k}", a["conv_w_2"][0, k])
            by_columns(a["conv_out_w_2"][0])
        else:
            by_columns(a["gdn_in_w_2"][0][:, :4096])
            pk.add("w_ba", a["gdn_in_w_2"][0][:, 4096:].reshape(C, P, 16).transpose(1, 0, 2).reshape(P, C * 16))
            for k in range(4):
                pk.features(f"gdn_conv{k}", a["gdn_conv_w_2"][0, k])
            pk.rows("gdn_a_log", a["gdn_a_log_2"][0])
            pk.rows("gdn_dt_bias", a["gdn_dt_bias_2"][0])
            pk.features("gdn_norm", a["gdn_norm_w_2"][0])
            by_columns(a["gdn_out_w_2"][0])
        router = np.concatenate([a["moe_group_w_2"][i], a["moe_expert_w_2"][i], a["shared_gate_w_2"][i]], 1)
        pk.add(f"router{i}", router.reshape(C, P, 73).transpose(1, 0, 2).reshape(P, C * 73))
        pk.rows(f"router_b{i}", np.concatenate([a["moe_group_b_2"][i], a["moe_expert_b_2"][i]]))
        gated(a["shared_w_gate_2"][i], a["shared_w_up_2"][i], a["shared_w_down_2"][i])
        for e in range(0, N_EXP, 2):
            for n, cut in (("gate", columns_slot), ("up", columns_slot), ("down", rows_slot)):
                slots += [cut(a[f"moe_w_{n}_2"][i, e + k]) for k in range(2)]
    xT = a["x"][0].T.reshape(C, P, T).transpose(1, 0, 2)
    return np.ascontiguousarray(xT), slots, pk


class Queue:

    def __init__(self, sem):
        self.sem, self.count, self.todo, self.seen = sem, 0, [], {}

    def wait(self, *tokens):
        for tok in tokens:
            if tok is None:
                continue
            if isinstance(tok, list):
                self.wait(*tok)
            elif self.seen.get(id(tok[0]), 0) < tok[1]:
                self.seen[id(tok[0])] = tok[1]
                self.todo.append(lambda e, s=tok[0], v=tok[1]: e.wait_ge(s, v))

    def silent(self, fn):
        self.todo.append(fn)

    def do(self, fn, *tokens):
        self.wait(*tokens)
        self.count += 1
        self.todo.append(lambda e, sem=self.sem: fn(e).then_inc(sem, 1))
        return (self.sem, self.count)

    def enter_branch(self, flag):
        def begin(e):
            self.branch = e.If(e.value_load(flag, min_val=0, max_val=1) > 0)
            self.branch.__enter__()
        self.todo.append(begin)

    def leave_branch(self):
        self.todo.append(lambda e: self.branch.__exit__(None, None, None))

    def play(self, e):
        for fn in self.todo:
            fn(e)


class Kernel:
    def __init__(self, nc, x_in, w_in, pack_in, out, n_slots, at):
        self.nc, self.x_in, self.w_in, self.pack_in, self.out = nc, x_in, w_in, pack_in, out
        self.n_slots, self.at = n_slots, at
        self.ctx = ExitStack()
        c = self.ctx
        sem = lambda n: c.enter_context(nc.semaphore(n))
        self.pe, self.dve = Queue(sem("pe_done")), Queue(sem("dve_done"))
        self.act, self.pool = Queue(sem("act_done")), Queue(sem("pool_done"))
        self.sp = Queue(None)
        self.in_sem, self.out_sem = sem("inputs_in"), sem("output_out")
        self.slot_sem = [sem(f"slot_in{i}") for i in range(RING + MOE_EXTRA)]
        self.slot_loads = [0] * (RING + MOE_EXTRA)
        self.where = {}
        self.next_load, self.extra_end = 0, 0
        sb = lambda n, s: c.enter_context(nc.sbuf_tensor(n, s, F32))
        self.ring = sb("weight_ring", [P, RING, SLOT])
        self.pk = sb("params_sb", [P, pack_in.shape[1]])
        self.x = sb("x_sb", [P, C, T])
        self.h = sb("h_sb", [P, C, T])
        self.y = sb("y_sb", [P, C, T])
        self.rms = sb("inv_rms", [P, 2, T])
        self.unused = sb("unused_result", [P, 1])
        self.unused_tok = None
        self.flags = c.enter_context(nc.sbuf_tensor("overflows", [P, 2], mybir.dt.int32))
        self.bank = [c.enter_context(nc.psum_tensor(f"bank{i}", [P, 512], F32)) for i in range(8)]
        self.free = {}
        self.turn = 0
        self.next_slot = 0
        self.stage_no = 0
        self.sp.silent(lambda e: e.dma_start(self.x[:, :, :], x_in).then_inc(self.in_sem, 16))
        self.sp.silent(lambda e: e.dma_start(self.pk[:, :], pack_in).then_inc(self.in_sem, 16))
        self.inputs = (self.in_sem, 32)
        for i in range(RING):
            self.load_next(i, self.ring[:, i, :])
        self.x_tok = [self.inputs] * C
        self.silu_c()
        self.h_free = self.y_free = self.rms_free = None
        self.filler = None

    def par(self, name, lo=0, n=None, rows=P):
        o, w = self.at[name]
        return self.pk[0:rows, o + lo:o + (w if n is None else lo + n)]

    def load_next(self, loc, mem, *after):
        i = self.next_load
        if i >= self.n_slots or (loc >= RING and i >= self.extra_end):
            return
        self.next_load += 1
        self.slot_loads[loc] += 1
        self.where[i] = (loc, mem, (self.slot_sem[loc], 16 * self.slot_loads[loc]))
        self.sp.wait(*after)
        self.sp.silent(lambda e: e.dma_start(mem, self.w_in[i]).then_inc(self.slot_sem[loc], 16))

    def more_slots(self, extra, stage_slots):
        self.extra_end = self.next_slot + stage_slots
        toks = [(q.sem, q.count) for q in (self.pe, self.dve, self.act, self.pool) if q.count]
        for n in range(extra.shape[1]):
            self.load_next(RING + n, extra[:, n, :], toks)

    def slot(self):
        i = self.next_slot
        self.next_slot += 1
        return (i, *self.where[i][1:])

    def slot_read(self, i, tok):
        self.load_next(*self.where[i][:2], tok)

    def half(self, banks=(4, 5, 6, 7)):
        ps, b, fr = self.full(banks)
        return ps[:, 0:T], b, fr

    def full(self, banks=(4, 5, 6, 7)):
        b = banks[self.turn % len(banks)]
        self.turn += 1
        return self.bank[b], b, self.free.get(b)

    def read_by(self, b, *toks):
        self.free[b] = list(toks)

    def mm(self, out, lhsT, rhs, start, stop, shared=False):
        self.pe.silent(lambda e: e.matmul(out, lhsT, rhs, start=start, stop=stop, skip_group_check=shared))

    def mm_end(self, out, lhsT, rhs, start, stop, shared=False):
        return self.pe.do(lambda e: e.matmul(out, lhsT, rhs, start=start, stop=stop, skip_group_check=shared))

    def transposed(self, out, in_, last=False):
        n = in_.shape[0]
        ident = self.par("ident", 0, n, n)
        if last:
            return self.pe.do(lambda e: e.transpose(out, in_, ident))
        self.pe.silent(lambda e: e.transpose(out, in_, ident))

    def tt(self, q, out, a, b, op, *tok):
        return q.do(lambda e: e.tensor_tensor(out, a, b, op), *tok)

    def ts(self, q, out, a, s1, s2, op0, op1, *tok):
        if op1 is None:
            return q.do(lambda e: e.tensor_scalar(out, a, s1, None, op0), *tok)
        return q.do(lambda e: e.tensor_scalar(out, a, s1, s2, op0, op1), *tok)

    def stt(self, out, a, s, b, op0, op1, *tok):
        return self.dve.do(lambda e: e.scalar_tensor_tensor(out=out, in0=a, scalar=s, in1=b, op0=op0, op1=op1), *tok)

    def func(self, out, a, f, *tok, scale=1.0, bias=0.0, accum=None):
        if accum is None:
            return self.act.do(lambda e: e.activation(out, a, f, scale=scale, bias=bias), *tok)
        return self.act.do(lambda e: e.activation(out, a, f, scale=scale, bias=bias, accum_out=accum), *tok)

    def copy(self, q, out, a, *tok):
        if q is self.act:
            return self.func(out, a, ACT.Copy, *tok)
        return q.do(lambda e: e.tensor_copy(out, a), *tok)

    def reduce(self, out, a, op, *tok):
        return self.dve.do(lambda e: e.tensor_reduce(out, a, AX, op), *tok)

    def barrier(self):
        toks = [(q.sem, q.count) for q in (self.pe, self.dve, self.act, self.pool) if q.count]
        for q in (self.pe, self.dve, self.act, self.pool):
            q.wait(*toks)

    def stage(self):
        self.barrier()
        self.stage_no += 1
        st = ExitStack()
        no, nc = self.stage_no, self.nc

        def sb(name, shape):
            return st.enter_context(nc.sbuf_tensor(f"{name}_{no}", shape, F32))
        return st, sb

    def inv_rms(self, squares, n, eps, toks, lhs="ones", scale=1.0, out=None):
        ps, key, fr = self.half()
        self.pe.wait(fr, self.inputs)
        for c, s in enumerate(squares):
            self.pe.wait(toks[c])
            if c == len(squares) - 1:
                tok = self.mm_end(ps[:, 0:s.shape[-1]], self.par(lhs), s, c == 0, True)
            else:
                self.mm(ps[:, 0:s.shape[-1]], self.par(lhs), s, c == 0, False)
        w = squares[0].shape[-1]
        out = self.rms[:, 0, :] if out is None else out
        s2 = 1.0 / (scale * scale)
        self.unused_tok = self.func(self.unused[:, :], self.par("ones", 0, 1), ACT.Sqrt, self.unused_tok)
        t = self.ts(self.dve, out, ps[:, 0:w], s2 / n, s2 * eps, ALU.mult, ALU.add, tok, self.rms_free)
        self.read_by(key, t)
        t = self.func(out, out, ACT.Sqrt, t)
        return self.dve.do(lambda e: e.reciprocal(out, out), t)

    def norm_x(self, gain, shift=None, tok=None):
        sq = self.y
        toks = []
        for c in range(C):
            toks.append(self.func(sq[:, c, :], self.x[:, c, :], ACT.Square, self.x_tok[c], self.y_free))
        r = self.inv_rms([sq[:, c, :] for c in range(C)], D, NORM_EPS, toks)
        self.y_free = (self.pe.sem, self.pe.count)
        out = []
        for c in range(C):
            t = self.stt(self.h[:, c, :], self.x[:, c, :], gain[:, c:c + 1], self.rms[:, 0, :], ALU.mult, ALU.mult,
                         r, self.h_free, tok)
            if shift is not None:
                t = self.func(self.h[:, c, :], self.h[:, c, :], ACT.Identity, t, bias=shift[:, c:c + 1])
            out.append(t)
        self.rms_free = (self.dve.sem, self.dve.count)
        return out

    def add_back(self, y_toks, gain, scale, tok=None):
        toks = []
        sq = self.h
        for b in range(4):
            t = self.func(sq[:, 2 * b:2 * b + 2, :], self.bank[b][:, :].rearrange("p (c t) -> p c t", c=2), ACT.Square, y_toks[b])
            toks += [t, t]
        r = self.inv_rms([sq[:, c, :] for c in range(C)], D, NORM_EPS, toks, scale=scale)
        self.h_free = (self.pe.sem, self.pe.count)
        xt = []
        for c in range(C):
            t = self.stt(self.y[:, c, :], self.bank[c // 2][:, (c % 2) * T:(c % 2 + 1) * T], gain[:, c:c + 1], self.rms[:, 0, :],
                         ALU.mult, ALU.mult, r, y_toks[c // 2], self.y_free, tok)
            if c % 2:
                self.read_by(c // 2, t)
            q = self.dve if c % 2 else self.pool
            xt.append(self.tt(q, self.x[:, c, :], self.x[:, c, :], self.y[:, c, :], ALU.add, t, self.x_tok[c]))
        self.rms_free = (self.dve.sem, self.dve.count)
        self.x_tok = xt
        self.y_free = xt[-2:]

    def shared_experts(self, h_toks, n_blocks, gate, gate_tok):
        st, sb = (self.scope, self.sbs)
        silu, hid = self.silu, self.hid
        pend = []

        def down():
            u, i_d, wd, d_tok, hid_tok = pend.pop(0)
            fc = u % 2
            self.pe.wait(hid_tok, d_tok)
            if u == 0:
                for b in range(4):
                    self.pe.wait(self.free.get(b))
            toks = []
            for c in range(C):
                args = (self.bank[c // 2][:, (c % 2) * T:(c % 2 + 1) * T], wd[:, fc * D + c * P:fc * D + (c + 1) * P],
                        hid[:, u % 4, :], u == 0 and c % 2 == 0, False, True)
                if c == C - 1:
                    toks.append(self.mm_end(*args))
                else:
                    self.mm(*args)
            self.hid_free[u % 4] = toks[-1]
            if fc == 1:
                self.slot_read(i_d, toks[-1])
            return toks

        for b in range(n_blocks):
            i_g, wg, g_tok = self.slot()
            i_u, wu, u_tok = self.slot()
            i_d, wd, d_tok = self.slot()
            for fc in range(2):
                u = 2 * b + fc
                bk = 4 + u % 3
                ps = self.bank[bk]
                self.pe.wait(self.free.get(bk))
                self.pe.wait(g_tok)
                for c in range(C):
                    if u == 0:
                        self.pe.wait(h_toks[c])
                    self.mm(ps[:, 0:T], wg[:, c * FB + fc * P:c * FB + (fc + 1) * P], self.h[:, c, :], c == 0, c == C - 1)
                self.pe.wait(u_tok)
                for c in range(C):
                    a = (ps[:, T:2 * T], wu[:, c * FB + fc * P:c * FB + (fc + 1) * P], self.h[:, c, :], c == 0, c == C - 1)
                    if c < C - 1:
                        self.mm(*a)
                    else:
                        up = self.mm_end(*a)
                if fc == 1:
                    self.slot_read(i_g, up)
                    self.slot_read(i_u, up)
                if fc == 0:
                    self.pe.wait(gate_tok, self.free.get(7))
                    gp = self.bank[7][:, 0:T]
                    gb = self.mm_end(gp, self.par("ident", 0, 1, 1).to_broadcast([1, P]), gate, True, True)
                    g_sb = self.gate_sb[:, b % 2, :]
                    gc = self.copy(self.act, g_sb, gp, gb, self.gate_free[b % 2])
                    self.read_by(7, gc)
                s = self.func(silu[:, u % 4, :], ps[:, 0:T], ACT.Silu, up, self.silu_free[u % 4])
                m = self.tt(self.dve, hid[:, u % 4, :], silu[:, u % 4, :], ps[:, T:2 * T], ALU.mult, s, up, self.hid_free[u % 4])
                self.silu_free[u % 4] = m
                self.read_by(bk, s, m)
                m = self.tt(self.dve, hid[:, u % 4, :], hid[:, u % 4, :], g_sb, ALU.mult, m, gc)
                self.gate_free[b % 2] = m
                pend.append((u, i_d, wd, d_tok, m))
                if len(pend) > 2:
                    toks = down()
        while pend:
            toks = down()
        return toks

    def gated_scope(self):
        self.scope, sb = self.stage()
        self.sbs = sb
        self.silu, self.hid, self.gate_sb = sb("silu", [P, 4, T]), sb("hid", [P, 4, T]), sb("gate_rows", [P, 2, T])
        self.silu_free, self.hid_free, self.gate_free = [None] * 4, [None] * 4, [None] * 2

    def split(self, hi, lo, a, *tok):
        t1 = self.func(hi, a, ACT.Copy, *tok)
        t2 = self.tt(self.dve, lo, a, hi.bitcast(F32), ALU.subtract, t1, *tok)
        return [t1, t2]

    def mm3(self, out, w, x, start, stop, shared=False, signal=False):
        self.mm(out, w[0], x[0], start, False, shared)
        self.mm(out, w[0], x[1], False, False, shared)
        return (self.mm_end if signal else self.mm)(out, w[1], x[0], False, stop, shared)

    def ffn(self, g_in, g_out):
        st, sb = self.stage()
        sbr = lambda n, shape: st.enter_context(self.nc.sbuf_tensor(f"{n}_{self.stage_no}", shape, F32R))
        units, NB = 2 * FFN_BLOCKS, 3
        self.more_slots(sb("more_slots", [P, FFN_EXTRA, SLOT]), 3 * FFN_BLOCKS)
        h_r = sbr("h_hi_lo", [P, 2, C, T])
        gu_r = sbr("gate_up_hi_lo", [P, NB, 2, 2, C, P])
        d_r = sbr("down_hi_lo", [P, 2, 2, D])
        hid_r = sbr("hidden_hi_lo", [P, 2, 2, T])
        silu, hid = sb("silu", [P, 2, T]), sb("hidden", [P, 2, T])
        gu_free, d_free, silu_free, hid_free, hr_free = [None] * NB, [None] * 2, [None] * 2, [None] * 2, [None] * 2
        blocks, gu_tok, d_tok = {}, {}, {}

        def split_gate_up(u):
            if u >= units:
                return
            b, fc, k = u // 2, u % 2, u % NB
            if fc == 0:
                blocks[b] = [self.slot() for _ in range(3)]
            toks = []
            for n in range(2):
                i, w, tok = blocks[b][n]
                half = w.rearrange("p (c f) -> p c f", c=C)[:, :, fc * P:(fc + 1) * P]
                t = self.split(gu_r[:, k, n, 0, :, :], gu_r[:, k, n, 1, :, :], half, tok, gu_free[k])
                toks += t
                if fc:
                    self.slot_read(i, t)
            gu_tok[u] = toks

        def split_down(u):
            if u >= units:
                return
            b, fc, k = u // 2, u % 2, u % 2
            i, w, tok = blocks[b][2]
            d_tok[u] = self.split(d_r[:, k, 0, :], d_r[:, k, 1, :], w[:, fc * D:(fc + 1) * D], tok, d_free[k])
            if fc:
                self.slot_read(i, d_tok[u])

        split_gate_up(0)
        h_toks = self.norm_x(self.par(g_in))
        hr_toks = [self.split(h_r[:, 0, c, :], h_r[:, 1, c, :], self.h[:, c, :], h_toks[c]) for c in range(C)]
        split_down(0)
        split_gate_up(1)
        self.h_free = hr_toks[-1]

        def gate_up(u):
            bk, k = 4 + u % 4, u % NB
            ps = self.bank[bk]
            self.pe.wait(self.free.get(bk), gu_tok[u])
            for n in range(2):
                for c in range(C):
                    if u == 0:
                        self.pe.wait(hr_toks[c])
                    end = self.mm3(ps[:, n * T:(n + 1) * T], (gu_r[:, k, n, 0, c, :], gu_r[:, k, n, 1, c, :]),
                                   (h_r[:, 0, c, :], h_r[:, 1, c, :]), c == 0, c == C - 1, signal=n and c == C - 1)
            gu_free[k] = end
            k = u % 2
            s = self.func(silu[:, k, :], ps[:, 0:T], ACT.Silu, end, silu_free[k])
            m = self.tt(self.dve, hid[:, k, :], silu[:, k, :], ps[:, T:2 * T], ALU.mult, s, hid_free[k])
            silu_free[k] = m
            self.read_by(bk, m)
            hid_free[k] = self.split(hid_r[:, k, 0, :], hid_r[:, k, 1, :], hid[:, k, :], m, hr_free[k])

        def down(u):
            k, out = u % 2, []
            self.pe.wait(d_tok[u], hid_free[k])
            for c in range(C):
                if u == 0 and c % 2 == 0:
                    self.pe.wait(self.free.get(c // 2))
                end = u == units - 1 and c % 2 == 1
                t = self.mm3(self.bank[c // 2][:, (c % 2) * T:(c % 2 + 1) * T], (d_r[:, k, 0, c * P:(c + 1) * P], d_r[:, k, 1, c * P:(c + 1) * P]),
                             (hid_r[:, k, 0, :], hid_r[:, k, 1, :]), u == 0 and c % 2 == 0, end, True, signal=end or c == C - 1)
                if end:
                    out.append(t)
            d_free[k] = hr_free[k] = t
            return out

        for u in range(units):
            split_gate_up(u + 2)
            if u:
                split_down(u)
            gate_up(u)
            if u:
                down(u - 1)
        self.add_back(down(units - 1), self.par(g_out), 0.5)
        st.close()

    def projection_buffers(self, st, chunks=C, depth=3):
        sbr = lambda n, shape: st.enter_context(self.nc.sbuf_tensor(f"{n}_{self.next_slot}", shape, F32R))
        self.x_r, self.w_r = sbr("source_hi_lo", [P, 2, chunks, T]), sbr("weight_hi_lo", [P, depth, 2, D])
        self.w_free, self.w_turn, self.xr_free, self.ready = [None] * depth, 0, None, []

    def source(self, src, toks, chunks=C):
        out = [self.split(self.x_r[:, 0, c, :], self.x_r[:, 1, c, :], src[:, c, :], toks[c], self.xr_free) for c in range(chunks)]
        self.x_split = out[-1]
        return out

    def prepare(self, half, times=1):
        for _ in range(times):
            if self.w_turn % 2 == 0:
                self.w_slot = self.slot()
            i, w, tok = self.w_slot
            k = self.w_turn % len(self.w_free)
            src = half(w, self.w_turn % 2)
            shaped = (lambda a: a.rearrange("p (c f) -> p c f", c=C)) if len(src.shape) == 3 else (lambda a: a)
            done = self.split(shaped(self.w_r[:, k, 0, :]), shaped(self.w_r[:, k, 1, :]), src, tok, self.w_free[k])
            self.ready.append((k, done))
            if self.w_turn % 2:
                self.slot_read(i, done)
            self.w_turn += 1

    def units(self, n_slots, half, product, then=None):
        ahead = len(self.w_free) - 1
        self.prepare(half, ahead - len(self.ready))
        for u in range(2 * n_slots):
            if u + ahead < 2 * n_slots:
                self.prepare(half)
            elif then is not None:
                self.prepare(then)
            k, tok = self.ready.pop(0)
            self.w_free[k] = product(u, (self.w_r[:, k, 0, :], self.w_r[:, k, 1, :]), tok)
        self.xr_free = (self.pe.sem, self.pe.count)

    @staticmethod
    def column_half(w, n):
        return w.rearrange("p (c f) -> p c f", c=C)[:, :, n * P:(n + 1) * P]

    @staticmethod
    def row_half(w, n):
        return w[:, n * D:(n + 1) * D]

    def columns(self, toks, n_slots, consume, then=None):
        def product(u, w, tok):
            ps, key, fr = self.half()
            self.pe.wait(fr, tok)
            for c in range(C):
                self.pe.wait(toks[c])
                cut = slice(c * P, (c + 1) * P)
                end = self.mm3(ps, (w[0][:, cut], w[1][:, cut]), (self.x_r[:, 0, c, :], self.x_r[:, 1, c, :]), c == 0, c == C - 1, signal=c == C - 1)
            self.read_by(key, consume(u, ps, end))
            return end
        self.units(n_slots, self.column_half, product, then)

    def project_out(self, n_chunks, toks):
        for b in range(4):
            self.pe.wait(self.free.get(b))
        out = []

        def product(kc, w, tok):
            self.pe.wait(tok, toks[kc])
            end = kc == n_chunks - 1
            for c in range(C):
                cut = slice(c * P, (c + 1) * P)
                last = end and c % 2 == 1
                t = self.mm3(self.bank[c // 2][:, (c % 2) * T:(c % 2 + 1) * T], (w[0][:, cut], w[1][:, cut]),
                             (self.x_r[:, 0, kc, :], self.x_r[:, 1, kc, :]), kc == 0 and c % 2 == 0, last, True, signal=last or c == C - 1)
                if last:
                    out.append(t)
            return t
        self.units(n_chunks // 2, self.row_half, product)
        return out

    def project_columns_out(self, toks):
        out = []

        def product(u, w, tok):
            self.pe.wait(self.free.get(u // 2), tok)
            for c in range(C):
                self.pe.wait(toks[c])
                cut = slice(c * P, (c + 1) * P)
                t = self.mm3(self.bank[u // 2][:, (u % 2) * T:(u % 2 + 1) * T], (w[0][:, cut], w[1][:, cut]),
                             (self.x_r[:, 0, c, :], self.x_r[:, 1, c, :]), c == 0, c == C - 1, signal=c == C - 1)
            if u % 2:
                out.append(t)
            return t
        self.units(4, self.column_half, product)
        return out

    def finish(self):
        self.sp.wait(self.x_tok)
        self.sp.silent(lambda e: e.dma_start(self.out, self.x[:, :, :]).then_inc(self.out_sem, 16))
        self.sp.silent(lambda e: e.wait_ge(self.out_sem, 16))
        block = self.ctx.enter_context(self.nc.Block())

        @block.sync
        def _(e):
            self.sp.play(e)

        @block.tensor
        def _(e):
            self.pe.play(e)

        @block.vector
        def _(e):
            self.dve.play(e)

        @block.scalar
        def _(e):
            self.act.play(e)

        @block.gpsimd
        def _(e):
            self.pool.play(e)
        self.ctx.close()

    def silu_c(self):
        self.cs = self.ctx.enter_context(self.nc.sbuf_tensor("silu_c", [P, C], F32))
        self.mod = [self.ctx.enter_context(self.nc.sbuf_tensor(f"mod{i}", [P, 6 * C], F32)) for i in range(2)]
        self.mod_rows = self.ctx.enter_context(self.nc.sbuf_tensor("mod_rows", [P, 2, FB], F32))
        self.mod_rows_free = [None, None]
        self.gain = self.ctx.enter_context(self.nc.sbuf_tensor("mod_gain", [P, 2, 4, C], F32))
        self.cs_tok = self.func(self.cs[:, :], self.par("c"), ACT.Silu, self.inputs)

    def modulation(self, i):
        self.pe.wait(self.cs_tok)
        ps = self.bank[0]
        self.pe.wait(self.free.get(0))
        for n in range(6 * D // FB):
            s, w, tok = self.slot()
            k = 1 + n % 2
            self.pe.wait(tok, self.free.get(k))
            for c in range(C):
                o = self.bank[k][32 * (c % 4):32 * (c % 4) + 32, 0:FB]
                a = (o, self.cs[:, c:c + 1].to_broadcast([P, 32]), w[:, c * FB:(c + 1) * FB], c < 4, c >= 4)
                end = self.mm_end(*a) if c == C - 1 else self.mm(*a)
            self.slot_read(s, end)
            t = self.copy(self.act, self.mod_rows[:, n % 2, :], self.bank[k][:, 0:FB], end, self.mod_rows_free[n % 2])
            self.read_by(k, t)
            yield
            self.pe.wait(t)
            for fc in range(2):
                a = (ps[:, 2 * n + fc:2 * n + fc + 1], self.mod_rows[:, n % 2, fc * P:(fc + 1) * P], self.par("one_32nd"), True, True)
                end = self.mm_end(*a) if fc else self.mm(*a)
            self.mod_rows_free[n % 2] = end
        b = 0
        mod, g = self.mod[i], self.gain
        t = self.tt(self.dve, mod[:, :], ps[:, 0:6 * C], self.par(f"ada_b{i}"), ALU.add, end, self.inputs)
        self.read_by(b, t)
        part = lambda n: mod[:, n * C:(n + 1) * C]
        toks = []
        for n, (m, w) in enumerate(((1, 0), (4, 2))):
            toks.append(self.stt(g[:, i, w, :], part(m), 1.0, self.par(f"b{i}_norm{w}"), ALU.add, ALU.mult, t))
        for m, w in ((2, 1), (5, 3)):
            toks.append(self.tt(self.dve, g[:, i, w, :], part(m), self.par(f"b{i}_norm{w}"), ALU.mult, t))
        self.mod_tok = toks[-1]

    def both_modulations(self):
        for i in range(2):
            yield from self.modulation(i)

    def background(self, n=1):
        for _ in range(n):
            if self.filler is not None and next(self.filler, True):
                self.filler = None

    def first_equal(self, out, vals, best, tmp, tok):
        t = self.ts(self.dve, tmp, vals, best, None, ALU.is_equal, None, tok)
        t = self.tt(self.dve, tmp, tmp, self.par("rank8"), ALU.mult, t)
        t = self.reduce(out[:, 0:1], tmp, ALU.max, t)
        t = self.ts(self.dve, tmp, tmp, out[:, 0:1], None, ALU.is_equal, None, t)
        return self.copy(self.dve, out, tmp, t)

    def router(self, i, sb, h_toks):
        gates, picks, shared = [], [], sb("shared_gate", [P, TT])
        g_tok, m_tok = [], []
        for q in range(TT):
            ps, key, fr = self.half()
            self.pe.wait(fr, self.inputs)
            for c in range(C):
                self.pe.wait(h_toks[c])
                a = (ps[:, 0:73], self.h[:, c, q * P:(q + 1) * P], self.par(f"router{i}", c * 73, 73), c == 0, c == C - 1)
                end = self.mm_end(*a) if c == C - 1 else self.mm(*a)
            lg, s = sb(f"logits{q}", [P, 73]), sb(f"route{q}", [P, 96])
            t = self.tt(self.dve, lg[:, 0:72], ps[:, 0:72], self.par(f"router_b{i}"), ALU.add, end)
            t_sh = self.func(shared[:, q:q + 1], ps[:, 72:73], ACT.Sigmoid, end, t)
            self.read_by(key, t_sh)
            gl, el = lg[:, 0:8], lg[:, 8:72]
            best, psel, tmp, grp, tmp2 = s[:, 0:1], s[:, 1:2], s[:, 8:16], s[:, 16:24], s[:, 24:32]
            t = self.reduce(best, gl, ALU.max, t)
            t1 = self.first_equal(grp, gl, best, tmp, t)
            t = self.ts(self.dve, tmp2, gl, best, None, ALU.subtract, None, t)
            t = self.func(tmp2, tmp2, ACT.Exp, t, accum=psel)
            t2 = self.dve.do(lambda e, psel=psel: e.reciprocal(psel, psel), t)
            prod = sb(f"picked{q}", [P, N_EXP])
            v = lambda a: a.rearrange("p (g e) -> p g e", g=N_GRP)
            t = self.tt(self.dve, v(prod[:, :]), v(el), grp.unsqueeze(2).to_broadcast([P, N_GRP, 8]), ALU.mult, t1)
            els = s[:, 32:40]
            t = self.reduce(els, prod[:, :].rearrange("p (g e) -> p e g", g=N_GRP), ALU.add, t)
            m1, m2, e1, e2, g1, g2 = s[:, 2:3], s[:, 3:4], s[:, 40:48], s[:, 48:56], s[:, 4:5], s[:, 5:6]
            t = self.reduce(m1, els, ALU.max, t)
            t = self.first_equal(e1, els, m1, tmp, t)
            rest, both = s[:, 56:64], s[:, 64:72]
            t = self.stt(rest, e1, NEG, els, ALU.mult, ALU.add, t)
            t = self.reduce(m2, rest, ALU.max, t)
            t = self.first_equal(e2, rest, m2, tmp, t)
            spread = lambda out, x, *tok: self.tt(self.dve, v(out), grp.unsqueeze(2).to_broadcast([P, N_GRP, 8]),
                                                  x.unsqueeze(1).to_broadcast([P, N_GRP, 8]), ALU.mult, *tok)
            t = self.tt(self.dve, both, e1, e2, ALU.add, t)
            t = spread(prod[:, :], both, t)
            picks.append(prod)
            m_tok.append(t)
            t = self.tt(self.dve, g2, m2, m1, ALU.subtract, t)
            t = self.func(g2, g2, ACT.Exp, t)
            t = self.ts(self.dve, g1, g2, 1.0, None, ALU.add, None, t)
            t = self.dve.do(lambda e, g1=g1: e.reciprocal(g1, g1), t)
            t = self.tt(self.dve, g1, g1, psel, ALU.mult, t, t2)
            t = self.tt(self.dve, g2, g2, g1, ALU.mult, t)
            t = self.ts(self.dve, e1, e1, g1, None, ALU.mult, None, t)
            t = self.stt(e1, e2, g2, e1, ALU.mult, ALU.add, t)
            gates.append(sb(f"gates{q}", [P, N_EXP]))
            g_tok.append(spread(gates[q][:, :], e1, t))
        row = sb("shared_gate_row", [1, T])
        ps, key, fr = self.half()
        self.pe.wait(fr, t_sh)
        for q in range(TT):
            end = self.transposed(ps[0:1, q * P:(q + 1) * P], shared[:, q:q + 1], last=True)
        t = self.copy(self.act, row[:, :], ps[0:1, 0:T], end)
        self.read_by(key, t)
        return gates, g_tok, picks, m_tok, row, t

    def ranks(self, i, sb, picks, m_tok):
        rank = sb("ranks", [P, TT, N_EXP])
        ps, key, fr = self.half()
        self.pe.wait(fr, m_tok)
        self.mm(ps[:, 0:64], self.par("upto"), picks[0][:, :], True, True)
        self.mm(ps[:, 64:128], self.par("ones"), picks[0][:, :], True, False)
        self.mm(ps[:, 64:128], self.par("upto"), picks[1][:, :], False, True)
        self.mm(ps[:, 128:192], self.par("ones"), picks[0][:, :], True, False)
        end = self.mm_end(ps[:, 128:192], self.par("ones"), picks[1][:, :], False, True)
        for q in range(TT):
            r_tok = self.tt(self.dve, rank[:, q, :], ps[:, q * 64:(q + 1) * 64], picks[q][:, :], ALU.mult, end)
        most = sb("most_tokens", [P, 1])
        t = self.reduce(most[:, :], ps[:, 128:192], ALU.max, end)
        self.read_by(key, t)
        flag = self.flags[:, i:i + 1]
        f_tok = self.ts(self.dve, flag[:, :], most[:, :], float(CAP), None, ALU.is_gt, None, t)
        return rank, r_tok, flag, f_tok

    def moe(self, i):
        self.gated_scope()
        sb = self.sbs
        extra = sb("more_slots", [P, MOE_EXTRA, SLOT])
        self.more_slots(extra, 3 * (SHARED_BLOCKS + N_EXP))
        part = lambda n: self.mod[i][:, n * C:(n + 1) * C]
        h_toks = self.norm_x(self.gain[:, i, 2, :], part(3), self.mod_tok)
        gates, g_tok, picks, m_tok, row, row_tok = self.router(i, sb, h_toks)
        self.shared_experts(h_toks, SHARED_BLOCKS, row[:, :], row_tok)
        rank, r_tok, flag, f_tok = self.ranks(i, sb, picks, m_tok)
        h_tok = self.scope.enter_context(self.nc.sbuf_tensor(f"h_tokens_hi_lo_{self.stage_no}", [P, 2, TT, D], F32R))
        for q in range(TT):
            for n in range(2):
                ps, b, fr = self.full()
                self.pe.wait(fr)
                for m in range(4):
                    end = self.transposed(ps[:, m * P:(m + 1) * P], self.h[:, 4 * n + m, q * P:(q + 1) * P], last=m == 3)
                cut = slice(n * 512, (n + 1) * 512)
                ht = self.split(h_tok[:, 0, q, cut], h_tok[:, 1, q, cut], ps[:, :], end)
                self.read_by(b, ht)
        first_expert = self.next_slot
        self.packed_experts(sb, gates, g_tok, rank, r_tok, h_tok, ht)
        y = self.experts_end
        self.y_free = y
        self.overflow(i, sb, flag, f_tok, gates, rank, extra, first_expert)
        self.add_back([y] * 4, self.gain[:, i, 3, :], 1.0)
        self.scope.close()

    def packed_experts(self, sb, gates, g_tok, rank, r_tok, h_tok, ht):
        two = lambda n, shape: [sb(f"{n}{k}", shape) for k in range(2)]
        sel = [self.scope.enter_context(self.nc.sbuf_tensor(f"places{k}_{self.stage_no}", [P, TT, 4, CAP], F32R)) for k in range(2)]
        selg, hc = two("gated_places", [P, TT, 4, CAP]), sb("packed_h", [P, C, 4 * CAP])
        out, turned = two("down", [P, D]), two("hidden_and_scatter_T", [P, 2 * T])
        silu, hid = two("packed_silu", [P, FB]), two("packed_hidden", [P, FB])
        free = {n: [None, None] for n in ("sel", "selg", "out", "turned", "silu", "hid")}
        free["hc"] = None
        done = {}
        PAIRS = N_EXP // 2

        def select(g):
            k = g % 2
            for q in range(TT):
                r = rank[:, q, 4 * g:4 * g + 4].unsqueeze(2).to_broadcast([P, 4, CAP])
                t = self.tt(self.dve, sel[k][:, q, :, :], self.par("places").unsqueeze(1).to_broadcast([P, 4, CAP]), r, ALU.is_equal, r_tok, free["sel"][k])
                done["sel", g, q] = t
                done["selg", g, q] = self.tt(self.dve, selg[k][:, q, :, :], sel[k][:, q, :, :].bitcast(F32),
                                             gates[q][:, 4 * g:4 * g + 4].unsqueeze(2).to_broadcast([P, 4, CAP]), ALU.mult, t, g_tok[q], free["selg"][k])

        def places(buf, p, q):
            return buf[(p // 2) % 2][:, q, 2 * (p % 2):2 * (p % 2) + 2, :]

        def gather(g, n):
            ps, b, fr = self.full()
            self.pe.wait(fr, ht, done["sel", g, 0], done["sel", g, 1])
            for m in range(2):
                c = 2 * n + m
                for x, (q, part) in enumerate((q, part) for q in range(TT) for part in range(2)):
                    a = (ps[:, m * T:(m + 1) * T], h_tok[:, part, q, c * P:(c + 1) * P],
                         sel[g % 2][:, q, :, :].rearrange("p e s -> p (e s)"), x == 0, x == 3)
                    end = self.mm_end(*a) if x == 3 and m else self.mm(*a)
            free["sel"][g % 2] = end
            t = self.copy(self.act, hc[:, 2 * n:2 * n + 2, :], ps[:, :].rearrange("p (m t) -> p m t", m=2), end, free["hc"])
            self.read_by(b, t)
            done["hc", g, n] = t

        def gate_up(p):
            w = [self.slot() for _ in range(6)]
            done["wd", p] = w[4:]
            ps, b, fr = self.full()
            self.pe.wait(fr, [done["hc", p // 2, n] for n in range(4)])
            for n in range(2):
                for c in range(C):
                    for e in range(2):
                        self.pe.wait(w[2 * n + e][2])
                        a = (ps[e * CAP:(e + 1) * CAP, n * FB:(n + 1) * FB], hc[:, c, (2 * (p % 2) + e) * CAP:(2 * (p % 2) + e + 1) * CAP],
                             w[2 * n + e][1][:, c * FB:(c + 1) * FB], c == 0, c == C - 1)
                        end = self.mm_end(*a) if e and c == C - 1 else self.mm(*a)
                for e in range(2):
                    self.slot_read(w[2 * n + e][0], end)
            free["hc"] = end
            k = p % 2
            t = self.func(silu[k][:, :], ps[:, 0:FB], ACT.Silu, end, free["silu"][k])
            t = self.tt(self.dve, hid[k][:, :], silu[k][:, :], ps[:, FB:2 * FB], ALU.mult, t, free["hid"][k])
            free["silu"][k] = t
            self.read_by(b, t)
            done["hid", p] = t

        def turn(p):
            ps, b, fr = self.full()
            self.pe.wait(fr, done["hid", p], done["selg", p // 2, 0], done["selg", p // 2, 1])
            for fc in range(2):
                self.transposed(ps[:, fc * P:(fc + 1) * P], hid[p % 2][:, fc * P:(fc + 1) * P])
            for q in range(TT):
                end = self.transposed(ps[:, T + q * P:T + (q + 1) * P], places(selg, p, q).rearrange("p e s -> p (e s)"), last=q == 1)
            if p % 2 == 1:
                free["selg"][(p // 2) % 2] = end
            free["hid"][p % 2] = end
            t = self.copy(self.act, turned[p % 2][:, :], ps[:, :], end, free["turned"][p % 2])
            self.read_by(b, t)
            done["turned", p] = t

        def down(p, n):
            ps, b, fr = self.full()
            self.pe.wait(fr, done["turned", p])
            for fc in range(2):
                for e in range(2):
                    i, wd, tok = done["wd", p][e]
                    self.pe.wait(tok)
                    a = (ps[e * CAP:(e + 1) * CAP, :], turned[p % 2][:, fc * P + e * CAP:fc * P + (e + 1) * CAP],
                         wd[:, fc * D + n * 512:fc * D + (n + 1) * 512], fc == 0, fc == 1)
                    end = self.mm_end(*a) if fc and e else self.mm(*a)
            if n == 1:
                for e in range(2):
                    self.slot_read(done["wd", p][e][0], end)
            t = self.copy(self.dve, out[p % 2][:, n * 512:(n + 1) * 512], ps[:, :], end, free["out"][p % 2])
            self.read_by(b, t)
            done["out", p, n] = t

        def scatter(p):
            self.pe.wait(done["out", p, 0], done["out", p, 1])
            for c in range(C):
                a = (self.bank[c // 2][:, (c % 2) * T:(c % 2 + 1) * T], out[p % 2][:, c * P:(c + 1) * P], turned[p % 2][:, T:2 * T],
                     False, p == PAIRS - 1 and c % 2 == 1, True)
                end = self.mm_end(*a) if c == C - 1 else self.mm(*a)
            free["out"][p % 2] = free["turned"][p % 2] = end
            return end

        select(0)
        for n in range(4):
            gather(0, n)
        for p in range(PAIRS):
            g = p // 2 + 1
            gate_up(p)
            if p % 2 == 0 and g < PAIRS // 2:
                select(g)
            parts = range(4) if p % 2 and g < PAIRS // 2 else ()
            for n in parts[:2]:
                gather(g, n)
            if p:
                scatter(p - 1)
            turn(p)
            for n in parts[2:]:
                gather(g, n)
            down(p, 0)
            down(p, 1)
        self.experts_end = scatter(PAIRS - 1)

    def overflow(self, i, sb, flag, f_tok, gates, rank, buf, first_expert):
        nc = self.nc
        queues = (self.sp, self.pe, self.dve, self.act, self.pool)
        ready = [f_tok, self.experts_end]
        saved, banks = [], dict(self.free)
        load = self.ctx.enter_context(nc.semaphore(f"overflow_load{i}"))
        for n, q in enumerate(queues):
            q.wait(*ready)
            saved.append((q.sem, q.count, dict(q.seen)))
            q.enter_branch(flag[0:1, 0:1])
            q.sem = self.ctx.enter_context(nc.semaphore(f"overflow_{n}_{i}")) if n else None
            q.count = 0
        late, gates_T = sb("late_gates", [P, N_EXP]), sb("late_gates_T", [N_EXP, T])
        t = None
        for q in range(TT):
            t = self.stt(late[:, :], rank[:, q, :], float(CAP), gates[q][:, :], ALU.is_gt, ALU.mult, t)
            self.pe.wait(t)
            end = self.transposed(self.bank[4][0:N_EXP, 0:P], late[:, :], last=True)
            t = self.copy(self.dve, gates_T[:, q * P:(q + 1) * P], self.bank[4][0:N_EXP, 0:P], end)
        grow, act_, hid = self.gate_sb, self.silu, self.hid
        end = None
        for e in range(N_EXP):
            for n in range(3):
                self.sp.wait(end)
                self.sp.silent(lambda q, n=n, e=e: q.dma_start(buf[:, n, :], self.w_in[first_expert + 6 * (e // 2) + 2 * n + e % 2]).then_inc(load, 16))
            self.pe.wait(t, (load, 48 * (e + 1)))
            gb = self.mm_end(self.bank[6][:, 0:T], self.par("ident", e, 1, N_EXP).to_broadcast([N_EXP, P]), gates_T[:, :], True, True)
            t_g = self.copy(self.act, grow[:, 0, :], self.bank[6][:, 0:T], gb)
            for fc in range(2):
                ps = self.bank[4 + fc]
                for n in range(2):
                    for c in range(C):
                        a = (ps[:, n * T:(n + 1) * T], buf[:, n, c * FB + fc * P:c * FB + (fc + 1) * P], self.h[:, c, :], c == 0, c == C - 1)
                        up = self.mm_end(*a) if n and c == C - 1 else self.mm(*a)
                t = self.func(act_[:, fc, :], ps[:, 0:T], ACT.Silu, up, t_g)
                t = self.tt(self.dve, hid[:, fc, :], act_[:, fc, :], ps[:, T:2 * T], ALU.mult, t)
                t = self.tt(self.dve, hid[:, fc, :], hid[:, fc, :], grow[:, 0, :], ALU.mult, t)
                self.pe.wait(t)
                for c in range(C):
                    a = (self.bank[c // 2][:, (c % 2) * T:(c % 2 + 1) * T], buf[:, 2, fc * D + c * P:fc * D + (c + 1) * P], hid[:, fc, :], False, False, True)
                    end = self.mm_end(*a) if c == C - 1 else self.mm(*a)
        ends = [(q.sem, q.count) for q in queues[1:] if q.count]
        for q, (sem, count, seen) in zip(queues, saved):
            q.wait(*ends)
            q.leave_branch()
            q.sem, q.count, q.seen = sem, count, seen
        self.free = banks

    def conv_mixer(self, i):
        st, sb = self.stage()
        part = lambda n: self.mod[i][:, n * C:(n + 1) * C]
        h_toks = self.norm_x(self.gain[:, i, 0, :], part(0), self.mod_tok)
        K = 3
        b_T, u, g_T = sb("conv_b", [P, C, T]), sb("conv_u", [P, C, K - 1 + T]), sb("conv_gate", [P, 2, T])
        out, taps = sb("conv_out", [P, C, T]), sb("conv_taps", [P, 2, T])
        z = self.pool.do(lambda e: e.memset(u[:, :, 0:K - 1], 0.0))
        self.projection_buffers(st)
        h_toks = self.source(self.h, h_toks)
        self.h_free = h_toks[-1]
        gate_free, taps_free, toks = [None] * 2, [None] * 2, []
        tok = {}

        def consume(unit, ps, end):
            j, part_no, n = unit // 6, unit % 6 // 2, unit % 2
            c = 2 * j + n
            if part_no == 0:
                t = self.copy(self.act, b_T[:, c, :], ps, end)
            elif part_no == 1:
                t = self.copy(self.act, g_T[:, n, :], ps, end, gate_free[n])
            else:
                r = t = gate_free[n] = self.tt(self.dve, u[:, c, K - 1:], g_T[:, n, :], ps, ALU.mult, end, tok[1, n])
                t = self.ts(self.dve, taps[:, n, :], u[:, c, 0:T], self.par("conv0")[:, c:c + 1], None, ALU.mult, None, t, z, taps_free[n])
                for k in range(1, K):
                    t = self.stt(taps[:, n, :], u[:, c, k:k + T], self.par(f"conv{k}")[:, c:c + 1], taps[:, n, :], ALU.mult, ALU.add, t)
                t = self.tt(self.pool, out[:, c, :], taps[:, n, :], b_T[:, c, :], ALU.mult, t, tok[0, n])
                taps_free[n] = t
                toks.append(t)
                t = r
            tok[part_no, n] = t
            return t
        self.columns(h_toks, 12, consume)
        toks = self.source(out, toks)
        self.add_back(self.project_columns_out(toks), self.gain[:, i, 1, :], 1.0)
        st.close()
    def conv_chunk(self, out, src, taps, bias, c, n_taps, tok, out_free=None):
        w = lambda k: self.par(f"{taps}{k}")[:, c:c + 1]
        if bias is None:
            t = self.ts(self.dve, out, src[:, 0:T], w(0), None, ALU.mult, None, tok, out_free)
        else:
            t = self.ts(self.dve, out, src[:, 0:T], w(0), bias[:, c:c + 1], ALU.mult, ALU.add, tok, out_free)
        for k in range(1, n_taps):
            t = self.stt(out, src[:, k:k + T], w(k), out, ALU.mult, ALU.add, t)
        return t

    def softplus(self, v, tmp, tok):
        t = self.stt(tmp, v, -1.0, v, ALU.mult, ALU.max, tok)
        t = self.func(tmp, tmp, ACT.Exp, t, scale=-1.0)
        t = self.func(tmp, tmp, ACT.Ln, t, bias=self.par("ones", 0, 1))
        return self.stt(v, v, 0.0, tmp, ALU.max, ALU.add, t)

    def rotate(self, dst, src, tok, tmp, tmp_free):
        ps, b, fr = self.half()
        self.pe.wait(fr, tok)
        end = self.mm_end(ps, self.par("turn"), src, True, True)
        t = self.tt(self.dve, tmp, ps, self.par("sin"), ALU.mult, end, tmp_free)
        self.read_by(b, t)
        t2 = self.tt(self.pool, src, src, self.par("cos"), ALU.mult, end)
        return self.tt(self.dve, dst, src, tmp, ALU.add, t, t2)

    def nsa_ssd_mixer(self):
        st, sb = self.stage()
        K, G = 4, 2
        mix = sb("mix_in", [P, 12, T])
        silu_z = sb("silu_z", [P, C, T])
        xbc = sb("xbc", [P, 12, T])
        small = sb("gate_dt", [P, TT, 40])
        middle = ExitStack()
        m_sb = lambda n, s: middle.enter_context(self.nc.sbuf_tensor(f"{n}_{self.stage_no}", s, F32))
        qT, kv, v_tok = m_sb("q_T", [P, 4, T]), m_sb("kc_vc_ks_kw_T", [P, 4, T]), m_sb("vs_vw", [P, TT, T])
        outer = ExitStack()
        tmp_sb = lambda n, s: outer.enter_context(self.nc.sbuf_tensor(f"{n}_{self.stage_no}", s, F32))
        raw, taps = tmp_sb("xbc_raw", [P, 2, K - 1 + T]), tmp_sb("xbc_taps", [P, 2, T])
        z0 = self.pool.do(lambda e: e.memset(raw[:, :, 0:K - 1], 0.0))
        raw_free, taps_free, late = [None] * 2, [None] * 2, []

        def conv_in(c, ps, end):
            n = c % 2
            activate()
            t = self.copy(self.act, raw[:, n, K - 1:], ps, end, raw_free[n])
            raw_free[n] = self.conv_chunk(taps[:, n, :], raw[:, n, :], "ssd_conv", self.par("ssd_conv_b"), c, K, [t, z0], taps_free[n])
            late.append((n, xbc[:, c, :], raw_free[n]))
            return t

        def activate():
            while late:
                n, dst, tok = late.pop()
                taps_free[n] = self.func(dst, taps[:, n, :], ACT.Silu, tok)
        self.projection_buffers(outer)
        self.prepare(self.column_half, 2)
        h_toks = self.norm_x(self.par("a0_gain2"))
        hs = self.source(self.h, h_toks)
        self.columns(hs, 6, conv_in, self.column_half)
        activate()
        z_tok = [None] * C

        def z_in(c, ps, end):
            z_tok[c] = self.func(silu_z[:, c, :], ps, ACT.Silu, end)
            return z_tok[c]
        self.columns(hs, 4, z_in, self.column_half)
        small_tok = []
        for q in range(TT):
            ps, b, fr = self.half()
            self.pe.wait(fr, self.inputs)
            for c in range(C):
                a = (ps[:, 0:40], self.h[:, c, q * P:(q + 1) * P], self.par("w_gl_dt", c * 40, 40), c == 0, c == C - 1)
                end = self.mm_end(*a) if c == C - 1 else self.mm(*a)
            t = self.func(small[:, q, 0:24], ps[:, 0:24], ACT.Sigmoid, end)
            t2 = self.tt(self.dve, small[:, q, 24:40], ps[:, 24:40], self.par("dt_bias"), ALU.add, end, t)
            self.read_by(b, t2)
            small_tok.append([t, t2])
        rope_tok, v_done = self.attention_inputs(hs, qT, kv, v_tok, tmp_sb("rope_tmp", [P, 2, T]))
        self.barrier()
        outer.close()
        self.attention(mix, small, qT, kv, v_tok, rope_tok, v_done)
        self.barrier()
        middle.close()
        self.projection_buffers(st, 12)
        self.prepare(self.row_half, 2)
        self.ssd(mix, small, xbc, silu_z)
        toks = self.source(mix, [(self.dve.sem, self.dve.count)] * 12, 12)
        self.h_free = (self.pe.sem, self.pe.count)
        self.add_back(self.project_out(12, toks), self.par("a0_gain3"), 1.0)
        st.close()

    def attention_inputs(self, hs, qT, kv, v_tok, tmp):
        tmp_free, rope_tok, n_rope = [None] * 2, {}, [0]

        def rope_into(dst, name):
            def consume(c, ps, end):
                t = self.copy(self.act, dst[:, c, :], ps, end)
                if name == "q" or c != 1:
                    n = n_rope[0] % 2
                    n_rope[0] += 1
                    rope_tok[name, c] = tmp_free[n] = self.rotate(dst[:, c, :], dst[:, c, :], t, tmp[:, n, :], tmp_free[n])
                else:
                    rope_tok[name, c] = t
                return t
            return consume
        self.columns(hs, 2, rope_into(qT, "q"), self.column_half)
        self.columns(hs, 2, rope_into(kv, "kv"))
        i, w, tok = self.slot()
        v_done = []
        self.pe.wait(tok)
        for q in range(TT):
            ps, b, fr = self.half()
            self.pe.wait(fr)
            for c in range(C):
                a = (ps, self.h[:, c, q * P:(q + 1) * P], w[:, c * FB:(c + 1) * FB], c == 0, c == C - 1)
                end = self.mm_end(*a) if c == C - 1 else self.mm(*a)
            v_done.append(self.copy(self.act, v_tok[:, q, :], ps, end))
            self.read_by(b, v_done[-1])
        self.slot_read(i, end)
        return rope_tok, v_done

    def attention(self, mix, small, qT, kv, v_tok, rope_tok, v_done):
        st = ExitStack()
        sb = lambda n, s: st.enter_context(self.nc.sbuf_tensor(f"{n}_{self.stage_no}", s, F32))
        n_cmp = 15
        hid = sb("cmp_hidden", [64, 2, 2, n_cmp])
        bias = sb("cmp_bias", [64, 2])
        windows = sb("cmp_windows", [P, 2, 32, n_cmp + 1])
        k_cmp, v_cmp = sb("k_cmp", [P, n_cmp]), sb("v_cmp", [n_cmp, P])
        cmp_tok = []
        for n, (name, chunk) in enumerate((("k", 0), ("v", 1))):
            i, w, tok = self.slot()
            win = windows[:, n, :, :]
            t = None
            for l in range(0, 32, 16):
                src = kv[:, chunk, l:l + 16 * n_cmp].rearrange("p (n l) -> p l n", l=16)
                t = self.copy(self.dve, win[:, l:l + 16, 0:n_cmp], src, rope_tok["kv", chunk])
            t = self.copy(self.dve, win[0:64, :, n_cmp:n_cmp + 1], self.par(f"cmp_pe_{name}", 0, 32, 64).unsqueeze(2), self.inputs)
            self.pe.wait(tok, t)
            banks = [self.half() for _ in range(2)]
            for l in range(32):
                for g, (ps, b, fr) in enumerate(banks):
                    base, wide = slice(g * 64, g * 64 + 64), n_cmp + 1 - g
                    self.pe.wait(fr)
                    a = (ps[0:64, 0:wide], w[base, l * 64:(l + 1) * 64], win[base, l, 0:wide], l == 0, l == 31)
                    end = self.mm_end(*a) if l == 31 else self.mm(*a)
            self.slot_read(i, end)
            for g, (ps, b, fr) in enumerate(banks):
                if g == 0:
                    t = tb = self.copy(self.dve, bias[:, n:n + 1], ps[0:64, n_cmp:n_cmp + 1], end)
                t = self.func(hid[:, n, g, :], ps[0:64, 0:n_cmp], ACT.Silu, end, tb, bias=bias[:, n:n + 1])
                self.read_by(b, t)
            ps, b, fr = self.half()
            self.pe.wait(fr, t)
            w2 = self.par(f"cmp_w2_{name}", rows=64)
            for g in range(2):
                if n == 0:
                    end = self.mm_end(ps[g * 64:g * 64 + 64, 0:n_cmp], w2, hid[:, n, g, :], True, True)
                else:
                    end = self.mm_end(ps[0:n_cmp, g * 64:g * 64 + 64], hid[:, n, g, :], w2, True, True)
            t = self.copy(self.dve, k_cmp[:, :] if n == 0 else v_cmp[:, :], ps[:, 0:n_cmp] if n == 0 else ps[0:n_cmp, 0:P], end)
            self.read_by(b, t)
            cmp_tok.append(t)
        all_rope = [rope_tok["q", c] for c in range(4)] + [rope_tok["kv", 2], rope_tok["kv", 3]]
        scale = 64.0 ** -0.5
        NB = 4
        p_buf = sb("probs", [P, NB, 4, T])
        pT = sb("probs_T", [P, NB, 8, P])
        stat = sb("softmax_stats", [P, NB, 12])
        pc, pcT, cs = sb("cmp_probs", [P, 8, n_cmp]), sb("cmp_probs_T", [n_cmp, 8, P]), sb("cmp_stats", [P, 3, 8])
        p_free, pT_free, pc_free, pcT_free = [None] * NB, [None] * NB, None, None
        out_free = None
        for q in range(TT):
            tq = slice(q * P, (q + 1) * P)
            nk = (q + 1) * P
            t = None
            for half in range(2):
                ps, b, fr = self.half()
                self.pe.wait(fr, all_rope, cmp_tok)
                base = slice(half * 64, half * 64 + 64)
                for j in range(4):
                    end = self.mm_end(ps[:, j * 16:j * 16 + n_cmp], qT[base, j, tq], k_cmp[base, :], True, True)
                add = self.par(f"cmp_add{q}").rearrange("p (h c) -> p h c", h=8)[:, 0:4, :]
                t = self.tt(self.dve, pc[:, half * 4:half * 4 + 4, :], ps[:, 0:64].rearrange("p (h c) -> p h c", h=4)[:, :, 0:n_cmp],
                            add, ALU.add, end, pc_free)
                self.read_by(b, t)
            mx, sm, sc = cs[:, 0, :], cs[:, 1, :], cs[:, 2, :]
            bc = lambda a: a.unsqueeze(2).to_broadcast([P, 8, n_cmp])
            t = self.reduce(mx, pc[:, :, :], ALU.max, t)
            t = self.tt(self.dve, pc[:, :, :], pc[:, :, :], bc(mx), ALU.subtract, t)
            t = self.func(pc[:, :, :], pc[:, :, :], ACT.Exp, t, scale=scale)
            t = self.tt(self.dve, pc[:, :, :], pc[:, :, :], self.par(f"cmp_keep{q}").rearrange("p (h c) -> p h c", h=8), ALU.mult, t)
            t = self.reduce(sm, pc[:, :, :], ALU.add, t)
            t = self.ts(self.dve, sm, sm, 1e-30, None, ALU.max, None, t)
            t = self.dve.do(lambda e: e.reciprocal(sc, sm), t)
            t = self.tt(self.dve, sc, sc, small[:, q, 0:24:3], ALU.mult, t)
            t = self.tt(self.dve, pc[:, :, :], pc[:, :, :], bc(sc), ALU.mult, t)
            for n in range(2):
                ps, b, fr = self.full()
                self.pe.wait(fr, t)
                for m in range(4):
                    end = self.transposed(ps[0:n_cmp, m * P:(m + 1) * P], pc[:, 4 * n + m, :], last=m == 3)
                tc = self.copy(self.act, pcT[:, 4 * n:4 * n + 4, :], ps[0:n_cmp, :].rearrange("c (m t) -> c m t", m=4), end, pcT_free)
                self.read_by(b, tc)
            pc_free = end
            o_bank = q
            self.pe.wait(self.free.get(o_bank), out_free)
            ends = {}

            def pair(j, n):
                v4 = lambda a: a.rearrange("p (h m) k -> p h m k", h=2)
                pb, s = p_buf[:, n, :, 0:nk], stat[:, n, :]
                mask = self.par(f"causal{q}", 0, nk).unsqueeze(1).to_broadcast([P, 2, nk])
                banks = [self.full() for _ in range(2)]
                for m in range(2):
                    for half, (ps, b, fr) in enumerate(banks):
                        base = slice(half * 64, half * 64 + 64)
                        self.pe.wait(fr)
                        end = self.mm_end(ps[:, m * T:m * T + nk], qT[base, j, tq], kv[base, 2 + m, 0:nk], True, True)
                for half, (ps, b, fr) in enumerate(banks):
                    view = ps[:, :].rearrange("p (m k) -> p m k", m=2)[:, :, 0:nk]
                    t = self.tt(self.dve, p_buf[:, n, 2 * half:2 * half + 2, 0:nk], view, mask, ALU.add, end, p_free[n])
                    self.read_by(b, t)
                t = self.reduce(s[:, 0:4], pb, ALU.max, t)
                t = self.ts(self.dve, s[:, 0:4], s[:, 0:4], -scale, None, ALU.mult, None, t)
                for m in range(4):
                    te = self.func(p_buf[:, n, m, 0:nk], p_buf[:, n, m, 0:nk], ACT.Exp, t, scale=scale, bias=s[:, m:m + 1], accum=s[:, 4 + m:5 + m])
                yield
                t = self.dve.do(lambda e: e.reciprocal(s[:, 8:12], s[:, 4:8]), te)
                for half in range(2):
                    h = 4 * half + j
                    t = self.tt(self.dve, s[:, 8 + 2 * half:10 + 2 * half], s[:, 8 + 2 * half:10 + 2 * half], small[:, q, 3 * h + 1:3 * h + 3], ALU.mult, t)
                t = self.tt(self.dve, pb, pb, s[:, 8:12].unsqueeze(2).to_broadcast([P, 4, nk]), ALU.mult, t)
                yield
                cuts = [(x, kt) for x in range(4) for kt in range(q + 1)]
                for g in range(q + 1):
                    ps, b, fr = self.full()
                    self.pe.wait(fr, t)
                    for y in range(4):
                        x, kt = cuts[4 * g + y]
                        end = self.transposed(ps[:, y * P:(y + 1) * P], p_buf[:, n, x, kt * P:(kt + 1) * P], last=y == 3)
                    tp = self.copy(self.act, pT[:, n, 4 * g:4 * g + 4, :], ps[:, :].rearrange("p (x t) -> p x t", t=P), end, pT_free[n])
                    self.read_by(b, tp)
                p_free[n] = end
                yield
                self.pe.wait(tc, tp, v_done)
                o = [self.bank[o_bank][half * 64:half * 64 + 64, j * P:(j + 1) * P] for half in range(2)]
                for half in range(2):
                    self.mm(o[half], v_cmp[:, half * 64:half * 64 + 64], pcT[:, half * 4 + j, :], True, False)
                per = len(cuts) // 2
                for y in range(per):
                    for half in range(2):
                        x, kt = cuts[half * per + y]
                        m = x % 2
                        a = (o[half], v_tok[:, kt, m * P + half * 64:m * P + half * 64 + 64], pT[:, n, half * per + y, :], False, y == per - 1)
                        end = self.mm_end(*a) if y == per - 1 else self.mm(*a)
                pT_free[n] = ends["last"] = end
            self.pipeline((pair(j, j % NB) for j in range(4)), NB)
            end = ends["last"]
            pcT_free = end
            t = self.copy(self.dve, mix[:, 0:4, tq], self.bank[o_bank][:, :].rearrange("p (j t) -> p j t", j=4), end)
            self.read_by(o_bank, t)
        st.close()

    def ssd(self, mix, small, xbc, silu_z):
        st = ExitStack()
        sb = lambda n, s: st.enter_context(self.nc.sbuf_tensor(f"{n}_{self.stage_no}", s, F32))
        H, N4 = 16, 4
        dt, dA, acs, tmp = small[:, :, 24:40], sb("dA", [P, TT, H]), sb("a_cumsum", [P, TT, H]), sb("dt_tmp", [P, TT, H])
        t = self.softplus(dt, tmp[:, :, :], None)
        tmp2 = sb("a_rate", [P, H])
        ta = self.func(tmp2[:, :], self.par("a_log"), ACT.Exp, self.inputs)
        for q in range(TT):
            t = self.stt(dA[:, q, :], tmp2[:, :], -1.0, small[:, q, 24:40], ALU.mult, ALU.mult, t, ta)
        ps, b, fr = self.half()
        self.pe.wait(fr, t)
        for q in range(TT):
            self.mm(ps[:, q * H:(q + 1) * H], self.par("upto"), dA[:, q, :], True, True)
        end = self.mm_end(ps[:, 32:32 + H], self.par("ones"), dA[:, 0, :], True, True)
        t = self.copy(self.dve, acs[:, :, :], ps[:, 0:32].rearrange("p (q h) -> p q h", q=TT), end)
        dec = sb("decay_to_end", [P, H])
        t = self.tt(self.dve, dec[:, :], ps[:, 32:32 + H], acs[:, 0, :], ALU.subtract, t)
        self.read_by(b, t)
        acs_tok = t
        t_dec = self.func(dec[:, :], dec[:, :], ACT.Exp, t)
        xd = sb("x_dt", [P, TT, D])
        spare = self.y[:, :, :].rearrange("p c t -> p (c t)")
        xdd, b_tok = spare[:, 0:D], spare[:, D:D + 2 * P].rearrange("p (g n) -> p g n", g=2)
        xd_tok = []
        for q in range(TT):
            for n in range(2):
                ps, b, fr = self.full()
                self.pe.wait(fr)
                for m in range(4):
                    end = self.transposed(ps[:, m * P:(m + 1) * P], xbc[:, 4 * n + m, q * P:(q + 1) * P], last=m == 3)
                t = self.tt(self.dve, xd[:, q, 512 * n:512 * n + 512].rearrange("p (h d) -> p h d", h=8), ps[:, :].rearrange("p (h d) -> p h d", h=8),
                            small[:, q, 24 + 8 * n:32 + 8 * n].unsqueeze(2).to_broadcast([P, 8, 64]), ALU.mult, end, acs_tok)
                self.read_by(b, t)
                xd_tok.append(t)
        t_xdd = self.tt(self.dve, xdd[:, :].rearrange("p (h d) -> p h d", h=H), xd[:, 0, :].rearrange("p (h d) -> p h d", h=H),
                        dec[:, :].unsqueeze(2).to_broadcast([P, H, 64]), ALU.mult, xd_tok, t_dec, self.y_free)
        ps, b, fr = self.half()
        self.pe.wait(fr)
        for g in range(2):
            end = self.transposed(ps[:, g * P:(g + 1) * P], xbc[:, 8 + g, 0:P], last=True)
        t_b = self.copy(self.act, b_tok[:, :, :], ps.rearrange("p (g n) -> p g n", g=2), end, self.y_free)
        self.read_by(b, t_b)
        state = sb("state_T", [P, 2, 512])
        for g in range(2):
            ps, b, fr = self.full()
            self.pe.wait(fr, t_b, t_xdd)
            end = self.mm_end(ps[:, :], b_tok[:, g, :], xdd[:, g * 512:(g + 1) * 512], True, True)
            t_state = self.copy(self.act, state[:, g, :], ps[:, :], end)
            self.read_by(b, t_state)
        NB = 3
        cb = spare[:, D + 2 * P:D + 4 * P].rearrange("p (g n) -> p g n", g=2)
        seg, grow = sb("seg_T", [P, NB, N4, P]), sb("C_grown", [P, NB, N4, P])
        cb_free, seg_free, cb_tok = [None] * 2, [None] * NB, {}

        def four_heads(q, g, r4, s):
            tq = slice(q * P, (q + 1) * P)
            n_cb, h0 = g, 8 * g + 4 * r4
            if r4 == 0:
                ps, b, fr = self.half()
                self.pe.wait(fr)
                end = self.mm_end(ps[:, 0:P], xbc[:, 8 + g, tq], xbc[:, 10 + g, tq], True, True)
                cb_tok[g] = self.tt(self.dve, cb[:, n_cb, :], ps[:, 0:P], self.par("upto"), ALU.mult, end, cb_free[n_cb])
                self.read_by(b, cb_tok[g])
            ps, b, fr = self.full()
            self.pe.wait(fr, acs_tok)
            for m in range(N4):
                end = self.mm_end(ps[:, m * P:(m + 1) * P], dA[:, q, h0 + m:h0 + m + 1].to_broadcast([P, P]), self.par("upto"), True, True)
            v = ps[:, :].rearrange("p (m t) -> p m t", m=N4)
            t = self.tt(self.dve, seg[:, s, :, :], v, acs[:, q, h0:h0 + N4].unsqueeze(2).to_broadcast([P, N4, P]), ALU.subtract, end, seg_free[s], acs_tok)
            t_g = None
            if q > 0:
                t_g = self.func(grow[:, s, :, :], v, ACT.Exp, end, t)
                self.read_by(b, t_g)
                t_g = self.tt(self.pool, grow[:, s, :, :], grow[:, s, :, :], xbc[:, 10 + g, tq].unsqueeze(1).to_broadcast([P, N4, P]), ALU.mult, t_g)
            else:
                self.read_by(b, t)
            t = self.ts(self.dve, seg[:, s, :, :], seg[:, s, :, :], 0.0, None, ALU.min, None, t)
            t = self.func(seg[:, s, :, :], seg[:, s, :, :], ACT.Exp, t)
            yield
            t = self.tt(self.dve, seg[:, s, :, :], seg[:, s, :, :], cb[:, n_cb, :].unsqueeze(1).to_broadcast([P, N4, P]), ALU.mult, t, cb_tok[g])
            cb_free[n_cb] = t
            yield
            yb, b, fr = self.half()
            self.pe.wait(fr, t, t_g, t_state if q else None, xd_tok)
            for m in range(0, N4, 2):
                o = [yb[n * 64:n * 64 + 64, (m // 2) * P:(m // 2 + 1) * P] for n in range(2)]
                for n in range(2):
                    h = h0 + m + n
                    end = self.mm_end(o[n], xd[:, q, h * 64:(h + 1) * 64], seg[:, s, m + n, :], True, not q)
                if q:
                    for n in range(2):
                        h = h0 + m + n
                        end = self.mm_end(o[n], state[:, g, (h % 8) * 64:(h % 8 + 1) * 64], grow[:, s, m + n, :], False, True)
            seg_free[s] = end
            for k in range(2):
                c = h0 // 2 + k
                t = self.stt(mix[:, 4 + c, tq], xbc[:, c, tq], self.par("d_skip")[:, c:c + 1], yb[:, k * P:(k + 1) * P], ALU.mult, ALU.add, end)
            self.read_by(b, t)
        self.pipeline((four_heads(n // 4, n // 2 % 2, n % 2, n % NB) for n in range(8)), NB)
        t = (self.dve.sem, self.dve.count)
        sq = self.y
        sq_tok = []
        for c in range(C):
            t1 = self.tt(self.dve, mix[:, 4 + c, :], mix[:, 4 + c, :], silu_z[:, c, :], ALU.mult, t)
            sq_tok.append(self.func(sq[:, c, :], mix[:, 4 + c, :], ACT.Square, t1, self.y_free))
        for g in range(2):
            r = self.inv_rms([sq[:, 4 * g + c, :] for c in range(4)], 512, 1e-5, sq_tok[4 * g:4 * g + 4], out=self.rms[:, g, :])
            for c in range(4 * g, 4 * g + 4):
                t = self.stt(mix[:, 4 + c, :], mix[:, 4 + c, :], self.par("ssd_norm")[:, c:c + 1], self.rms[:, g, :], ALU.mult, ALU.mult, r)
        self.y_free = (self.pe.sem, self.pe.count)
        self.rms_free = t
        self.barrier()
        st.close()

    def invert(self, buf, nt, tok, levels):
        t_, tt, x, nl = buf["t"], buf["tt"], buf["x"], buf["nl"]
        four = lambda a: a.unsqueeze(1).to_broadcast([P, 4, P])
        as4 = lambda ps: ps[:, :].rearrange("p (m t) -> p m t", m=4)
        k = self.tt(self.dve, nl[:, :, :], nt, four(self.par("level1")), ALU.mult, tok, buf["nl_free"])
        t_tt = self.tt(self.dve, tt[:, :, :], four(self.par("ident")), nl[:, :, :], ALU.subtract, k, buf["tt_free"])
        ps, b, fr = self.full()
        self.pe.wait(fr, t_tt)
        for m in range(4):
            end = self.transposed(ps[:, m * P:(m + 1) * P], tt[:, m, :], last=m == 3)
        t_t = self.copy(self.act, t_[:, :, :], as4(ps), end, buf["x_free"])
        self.read_by(b, t_t)
        x_free, nl_free = buf["x_free"], t_tt
        for l in levels[1:]:
            t_nl = self.tt(self.pool, nl[:, :, :], nt, four(self.par(f"level{l}")), ALU.mult, nl_free, tok)
            yield
            ps, b, fr = self.full()
            self.pe.wait(fr, t_nl, t_t)
            for m in range(4):
                a = (ps[:, m * P:(m + 1) * P], nl[:, m, :], t_[:, m, :], True, True)
                end = self.mm_end(*a) if m == 3 else self.mm(*a)
            nl_free = end
            t_x = self.copy(self.act, x[:, :, :], as4(ps), end, x_free)
            self.read_by(b, t_x)
            yield
            last = l == levels[-1]
            ps, b, fr = self.full()
            self.pe.wait(fr, t_x, t_tt)
            for m in range(4):
                a = (ps[:, m * P:(m + 1) * P], x[:, m, :], tt[:, m, :], True, True)
                end = self.mm_end(*a) if m == 3 else self.mm(*a)
            if not last:
                ps2, b2, fr = self.full()
                self.pe.wait(fr)
                for m in range(4):
                    a = (ps2[:, m * P:(m + 1) * P], tt[:, m, :], x[:, m, :], True, True)
                    end2 = self.mm_end(*a) if m == 3 else self.mm(*a)
                t_t = self.tt(self.dve, t_[:, :, :], t_[:, :, :], as4(ps2), ALU.subtract, end2, t_t)
                self.read_by(b2, t_t)
                end = end2
            t_tt = self.tt(self.dve, tt[:, :, :], tt[:, :, :], as4(ps), ALU.subtract, end)
            self.read_by(b, t_tt)
            x_free = end
        buf["x_free"] = buf["nl_free"] = (self.pe.sem, self.pe.count)
        buf["done"] = t_tt

    def pipeline(self, generators, depth):
        waiting, running = iter(generators), []
        more = True
        while more or running:
            self.background()
            for g in list(running):
                if next(g, True):
                    running.remove(g)
            if more and len(running) < depth:
                g = next(waiting, None)
                more = g is not None
                if more and not next(g, True):
                    running.append(g)

    def interleave(self, *generators):
        left = list(generators)
        while left:
            self.background()
            for g in list(left):
                if next(g, True):
                    left.remove(g)

    def rwkv_mixer(self):
        st, sb = self.stage()
        h_toks = self.norm_x(self.par("a1_gain2"))
        r, k, v, sg, a = (sb(n, [P, C, T]) for n in ("r", "k", "v", "decay", "a"))
        g_hid = sb("gate_hidden", [P, 2, T])
        pend = sb("chunk_decay", [P, C, 4])
        inner = ExitStack()
        isb = lambda n, s: inner.enter_context(self.nc.sbuf_tensor(f"{n}_{self.stage_no}", s, F32))
        xx, m0, m1 = isb("x_shifted", [P, C, T]), isb("mixed0", [P, C, T]), isb("mixed1", [P, C, T])
        hw = isb("lora_hidden", [P, 2, T])
        self.projection_buffers(inner, depth=2)
        h, y = self.h, self.y
        t = self.tt(self.dve, xx[:, :, 1:], h[:, :, 0:T - 1], h[:, :, 1:], ALU.subtract, h_toks)
        t = self.ts(self.dve, xx[:, :, 0:1], h[:, :, 0:1], -1.0, None, ALU.mult, None, t)
        mixed, m_free = [m0, m1], [None, None]
        turn = [0]

        def mix(n):
            i = turn[0] % 2
            turn[0] += 1
            toks = [self.stt(mixed[i][:, c, :], xx[:, c, :], self.par(f"mu{n}")[:, c:c + 1], h[:, c, :], ALU.mult, ALU.add, t, m_free[i])
                    for c in range(C)]
            return i, mixed[i], toks

        s1, w1, tok1 = self.slot()
        s2, g1, tok2 = self.slot()
        hid_tok = []
        for n, (mu, w, tok, lo, m, fn) in enumerate(((1, w1, tok1, 0, 64, ACT.Tanh), (4, w1, tok1, 64, 64, ACT.Copy),
                                                     (5, g1, tok2, 0, 128, ACT.Sigmoid), (5, g1, tok2, 128, 32, ACT.Sigmoid))):
            if n < 3:
                i, src, toks = mix(mu)
            ps, b, fr = self.half()
            self.pe.wait(fr, tok, toks)
            for c in range(C):
                args = (ps[0:m, :], w[:, c * FB + lo:c * FB + lo + m], src[:, c, :], c == 0, c == C - 1)
                end = self.mm_end(*args) if c == C - 1 else self.mm(*args)
            m_free[i] = end
            hid_tok.append(self.func((hw if n < 2 else g_hid)[0:m, n % 2, :], ps[0:m, :], fn, end))
            self.read_by(b, hid_tok[-1])
            if n in (1, 3):
                self.slot_read(s1 if n == 1 else s2, end)
        for n, (dst, bias) in enumerate(((sg, "w0"), (a, "a0"))):
            if n == 0:
                s1, w, tok = self.slot()
            for c in range(C):
                ps, b, fr = self.half()
                self.pe.wait(fr, tok, hid_tok[n])
                end = self.mm_end(ps, w[0:64, n * D + c * P:n * D + (c + 1) * P], hw[0:64, n, :], True, True)
                t2 = self.func(dst[:, c, :], ps, ACT.Sigmoid, end, bias=self.par(bias)[:, c:c + 1])
                self.read_by(b, t2)
        self.slot_read(s1, end)
        for mu, dst in ((0, r), (2, k), (3, v)):
            i, src, toks = mix(mu)
            toks = self.source(src, toks)
            m_free[i] = toks[-1]

            def consume(c, ps, end, dst=dst):
                return self.copy(self.act, dst[:, c, :], ps, end)
            self.columns(toks, 4, consume, None if mu == 3 else self.column_half)
        self.barrier()
        self.filler = self.both_modulations()
        self.background(5)
        kappa = float(np.exp(-0.5))
        gs, kk, t3, t4 = m0, m1, xx, y
        for c in range(C):
            t_gs = self.dve.do(lambda e, c=c: e.tensor_tensor_scan(gs[:, c, :], self.par("not_first64"), sg[:, c, :], 0.0, ALU.mult, ALU.add))
            t_kk = self.ts(self.dve, kk[:, c, :], k[:, c, :], self.par("k_k")[:, c:c + 1], None, ALU.mult, None)
        al = lambda x: x[:, :, :]
        t = self.tt(self.pool, al(t4), al(gs), al(sg), ALU.subtract, t_gs)
        t_pprev = self.func(al(t4), al(t4), ACT.Exp, t, scale=-kappa)
        t = self.func(al(t3), al(kk), ACT.Square, t_kk)

        def head_sums(src, tok, use):
            out = []
            for n in range(4):
                ps, b, fr = self.full()
                self.pe.wait(fr, tok)
                end = self.mm_end(ps[:, :], self.par("half_ones"), src[:, 2 * n:2 * n + 2, :], True, True)
                t = use(n, ps[:, :].rearrange("p (c t) -> p c t", c=2), end)
                self.read_by(b, t)
                out.append(t)
            return out
        t = head_sums(t3, t, lambda n, ps, end: self.ts(self.dve, t3[:, 2 * n:2 * n + 2, :], ps, 1e-24, None, ALU.max, None, end))
        t = self.func(al(t3), al(t3), ACT.Ln, t, scale=65536.0)
        t = self.func(al(t3), al(t3), ACT.Exp, t, scale=-0.5)
        self.background(5)
        t_kk = self.stt(al(kk), al(kk), 256.0, al(t3), ALU.mult, ALU.mult, t, t_kk)
        t_A = self.stt(al(sg), al(kk), -1.0, al(t4), ALU.mult, ALU.mult, t_kk, t_pprev)
        one_less = isb("one_less_ka", [P, C])
        t = self.ts(self.dve, one_less[:, :], self.par("k_a"), -1.0, 1.0, ALU.mult, ALU.add)
        for c in range(C):
            t1 = self.ts(self.dve, t3[:, c, :], a[:, c, :], self.par("k_a")[:, c:c + 1], one_less[:, c:c + 1], ALU.mult, ALU.add, t, t_kk)
        t_k = self.tt(self.dve, al(k), al(k), al(t3), ALU.mult, t1)
        t_b = self.tt(self.pool, al(a), al(kk), al(a), ALU.mult, t1, t_kk)
        t = self.tt(self.dve, al(t3), al(r), al(k), ALU.mult, t_k)
        for c in range(C):
            t1 = self.ts(self.dve, t3[:, c, :], t3[:, c, :], self.par("r_k")[:, c:c + 1], None, ALU.mult, None, t)
        t_bonus = head_sums(t3, t1, lambda n, ps, end: self.tt(self.dve, h[:, 2 * n:2 * n + 2, :], v[:, 2 * n:2 * n + 2, :], ps, ALU.mult, end))
        t = self.func(al(t4), al(gs), ACT.Exp, t_A, scale=kappa)
        t_B = self.tt(self.pool, al(a), al(a), al(t4), ALU.mult, t, t_b)
        t_K = self.tt(self.dve, al(k), al(k), al(t4), ALU.mult, t, t_bonus)
        t = self.func(al(t3), al(gs), ACT.Exp, t_bonus, t_K, scale=-kappa)
        self.background(2)
        t_R = self.tt(self.dve, al(r), al(r), al(t3), ALU.mult, t)
        self.copy(self.dve, pend[:, :, :], t3[:, :, 63:T:64], t)
        self.barrier()
        inner.close()
        A, B, K, R = sg, a, k, r
        inner = ExitStack()
        isb = lambda n, s: inner.enter_context(self.nc.sbuf_tensor(f"{n}_{self.stage_no}", s, F32))
        tokT = {n: isb(f"{n}_tokens", [P, 4, P]) for n in "BKV"}
        bufs = []
        for par in range(2):
            bufs.append({n: isb(f"{n}{par}", [P, 4, P]) for n in ("nt", "rb", "rk", "t", "tt", "x", "nl")})
            bufs[par].update(x_free=None, nl_free=None, tt_free=None)
        lv, S = isb("LakV", [P, 4, P]), [isb(f"state{i}", [P, 4, P]) for i in range(2)]
        U = isb("U", [P, 4, P])
        U_half, V_half, R_half = ([isb(f"{n}_half{i}", [P, 4, P]) for i in range(2)] for n in "UVR")
        W, Stmp = isb("W", [P, 4, P]), isb("state_sum", [P, 4, P])
        for i in range(2):
            self.pool.do(lambda e, i=i: e.memset(U_half[i][:, :, :], 0.0))
        rows_of = lambda i: self.par("half_ones", 64 * i, 1)
        cols_of = lambda i: self.par("cols_half", P * i, P).unsqueeze(1).to_broadcast([P, 4, P])
        as4 = lambda ps: ps[:, :].rearrange("p (m t) -> p m t", m=4)
        four = lambda m: m.unsqueeze(1).to_broadcast([P, 4, P])
        for sg_ in range(2):
            ch = lambda m: 4 * sg_ + m
            for q in range(TT):
                tq = slice(q * P, (q + 1) * P)
                self.barrier()
                for n, src in (("B", B), ("K", K), ("V", v)):
                    ps, b, fr = self.full()
                    self.pe.wait(fr)
                    for m in range(4):
                        end = self.transposed(ps[:, m * P:(m + 1) * P], src[:, ch(m), tq], last=m == 3)
                    t_tok = self.copy(self.act, tokT[n][:, :, :], as4(ps), end)
                    self.read_by(b, t_tok)
                half_tok = [self.ts(self.pool, V_half[i][:, :, :], tokT["V"][:, :, :], rows_of(i), None, ALU.mult, None, t_tok) for i in range(2)]
                half_tok += [self.tt(self.pool, R_half[i][:, :, :], R[:, 4 * sg_:4 * sg_ + 4, tq], cols_of(i), ALU.mult) for i in range(2)]
                lak_tok = []
                for par in range(2):
                    bf = bufs[par]
                    m_tok = [self.ts(self.dve, bf[n][:, :, :], L[:, 4 * sg_:4 * sg_ + 4, tq], rows_of(par), None, ALU.mult, None)
                             for n, L in (("t", B), ("x", K))]
                    for dst, L, Rh, mask, sign in (("nt", "t", A, "before64", -1.0), ("nl", "x", A, "before64", 1.0),
                                                   ("rb", "t", R, "upto64", 1.0), ("rk", "x", R, "upto64", 1.0)):
                        ps, b, fr = self.full()
                        self.pe.wait(fr, m_tok)
                        for m in range(4):
                            end = self.mm_end(ps[:, m * P:(m + 1) * P], bf[L][:, m, :], Rh[:, ch(m), tq], True, True)
                        bf["x_free"] = end
                        t = self.stt(bf[dst][:, :, :], as4(ps), sign, four(self.par(mask)), ALU.mult, ALU.mult, end)
                        self.read_by(b, t)
                        if dst == "nt":
                            bf["nt_tok"] = t
                        if dst == "nl":
                            lak_tok.append(t)
                for par in range(2):
                    ps, b, fr = self.full()
                    self.pe.wait(fr, lak_tok, t_tok)
                    for m in range(4):
                        end = self.mm_end(ps[:, m * P:(m + 1) * P], bufs[par]["nl"][:, m, :], tokT["V"][:, m, :], True, True)
                    f = slice(par * 64, par * 64 + 64)
                    t_lv = self.copy(self.act, lv[:, :, f], as4(ps)[:, :, f], end)
                    self.read_by(b, t_lv)
                    bufs[par]["nl_free"] = end
                    bufs[par]["tt_free"] = None
                self.interleave(*(self.invert(bf, bf["nt"][:, :, :], bf["nt_tok"], (1, 2, 4, 8, 16, 32)) for bf in bufs))
                inv = [bf["done"] for bf in bufs] + [bufs[0]["x_free"], bufs[1]["x_free"]]
                for j in (2 * q, 2 * q + 1):
                    self.background(2)
                    rows = slice((j % 2) * 64, (j % 2) * 64 + 64)
                    s_now, s_next = S[j % 2], S[(j + 1) % 2]
                    if j == 0:
                        w_src, t_w = lv, t_lv
                    else:
                        ps, b, fr = self.full()
                        self.pe.wait(fr, t_s, inv)
                        for m in range(4):
                            end = self.mm_end(ps[:, m * P:(m + 1) * P], A[:, ch(m), tq], s_now[:, m, :], True, True)
                        w_src = W
                        t_w = self.tt(self.dve, W[:, :, :], lv[:, :, :], as4(ps), ALU.add, end, inv, t_lv)
                        self.read_by(b, t_w)
                    t_u = []
                    for par in range(2):
                        ps, b, fr = self.full()
                        self.pe.wait(fr, t_w, inv)
                        for m in range(4):
                            end = self.mm_end(ps[:, m * P:(m + 1) * P], bufs[par]["tt"][:, m, :], w_src[:, m, :], True, True)
                        o = slice(par * 64, par * 64 + 64)
                        t = self.copy(self.act, U_half[j % 2][rows, :, o], as4(ps)[rows, :, o], end)
                        self.read_by(b, t)
                        t_u += [t, self.copy(self.pool, U[rows, :, o], U_half[j % 2][rows, :, o], t)]
                    if j < 3:
                        ps, b, fr = self.full()
                        self.pe.wait(fr, t_u, half_tok)
                        for m in range(4):
                            o = ps[:, m * P:(m + 1) * P]
                            self.mm(o, tokT["B"][:, m, :], U_half[j % 2][:, m, :], True, False)
                            end = self.mm_end(o, tokT["K"][:, m, :], V_half[j % 2][:, m, :], False, True)
                        t = self.tt(self.dve, Stmp[:, :, :], as4(ps), four(self.par("half_ones")), ALU.mult, end, inv)
                        self.read_by(b, t)
                        if j > 0:
                            t = self.tt(self.dve, Stmp[:, :, :], Stmp[:, :, :], s_now[:, :, :], ALU.add, t, t_s)
                        t_new = (t, j)
                    if j % 2:
                        ps, b, fr = self.full()
                        self.pe.wait(fr, t_u, half_tok)
                        for m in range(4):
                            o = ps[:, m * P:(m + 1) * P]
                            first = True
                            for i in (2 * q, j):
                                if i:
                                    self.mm(o, S[i % 2][:, m, :], R_half[i % 2][:, m, :], first, False, True)
                                    first = False
                            for par in range(2):
                                f = slice(par * 64, par * 64 + 64)
                                self.mm(o[f], U[:, m, f], bufs[par]["rb"][:, m, :], False, False, True)
                                end = self.mm_end(o[f], tokT["V"][:, m, f], bufs[par]["rk"][:, m, :], False, par == 1, True)
                        t_y = self.copy(self.act, y[:, 4 * sg_:4 * sg_ + 4, tq], as4(ps), end)
                        self.read_by(b, t_y)
                    if j < 3:
                        t_s = self.tt(self.dve, s_next[:, :, :], Stmp[:, :, :],
                                      pend[:, 4 * sg_:4 * sg_ + 4, j:j + 1].to_broadcast([P, 4, P]), ALU.mult, t_new[0],
                                      (self.pe.sem, self.pe.count))
        self.background(99)
        self.barrier()
        inner.close()
        s1, w_gate, gate_tok = self.slot()
        self.projection_buffers(st)
        self.prepare(self.column_half, 2)
        d, sq = A, B
        t = head_sums(y, None, lambda n, ps, end: self.stt(d[:, 2 * n:2 * n + 2, :], ps, -1.0 / 64, y[:, 2 * n:2 * n + 2, :], ALU.mult, ALU.add, end))
        t2 = self.func(al(sq), al(d), ACT.Square, t)
        t2 = head_sums(sq, t2, lambda n, ps, end: self.ts(self.dve, sq[:, 2 * n:2 * n + 2, :], ps, 1.0 / 64, 64e-5, ALU.mult, ALU.add, end))
        t2 = self.func(al(sq), al(sq), ACT.Ln, t2)
        t2 = self.func(al(sq), al(sq), ACT.Exp, t2, scale=-0.5)
        t = self.tt(self.dve, al(d), al(d), al(sq), ALU.mult, t2)
        toks = []
        for c in range(C):
            t1 = self.ts(self.dve, d[:, c, :], d[:, c, :], self.par("ln_g")[:, c:c + 1], self.par("ln_b")[:, c:c + 1], ALU.mult, ALU.add, t)
            t1 = self.tt(self.pool, d[:, c, :], d[:, c, :], h[:, c, :], ALU.add, t1)
            ps, b, fr = self.half()
            self.pe.wait(fr, gate_tok)
            self.mm(ps, w_gate[:, c * P:(c + 1) * P], g_hid[:, 0, :], True, False)
            end = self.mm_end(ps, w_gate[0:32, D + c * P:D + (c + 1) * P], g_hid[0:32, 1, :], False, True)
            toks.append(self.tt(self.dve, d[:, c, :], d[:, c, :], ps, ALU.mult, t1, end))
            self.read_by(b, toks[-1])
        self.slot_read(s1, end)
        self.h_free = self.y_free = toks[-1]
        toks = self.source(d, toks)
        self.add_back(self.project_columns_out(toks), self.par("a1_gain3"), 1.0)
        st.close()

    def delta_mixer(self):
        i, H, K = 1, 8, 4
        st, sb = self.stage()
        part = lambda n: self.mod[i][:, n * C:(n + 1) * C]
        q_T, k_T, v_T, z = (sb(n, [P, C, T]) for n in ("q", "k", "v", "silu_z"))
        ba = sb("beta_g", [P, TT, 16])
        inner = ExitStack()
        isb = lambda n, s: inner.enter_context(self.nc.sbuf_tensor(f"{n}_{self.stage_no}", s, F32))
        raw, taps = isb("qkv_raw", [P, 2, K - 1 + T]), isb("qkv_taps", [P, 2, T])
        z0 = self.pool.do(lambda e: e.memset(raw[:, :, 0:K - 1], 0.0))
        raw_free, taps_free, late = [None] * 2, [None] * 2, []

        def conv_in(c, ps, end):
            n = c % 2
            dst = (q_T, k_T, v_T)[c // C][:, c % C, :]
            activate()
            t = self.copy(self.act, raw[:, n, K - 1:], ps, end, raw_free[n])
            raw_free[n] = self.conv_chunk(taps[:, n, :], raw[:, n, :], "gdn_conv", None, c, K, [t, z0], taps_free[n])
            late.append((n, dst, raw_free[n]))
            return t

        def activate():
            while late:
                n, dst, tok = late.pop()
                taps_free[n] = self.func(dst, taps[:, n, :], ACT.Silu, tok)
        self.projection_buffers(inner)
        self.prepare(self.column_half, 2)
        h_toks = self.norm_x(self.gain[:, i, 0, :], part(0), self.mod_tok)
        hs = self.source(self.h, h_toks)
        self.columns(hs, 12, conv_in, self.column_half)
        activate()
        self.columns(hs, 4, lambda c, ps, end: self.func(z[:, c, :], ps, ACT.Silu, end))
        for q in range(TT):
            ps, b, fr = self.half()
            self.pe.wait(fr, self.inputs)
            for c in range(C):
                a = (ps[:, 0:16], self.h[:, c, q * P:(q + 1) * P], self.par("w_ba", c * 16, 16), c == 0, c == C - 1)
                end = self.mm_end(*a) if c == C - 1 else self.mm(*a)
            t = self.func(ba[:, q, 0:8], ps[:, 0:8], ACT.Sigmoid, end)
            t = self.tt(self.dve, ba[:, q, 8:16], ps[:, 8:16], self.par("gdn_dt_bias"), ALU.add, end, t)
            self.read_by(b, t)
        self.barrier()
        inner.close()
        tmp = sb("g_tmp", [P, TT, H])
        rate = sb("g_rate", [P, H])
        t = self.softplus(ba[:, :, 8:16], tmp[:, :, :], None)
        ta = self.func(rate[:, :], self.par("gdn_a_log"), ACT.Exp, t)
        for q in range(TT):
            t = self.stt(ba[:, q, 8:16], rate[:, :], -1.0, ba[:, q, 8:16], ALU.mult, ALU.mult, t, ta)
        gc, kdec = sb("g_cumsum", [P, TT, H]), sb("decay_to_end", [P, H])
        ps, b, fr = self.half()
        self.pe.wait(fr, t)
        for q in range(TT):
            self.mm(ps[:, q * H:(q + 1) * H], self.par("upto"), ba[:, q, 8:16], True, True)
        end = self.mm_end(ps[:, 16:24], self.par("ones"), ba[:, 0, 8:16], True, True)
        t = self.copy(self.dve, gc[:, :, :], ps[:, 0:16].rearrange("p (q h) -> p q h", q=TT), end)
        t = self.tt(self.dve, kdec[:, :], ps[:, 16:24], gc[:, 0, :], ALU.subtract, t)
        self.read_by(b, t)
        t_kd = self.func(kdec[:, :], kdec[:, :], ACT.Exp, t)
        sq = self.y
        for dst, s2 in ((q_T, float(P)), (k_T, 1.0)):
            for n in range(4):
                two = slice(2 * n, 2 * n + 2)
                t = self.func(sq[:, two, :], dst[:, two, :], ACT.Square, self.y_free)
                ps, b, fr = self.full()
                self.pe.wait(fr, t)
                end = self.mm_end(ps[:, :], self.par("ones"), sq[:, two, :], True, True)
                t1 = self.ts(self.dve, sq[:, two, :], ps[:, :].rearrange("p (c t) -> p c t", c=2), s2, s2 * NORM_EPS, ALU.mult, ALU.add, end)
                self.read_by(b, t1)
            t1 = self.func(sq[:, :, :], sq[:, :, :], ACT.Ln, t1)
            for n in range(4):
                two = slice(2 * n, 2 * n + 2)
                t2 = self.func(sq[:, two, :], sq[:, two, :], ACT.Exp, t1, scale=-0.5)
                free = self.tt(self.dve, dst[:, two, :], dst[:, two, :], sq[:, two, :], ALU.mult, t2)
            self.y_free = free
        self.barrier()
        o_T = self.h
        names = ("nt", "attn", "t", "tt", "x", "nl", "dec", "k_tok", "vb", "kg", "qd", "state")
        bst = ExitStack()
        bsb = lambda n: bst.enter_context(self.nc.sbuf_tensor(f"{n}_{self.stage_no}", [P, 4, P], F32))
        bufs = [{n: bsb(f"{n}{hg}") for n in names} for hg in range(2)]
        as4 = lambda ps: ps[:, :].rearrange("p (m t) -> p m t", m=4)
        four = lambda m: m.unsqueeze(1).to_broadcast([P, 4, P])
        col = lambda x: x.unsqueeze(2).to_broadcast([P, 4, P])

        def four_heads(hg, q):
            bf = bufs[hg]
            S, h0, tq = bf["state"], 4 * hg, slice(q * P, (q + 1) * P)
            pg, b, fr = self.full()
            self.pe.wait(fr)
            for m in range(4):
                end = self.mm_end(pg[:, m * P:(m + 1) * P], ba[:, q, 8 + h0 + m:9 + h0 + m].to_broadcast([P, P]), self.par("upto"), True, True)
            dec = bf["dec"][:, :, :]
            t = self.tt(self.dve, dec, as4(pg), col(gc[:, q, h0:h0 + 4]), ALU.subtract, end)
            t = self.ts(self.dve, dec, dec, 0.0, None, ALU.min, None, t)
            t_dec = self.func(dec, dec, ACT.Exp, t)
            t_kg = self.func(bf["kg"][:, :, :], as4(pg), ACT.Exp, end, t)
            self.read_by(b, t_kg)
            yield
            t_qd = self.tt(self.pool, bf["qd"][:, :, :], q_T[:, h0:h0 + 4, tq], bf["kg"][:, :, :], ALU.mult, t_kg)
            t_kg = self.tt(self.pool, bf["kg"][:, :, :], k_T[:, h0:h0 + 4, tq], bf["kg"][:, :, :], ALU.mult, t_qd)
            ps, b, fr = self.full()
            self.pe.wait(fr)
            for m in range(4):
                end = self.mm_end(ps[:, m * P:(m + 1) * P], k_T[:, h0 + m, tq], k_T[:, h0 + m, tq], True, True)
            t_nt = self.tt(self.dve, bf["nt"][:, :, :], as4(ps), dec, ALU.mult, end, t_dec)
            self.read_by(b, t_nt)
            ps, b, fr = self.full()
            self.pe.wait(fr)
            for m in range(4):
                end = self.mm_end(ps[:, m * P:(m + 1) * P], ba[:, q, h0 + m:h0 + m + 1].to_broadcast([P, P]), self.par("ident"), True, True)
            t_nt = self.tt(self.dve, bf["nt"][:, :, :], bf["nt"][:, :, :], as4(ps), ALU.mult, end, t_nt)
            self.read_by(b, t_nt)
            t_nt = self.tt(self.pool, bf["nt"][:, :, :], bf["nt"][:, :, :], four(self.par("before")), ALU.mult, t_nt)
            ps, b, fr = self.full()
            self.pe.wait(fr)
            for m in range(4):
                end = self.mm_end(ps[:, m * P:(m + 1) * P], k_T[:, h0 + m, tq], q_T[:, h0 + m, tq], True, True)
            t_at = self.tt(self.dve, bf["attn"][:, :, :], as4(ps), dec, ALU.mult, end, t_dec)
            self.read_by(b, t_at)
            t_at = self.tt(self.pool, bf["attn"][:, :, :], bf["attn"][:, :, :], four(self.par("upto")), ALU.mult, t_at)
            yield
            ps, b, fr = self.full()
            self.pe.wait(fr)
            for m in range(4):
                end = self.transposed(ps[:, m * P:(m + 1) * P], v_T[:, h0 + m, tq], last=m == 3)
            t_vb = self.tt(self.dve, bf["vb"][:, :, :], as4(ps), col(ba[:, q, h0:h0 + 4]), ALU.mult, end)
            self.read_by(b, t_vb)
            t_kt = None
            if q == 0:
                ps, b, fr = self.full()
                self.pe.wait(fr)
                for m in range(4):
                    end = self.transposed(ps[:, m * P:(m + 1) * P], k_T[:, h0 + m, tq], last=m == 3)
                t_kt = self.tt(self.dve, bf["k_tok"][:, :, :], as4(ps), col(kdec[:, h0:h0 + 4]), ALU.mult, end, t_kd)
                self.read_by(b, t_kt)
            bf.update(x_free=None, nl_free=None, tt_free=None)
            yield
            yield from self.invert(bf, bf["nt"][:, :, :], t_nt, (1, 2, 4, 8, 16, 32, 64))
            inv = [bf["done"], bf["x_free"]]
            w = bf["vb"]
            if q:
                ps, b, fr = self.full()
                self.pe.wait(fr, bf["state_tok"], t_kg)
                for m in range(4):
                    end = self.mm_end(ps[:, m * P:(m + 1) * P], bf["kg"][:, m, :], S[:, m, :], True, True)
                w = bf["x"]
                t = self.tt(self.dve, w[:, :, :], as4(ps), col(ba[:, q, h0:h0 + 4]), ALU.mult, end, inv)
                self.read_by(b, t)
                t_vb = self.tt(self.dve, w[:, :, :], bf["vb"][:, :, :], w[:, :, :], ALU.subtract, t, t_vb)
            yield
            ps, b, fr = self.full()
            self.pe.wait(fr, t_vb, inv)
            for m in range(4):
                end = self.mm_end(ps[:, m * P:(m + 1) * P], bf["tt"][:, m, :], w[:, m, :], True, True)
            U = bf["nl"]
            t_u = self.copy(self.act, U[:, :, :], as4(ps), end, inv)
            self.read_by(b, t_u)
            yield
            ps, b, fr = self.full()
            self.pe.wait(fr, t_u, t_at, t_qd)
            for m in range(4):
                o = ps[:, m * P:(m + 1) * P]
                if q:
                    self.mm(o, S[:, m, :], bf["qd"][:, m, :], True, False)
                end = self.mm_end(o, U[:, m, :], bf["attn"][:, m, :], not q, True)
            t = self.copy(self.dve, o_T[:, h0:h0 + 4, tq], as4(ps), end, self.h_free)
            self.read_by(b, t)
            if q == 0:
                ps, b, fr = self.full()
                self.pe.wait(fr, t_u, t_kt)
                for m in range(4):
                    end = self.mm_end(ps[:, m * P:(m + 1) * P], bf["k_tok"][:, m, :], U[:, m, :], True, True)
                bf["state_tok"] = self.copy(self.act, S[:, :, :], as4(ps), end)
                self.read_by(b, bf["state_tok"])

        for q in range(TT):
            self.barrier()
            self.interleave(four_heads(0, q), four_heads(1, q))
        self.barrier()
        bst.close()
        self.projection_buffers(st)
        self.prepare(self.column_half, 2)
        out_tok = []
        for n in range(4):
            two = slice(2 * n, 2 * n + 2)
            t = self.func(sq[:, two, :], o_T[:, two, :], ACT.Square)
            ps, b, fr = self.full()
            self.pe.wait(fr, t)
            end = self.mm_end(ps[:, :], self.par("ones"), sq[:, two, :], True, True)
            t1 = self.ts(self.dve, sq[:, two, :], ps[:, :].rearrange("p (c t) -> p c t", c=2), 1.0 / P, NORM_EPS, ALU.mult, ALU.add, end)
            self.read_by(b, t1)
            out_tok.append(t1)
        t_ln = self.func(sq[:, :, :], sq[:, :, :], ACT.Ln, out_tok)
        for n in range(4):
            two = slice(2 * n, 2 * n + 2)
            t1 = self.func(sq[:, two, :], sq[:, two, :], ACT.Exp, t_ln, scale=-0.5)
            t1 = self.stt(q_T[:, two, :], o_T[:, two, :], self.par("gdn_norm"), sq[:, two, :], ALU.mult, ALU.mult, t1)
            out_tok[n] = self.tt(self.pool, q_T[:, two, :], q_T[:, two, :], z[:, two, :], ALU.mult, t1)
        self.h_free = self.y_free = t1
        toks = self.source(q_T, [out_tok[c // 2] for c in range(C)])
        self.add_back(self.project_columns_out(toks), self.gain[:, i, 1, :], 1.0)
        st.close()


def program(nc, x_in, w_in, pack_in, out, n_slots, at):
    k = Kernel(nc, x_in, w_in, pack_in, out, n_slots, at)
    for name, stage in STAGES:
        stage(k)
    k.finish()


STAGES = [
    ("a0_ffn1", lambda k: k.ffn("a0_gain0", "a0_gain1")),
    ("a0_mix", lambda k: k.nsa_ssd_mixer()),
    ("a0_ffn2", lambda k: k.ffn("a0_gain4", "a0_gain5")),
    ("a1_ffn1", lambda k: k.ffn("a1_gain0", "a1_gain1")),
    ("a1_mix", lambda k: k.rwkv_mixer()),
    ("a1_ffn2", lambda k: k.ffn("a1_gain4", "a1_gain5")),
    ("b0_mix", lambda k: k.conv_mixer(0)),
    ("b0_moe", lambda k: k.moe(0)),
    ("b1_mix", lambda k: k.delta_mixer()),
    ("b1_moe", lambda k: k.moe(1)),
]


def kernel(**inputs):
    from concourse import bacc
    from concourse.bass_utils import run_bass_kernel_spmd

    xT, slots, pk = lay_out(inputs)
    weights = np.stack(slots)
    small = np.concatenate(pk.parts, axis=1)
    nc = bacc.Bacc("TRN2", target_bir_lowering=False, num_devices=1)
    args = []
    arrays = {"x_T": xT, "weight_slots": weights, "small_params": small}
    for name, arr in arrays.items():
        args.append(nc.dram_tensor(name, arr.shape, F32, kind="ExternalInput").ap())
    out = nc.dram_tensor("out_T", xT.shape, F32, kind="ExternalOutput").ap()
    program(nc, *args, out, len(slots), pk.at)
    got = run_bass_kernel_spmd(nc, [arrays], core_ids=[0]).results[0]["out_T"]
    return np.ascontiguousarray(got.transpose(2, 1, 0).reshape(1, T, D))
```
